# Optimizing a Trainium2 kernel written in Bass

```python
import math
import jax, jax.numpy as jnp
from jax import lax
import numpy as np

D_MODEL = 2048
BATCH = 1
SEQ = 1024
DEPTH = 1

CTX_LEN = 256
GRID_W = 64
MIX_WIDTH = D_MODEL
POOL_WIDTH = MIX_WIDTH // 2
SSM_WIDTH = MIX_WIDTH - POOL_WIDTH
POOL_WINDOWS = (2, 4, 8, 16)
POOL_GROUPS = len(POOL_WINDOWS)
POOL_GROUP_W = POOL_WIDTH // POOL_GROUPS
SSM_GROUP_CH = 16
SSM_GROUPS = SSM_WIDTH // SSM_GROUP_CH
SSM_STATE = 64
DT_MIN = 1e-3
DT_MAX = 1e-1
EPS = 1e-6

kernel_name = "hybrid_pool_s5_prefix_dit_block"

def _rmsnorm(v, g):
    v32 = v.astype(jnp.float32)
    out = v32 * lax.rsqrt(jnp.mean(v32 * v32, axis=-1, keepdims=True) + EPS)
    return (out * g.astype(jnp.float32)).astype(v.dtype)

def _centred_window_mean(v, window, axis):
    n = v.shape[axis]
    pad = [(0, 0)] * v.ndim
    pad[axis] = (1, 0)
    cs = jnp.pad(jnp.cumsum(v.astype(jnp.float32), axis=axis), pad)
    t = jnp.arange(n)
    lo = jnp.clip(t - window // 2, 0, n)
    hi = jnp.clip(t + window - window // 2, 0, n)
    s = jnp.take(cs, hi, axis=axis) - jnp.take(cs, lo, axis=axis)
    shape = [1] * v.ndim
    shape[axis] = n
    cnt = (hi - lo).astype(jnp.float32).reshape(shape)
    return (s / cnt).astype(v.dtype)

def _pool_mix(u, pool_w, pool_scale, axes):
    outs = []
    for g, w in enumerate(POOL_WINDOWS):
        ug = u[..., g * POOL_GROUP_W:(g + 1) * POOL_GROUP_W]
        m = ug
        for ax in axes:
            m = _centred_window_mean(m, w, ax)
        outs.append(jnp.einsum('...c,cd->...d', m - ug, pool_w[g]))
    return jnp.concatenate(outs, axis=-1) * pool_scale

def _linear_combine(left, right):
    a_l, b_l = left
    a_r, b_r = right
    return a_l * a_r, a_r * b_l + b_r

def _s5_scan(u, lam_re, lam_im, log_dt, b_re, b_im, h0, reverse):
    bsz, n = u.shape[0], u.shape[1]
    lam = lax.complex(lam_re.astype(jnp.float32), lam_im.astype(jnp.float32))
    dt = jnp.exp(log_dt.astype(jnp.float32))[:, None]
    a_bar = jnp.exp(lam * dt)
    b = lax.complex(b_re.astype(jnp.float32), b_im.astype(jnp.float32))
    b_bar = ((a_bar - 1.0) / lam)[..., None] * b
    ug = u.astype(jnp.float32).reshape(bsz, n, SSM_GROUPS, SSM_GROUP_CH)
    bu = lax.complex(jnp.einsum('blgh,gnh->blgn', ug, b_bar.real),
                     jnp.einsum('blgh,gnh->blgn', ug, b_bar.imag))
    first = n - 1 if reverse else 0
    bu = bu.at[:, first].add(a_bar * h0)
    a = jnp.broadcast_to(a_bar, bu.shape)
    _, hs = lax.associative_scan(_linear_combine, (a, bu), reverse=reverse, axis=1)
    return hs

def _s5_readout(hs, c_re, c_im):
    y = (jnp.einsum('blgn,ghn->blgh', hs.real, c_re.astype(jnp.float32))
         - jnp.einsum('blgn,ghn->blgh', hs.imag, c_im.astype(jnp.float32)))
    return y.reshape(hs.shape[0], hs.shape[1], SSM_WIDTH)

def _merge_branches(pool_out, u_ssm, hs_f, hs_b, z, c_re, c_im, d_skip, glu_w, glu_b, out_w):
    y = (_s5_readout(hs_f, c_re[0], c_im[0]) + _s5_readout(hs_b, c_re[1], c_im[1])).astype(u_ssm.dtype)
    y = jax.nn.gelu(y + d_skip * u_ssm)
    y1, y2 = jnp.split(y @ glu_w + glu_b, 2, axis=-1)
    ssm_out = y1 * jax.nn.sigmoid(y2)
    branch = jnp.concatenate([pool_out, ssm_out], axis=-1) * jax.nn.silu(z)
    return branch @ out_w

def _layer(x, ctx, c, c_ctx, ada_w, ada_b, norm_g, in_w, pool_w, pool_scale,
           lam_re, lam_im, log_dt, b_re, b_im, c_re, c_im, d_skip, glu_w, glu_b, out_w, update_ctx):
    bsz, seq = x.shape[0], x.shape[1]
    rows = seq // GRID_W
    shift, scale, gate = jnp.split(jax.nn.silu(c) @ ada_w + ada_b, 3, axis=-1)
    shift_c, scale_c, gate_c = jnp.split(jax.nn.silu(c_ctx) @ ada_w + ada_b, 3, axis=-1)
    h = _rmsnorm(x, norm_g) * (1.0 + scale[:, None]) + shift[:, None]
    hc = _rmsnorm(ctx, norm_g) * (1.0 + scale_c) + shift_c

    uc_ssm = hc @ in_w[:, POOL_WIDTH:MIX_WIDTH]
    zeros_h = jnp.zeros((bsz, SSM_GROUPS, SSM_STATE), jnp.complex64)
    hs_cf = _s5_scan(uc_ssm, lam_re[0], lam_im[0], log_dt[0], b_re[0], b_im[0], zeros_h, False)
    hs_cb = _s5_scan(uc_ssm, lam_re[1], lam_im[1], log_dt[1], b_re[1], b_im[1], zeros_h, True)
    if update_ctx:
        uc_pool = hc @ in_w[:, :POOL_WIDTH]
        zc = hc @ in_w[:, MIX_WIDTH:]
        pool_c = _pool_mix(uc_pool, pool_w, pool_scale, (1,))
        mix_c = _merge_branches(pool_c, uc_ssm, hs_cf, hs_cb, zc, c_re, c_im, d_skip, glu_w, glu_b, out_w)
        ctx = ctx + gate_c * mix_c

    proj = h @ in_w
    u_pool = proj[..., :POOL_WIDTH]
    u_ssm = proj[..., POOL_WIDTH:MIX_WIDTH]
    z = proj[..., MIX_WIDTH:]
    grid = u_pool.reshape(bsz, rows, GRID_W, POOL_WIDTH)
    pool_out = _pool_mix(grid, pool_w, pool_scale, (1, 2)).reshape(bsz, seq, POOL_WIDTH)
    hs_f = _s5_scan(u_ssm, lam_re[0], lam_im[0], log_dt[0], b_re[0], b_im[0], hs_cf[:, -1], False)
    hs_b = _s5_scan(u_ssm, lam_re[1], lam_im[1], log_dt[1], b_re[1], b_im[1], hs_cb[:, 0], True)
    mix = _merge_branches(pool_out, u_ssm, hs_f, hs_b, z, c_re, c_im, d_skip, glu_w, glu_b, out_w)
    x = x + gate[:, None] * mix
    return x, ctx

def setup_inputs(seed: int = 0) -> dict:
    key = jax.random.key(seed)
    k = jax.random.split(key, 24)
    nrm = jax.random.normal
    D, G, N, H = D_MODEL, SSM_GROUPS, SSM_STATE, SSM_GROUP_CH
    n_idx = jnp.arange(N, dtype=jnp.float32)
    return {
        "x": nrm(k[0], (BATCH, SEQ, D), jnp.float32),
        "c": nrm(k[1], (BATCH, D), jnp.float32),
        "ctx": nrm(k[2], (BATCH, CTX_LEN, D), jnp.float32),
        "c_ctx": nrm(k[3], (D,), jnp.float32),
        "ada_w": nrm(k[4], (DEPTH, D, 3 * D), jnp.float32) * (0.5 * D ** -0.5),
        "ada_b": 0.01 * nrm(k[5], (DEPTH, 3 * D), jnp.float32),
        "norm_g": 1.0 + 0.01 * nrm(k[6], (DEPTH, D), jnp.float32),
        "in_w": nrm(k[7], (DEPTH, D, 2 * MIX_WIDTH), jnp.float32) * D ** -0.5,
        "pool_w": nrm(k[8], (DEPTH, POOL_GROUPS, POOL_GROUP_W, POOL_GROUP_W), jnp.float32) * POOL_GROUP_W ** -0.5,
        "pool_scale": 1.0 + 0.1 * nrm(k[9], (DEPTH, POOL_WIDTH), jnp.float32),
        "s5_lam_re": -0.5 + 0.01 * nrm(k[10], (DEPTH, 2, G, N), jnp.float32),
        "s5_lam_im": jnp.pi * n_idx + 0.01 * nrm(k[11], (DEPTH, 2, G, N), jnp.float32),
        "s5_log_dt": jax.random.uniform(k[12], (DEPTH, 2, G), jnp.float32,
                                        minval=math.log(DT_MIN), maxval=math.log(DT_MAX)),
        "s5_b_re": nrm(k[13], (DEPTH, 2, G, N, H), jnp.float32) * (2 * H) ** -0.5,
        "s5_b_im": nrm(k[14], (DEPTH, 2, G, N, H), jnp.float32) * (2 * H) ** -0.5,
        "s5_c_re": nrm(k[15], (DEPTH, 2, G, H, N), jnp.float32) * N ** -0.5,
        "s5_c_im": nrm(k[16], (DEPTH, 2, G, H, N), jnp.float32) * N ** -0.5,
        "s5_d": nrm(k[17], (DEPTH, SSM_WIDTH), jnp.float32),
        "glu_w": nrm(k[18], (DEPTH, SSM_WIDTH, 2 * SSM_WIDTH), jnp.float32) * SSM_WIDTH ** -0.5,
        "glu_b": 0.01 * nrm(k[19], (DEPTH, 2 * SSM_WIDTH), jnp.float32),
        "out_w": nrm(k[20], (DEPTH, MIX_WIDTH, D), jnp.float32) * MIX_WIDTH ** -0.5,
        "final_g": 1.0 + 0.01 * nrm(k[21], (D,), jnp.float32),
    }

def reference(x, c, ctx, c_ctx, ada_w, ada_b, norm_g, in_w, pool_w, pool_scale,
              s5_lam_re, s5_lam_im, s5_log_dt, s5_b_re, s5_b_im, s5_c_re, s5_c_im, s5_d,
              glu_w, glu_b, out_w, final_g):
    for i in range(DEPTH):
        x, ctx = _layer(x, ctx, c, c_ctx, ada_w[i], ada_b[i], norm_g[i], in_w[i], pool_w[i], pool_scale[i],
                        s5_lam_re[i], s5_lam_im[i], s5_log_dt[i], s5_b_re[i], s5_b_im[i],
                        s5_c_re[i], s5_c_im[i], s5_d[i], glu_w[i], glu_b[i], out_w[i],
                        update_ctx=(i < DEPTH - 1))
    return _rmsnorm(x, final_g)


_drawn_inputs = setup_inputs


def setup_inputs(seed=0):
    import zlib

    import numpy as np

    out = dict(_drawn_inputs(seed))
    spreads = {}
    factors = {'ctx': 64.0,
     'c_ctx': 64.0,
     'ada_b': 8.0,
     'norm_g': 31.402,
     'pool_scale': 4.068,
     's5_lam_re': 64.0,
     's5_lam_im': 54.392,
     's5_log_dt': 64.0,
     's5_b_re': 64.0,
     's5_b_im': 64.0,
     's5_c_re': 64.0,
     's5_c_im': 64.0,
     'glu_b': 64.0,
     'final_g': 29.898}
    for name, (base, spread) in spreads.items():
        noise = np.random.default_rng([zlib.crc32(name.encode()), seed]).standard_normal(out[name].shape)
        drawn = base * np.exp(spread * noise) if base else spread * noise
        out[name] = __import__('jax').numpy.asarray(drawn.astype(out[name].dtype))
    for name, factor in factors.items():
        out[name] = (out[name] * factor).astype(out[name].dtype)
    return out
```

```python
import math
from contextlib import ExitStack

import numpy as np

import concourse.bass as bass
from concourse import mybir

D = 2048
T = 1024
TC = 256
GW = 64
GR = T // GW
PW = D // 2
SW = D // 2
WINDOWS = (2, 4, 8, 16)
PGW = PW // len(WINDOWS)
SG, SH, SN = 64, 16, 64
KT = D // 128
L = 8
CX, CC = T // L, TC // L
SEQC = CX + CC
XC = SEQC + CC
GQ = 4
NQ = SG // GQ
EPS = 1e-6
NB = 512
LANES = 2 * L - 1
JP = L + 2

V_C, V_CC, V_ADAB, V_NG, V_D, V_GLUB, V_PS = 0, 16, 32, 80, 96, 104, 120


def hybrid_block(nc, x, c, ctx_in, c_ctx, ada_w, ada_b, norm_g, in_w, pool_w, pool_scale,
                 lam_re, lam_im, log_dt, b_re, b_im, c_re, c_im, d_skip, glu_w, glu_b, out_w, final_g,
                 inv_count, out, debug=None):
    f32, f32r, i32, bf16 = mybir.dt.float32, mybir.dt.float32r, mybir.dt.int32, mybir.dt.bfloat16
    ALU = mybir.AluOpType
    ACT = mybir.ActivationFunctionType
    ds = bass.ds
    es = ExitStack()
    with es:
        def sem(name):
            return es.enter_context(nc.semaphore(name))

        def scratch(name, shape):
            kind = "ExternalOutput" if debug else "Internal"
            return nc.dram_tensor(name, shape, f32, kind=kind).ap()

        u_scr = scratch("u_scr", [SW, L, XC])
        y_scr = scratch("y_scr", [SW, L, CX])
        z_scr = scratch("z_scr", [D, T])
        up_scr = scratch("up_scr", [PW, T])
        pb_scr = scratch("pb_scr", [PW, T])
        yo_scr = scratch("yo_scr", [T, D])
        p_scr = scratch("p_scr", [NQ, 2, L, 2, GQ, SN])
        b_scr = scratch("b_scr", [NQ, 2, SH, 2, GQ, SN])
        ctab = scratch("ctab", [128, SG, 3, SH])
        qtab = scratch("qtab", [128, SG, 2, JP])
        btab = scratch("btab", [128, SG, 2, SH])

        BASE = 16512
        HI, LO, RAW = BASE, BASE + 65536, BASE + 131072
        WHI, WLO = RAW + 8192, RAW + 16384
        SMALL = RAW + 24576
        WK = SMALL + 3584

        def at(name, shape, offset, dt=f32):
            return nc.alloc_sbuf_tensor_at(name, shape, dt, offset=offset)

        act_hi = at("act_hi", [128, KT, T], HI, f32r)
        act_lo = at("act_lo", [128, KT, T], LO, f32r)
        w_raw = [at(f"w_raw{s}", [128, 1024], RAW + 4096 * s) for s in range(2)]
        w_hi = [at(f"w_hi{s}", [128, 1024], WHI + 4096 * s, f32r) for s in range(2)]
        w_lo = [at(f"w_lo{s}", [128, 1024], WLO + 4096 * s, f32r) for s in range(2)]

        o = [SMALL]

        def small(name, shape, dt=f32):
            t = at(name, shape, o[0], dt)
            o[0] += (4 * int(np.prod(shape[1:])) + 31) // 32 * 32
            assert o[0] <= WK
            return t

        ident = small("ident", [128, 128])
        ones = small("ones", [128, 128])
        vT = small("vT", [128, 128])
        cs = small("cs", [128, KT, 2])
        modT = small("modT", [128, 2, KT, 2])
        gmul = small("gmul", [128, KT, 2])
        wT = small("wT", [128, 3, SG])
        ssq = small("ssq", [128, 2, 4])
        b2col = small("b2col", [128, 8])
        rs = small("rs", [128, 4])
        ysq = small("ysq", [128, 8, 4])

        ada_buf = [at(f"ada_buf{s}", [128, D], HI + 8192 * s) for s in range(4)]
        x_tile = [at(f"x_tile{s}", [128, D], HI + 32768 + 8192 * s) for s in range(2)]
        xT = at("xT", [128, KT, T], LO)
        cT = at("cT", [128, KT, TC], WK)
        c_lo = at("c_lo", [128, KT, TC], WK, f32r)
        c_hi = at("c_hi", [128, KT, TC], WK + 16384, f32r)
        ust = at("ust", [128, 2, L, XC], WK + 32768)
        vecs = at("vecs", [128, 128], WK + 32768)
        ada_row = at("ada_row", [128, 2, NB], WK + 32768 + 512)
        sq_junk = at("sq_junk", [128, NB], WK + 32768 + 4608 + 5120 + 8192, bf16)
        SA, SB = HI + 49152, RAW
        pp = {}
        names = ["lre", "lim", "zr", "zi", "n", "t", "r", "p", "e", "y", "sh", "s1", "cm", "inv", "t2", "t3",
                 "kr", "ki", "y8", "wr", "wi", "r8"]
        for i, n_ in enumerate(names):
            pp[n_] = at(f"p_{n_}", [128, SN], SA + 256 * i)
        e_bits = at("e_bits", [128, SN], SA + 256 * len(names), i32)
        dt_col = at("dt_col", [128, 8], SA + 256 * (len(names) + 1))
        dt_bits = at("dt_bits", [128, 1], SA + 256 * (len(names) + 1) + 64, i32)
        pw_ = at("pw", [128, L + 1, 2, SN], SA + 256 * (len(names) + 2))
        ptmp = at("ptmp", [128, 2, 4, 2, SN], SA + 256 * (len(names) + 2) + 4608)
        assert 256 * (len(names) + 2) + 4608 + 4096 <= 16384
        b_nat = at("b_nat", [128, 2, SN, SH], SB)
        b_bar = at("b_bar", [128, SH, 2, SN], SB + 8192)
        b_tmp = at("b_tmp", [128, 2, SH, SN], SB + 16384)
        c_nat = at("c_nat", [128, 8, 3, 2, SN], SB)
        c_st = at("c_st", [128, SG, 3, SH], SB + 12288)
        q_st = at("q_st", [128, SG, 2, JP], WK + 32768 + 4608)
        b_st = at("b_st", [128, SG, 2, SH], WK + 32768 + 4608 + 5120)
        assert WK + 32768 + 4608 + 5120 + 8192 <= 229368

        z_st = [at(f"z_st{s}", [128, NB], WK + 49152 + 2048 * s) for s in range(2)]

        w_ = [WK]

        def work(name, shape, over=None):
            off = w_[0] if over is None else over
            t = at(name, shape, off)
            if over is None:
                w_[0] += 4 * int(np.prod(shape[1:]))
            assert w_[0] <= WK + 49152
            return t, off

        X, _ = work("X", [128, GQ, XC])
        PT, o_pt = work("PT", [128, 2, 2, GQ * SN])
        H, _ = work("H", [128, GQ, 2, CX], o_pt)
        BT, o_bt = work("BT", [128, 2, 2, GQ * SN])
        M, _ = work("M", [128, GQ, L * SH], o_bt)
        yst, _ = work("yst", [128, GQ, CX], o_bt + 2048)
        CQ, _ = work("CQ", [128, GQ, 3, SH])
        QQ, _ = work("QQ", [128, GQ, 2, JP])
        BZ, _ = work("BZ", [128, 2, GQ, 2, SH])
        E, _ = work("E", [128, 2, 2, GQ * SN])
        TG, _ = work("TG", [128, 2, 2 * GQ * SN])
        F, _ = work("F", [128, GQ, 2, JP, SH])
        strip, _ = work("strip", [SH, GQ, LANES, SH])
        R, _ = work("R", [128, GQ, 2, SEQC])
        TV, _ = work("TV", [128, 2, 1024])
        G, _ = work("G", [128, GQ, 2, SEQC])

        y_in = at("y_in", [128, T], WK)
        u_in = at("u_in", [128, L, CX], WK + 4096)
        sg = at("sg", [128, T], WK)
        br = at("br", [128, T], WK + 4096)
        z_in = at("z_in", [128, T], WK + 8192)
        bf = at("bf", [128, T], WK + 12288)
        up_in = at("up_in", [128, 2, T], WK + 16384)
        inv_in = at("inv_in", [128, T], WK + 24576)
        PA = at("PA", [128, 2048], WK + 28672)
        PB = at("PB", [128, 2048], WK + 36864)
        bp = at("bp", [128, 2, T], WK + 28672)
        zp_in = at("zp_in", [128, T], WK + 36864)
        pw_in = at("pw_in", [128, 2, PGW], WK + 40960)
        gate_row = at("gate_row", [128, NB], WK + 51200)

        yb = at("yb", [128, 8, NB], WK)
        adab_bc = at("adab_bc", [128, D], WK)
        xb = at("xb", [128, 8, NB], WK + 16384)
        pb_in = [at(f"pb_in{s}", [128, T], WK + 16384 + 4096 * s) for s in range(2)]
        gate_bc = at("gate_bc", [128, D], WK + 32768)
        fg_bc = at("fg_bc", [128, D], WK + 40960)
        yfin = [at(f"yfin{s}", [128, 4, 3 * NB], (HI, LO)[s] + 32768) for s in range(2)]
        sq_junk2 = at("sq_junk2", [128, NB], WK + 49152)

        S = {}

        def sm(name):
            if name not in S:
                S[name] = es.enter_context(nc.semaphore(name))
            return S[name]

        START = {"bank_free0": 1, "bank_free1": 1, "strip_evicted": 1, "s_read": 1, "y_evicted": 1, "pool_evicted": 1,
                 "zst_stored0": 16, "zst_stored1": 16, "y_done": 1, "yst_stored": 16, "hs_ready": 1,
                 "s_done": 1, "y_ready": 1, "y_added": 1}

        def past(name, n):
            return sm(name), n + START[name]

        ps = es.enter_context(nc.psum_tensor("ps", [128, 8, NB], f32))
        block = es.enter_context(nc.Block())

        T_SSM, T_Z, T_POOL, T_GLU, T_OUT, T_END = 0, 16, 48, 64, 80, 112
        G_SSM, G_Z, G_POOL, G_GLU = 0, 4, 12, 16
        OUT_ORDER = (4, 5, 6, 0, 1, 2, 3, 7)

        vec_src = [(c, V_C, 16), (c_ctx, V_CC, 16), (ada_b, V_ADAB, 48), (norm_g, V_NG, 16), (d_skip, V_D, 8),
                   (glu_b, V_GLUB, 16), (pool_scale, V_PS, 8)]

        in_tiles = in_w.rearrange("o (a b p) n -> p (o a) b n", p=128, b=4)
        glu_tiles = glu_w.rearrange("o (b p) n -> p (o b) n", p=128)
        out_tiles = out_w.rearrange("o (a b p) n -> p (o a) b n", p=128, b=2)
        ada_rows = ada_w.rearrange("o (k p) n -> p (o k) n", p=128)

        @block.sync
        def _(sp):
            for v, row, n in vec_src:
                flat = v.rearrange("o (r q) -> (o r) q", q=128) if len(v.shape) == 2 else v.rearrange("(r q) -> r q", q=128)
                sp.dma_start(vecs[row:row + n, :], flat).then_inc(sm("vecs_loaded"), 16)

            def apart(semaphore, value):
                sp.wait_ge(semaphore, value)
                sp.sem_inc(sm("sp_passed"), 1)

            def ada_load(k, piece, s):
                sp.dma_start(ada_buf[s][:, :].unsqueeze(1), ada_rows[:, ds(k, 1), piece * D:(piece + 1) * D]) \
                    .then_inc(sm(f"ada_loaded{s}"), 16)

            for s in range(4):
                ada_load(s // 2, s % 2, s)
            with sp.Fori(1, 8) as i:
                for s in range(4):
                    apart(sm("ada_used"), i * 4 + (s - 3))
                    ada_load(i * 2 + s // 2, s % 2, s)

            def raw_free(t):
                apart(sm("w_lo_ready"), t - 1)

            def in_tile(col, a, s):
                sp.dma_start(w_raw[s][:, :].rearrange("p (b n) -> p b n", b=4),
                             in_tiles[:, a, :, ds(col, 256)]).then_inc(sm(f"w_loaded{s}"), 16)

            for j in range(4):
                if j < 2:
                    sp.wait_ge(sm("params_stored"), 16 * 3)
                else:
                    raw_free(T_SSM + j)
                in_tile(PW, j, j % 2)
            with sp.Fori(1, 4) as i:
                for j in range(4):
                    raw_free(i * 4 + (T_SSM + j))
                    in_tile(i * 256 + PW, j, j % 2)
            with sp.Fori(0, 8) as i:
                for j in range(4):
                    raw_free(i * 4 + (T_Z + j))
                    in_tile(i * 256 + D, j, j % 2)
            with sp.Fori(0, 4) as i:
                for j in range(4):
                    raw_free(i * 4 + (T_POOL + j))
                    in_tile(i * 256, j, j % 2)

            def glu_tile_pair(i):
                for half in range(2):
                    raw_free(i * 2 + (T_GLU + half))
                    sp.dma_start(w_raw[half][:, :].rearrange("p (b n) -> p b n", b=8),
                                 glu_tiles[:, :, ds(i * 128 + half * SW, 128)]).then_inc(sm(f"w_loaded{half}"), 16)

            glu_tile_pair(0)
            sp.wait_ge(sm("w_used"), T_GLU)
            for s in range(4):
                ada_load(s, 2, s)
            with sp.Fori(1, 4) as i:
                for s in range(4):
                    apart(sm("ada_used"), i * 4 + (32 - 3 + s))
                    ada_load(i * 4 + s, 2, s)
            with sp.Fori(1, 8) as i:
                glu_tile_pair(i)
            with sp.Fori(0, 4) as i:
                for j, a in enumerate(OUT_ORDER):
                    raw_free(i * 8 + (T_OUT + j))
                    sp.dma_start(w_raw[j % 2][:, :].rearrange("p (b n) -> p b n", b=2),
                                 out_tiles[:, a, :, ds(i * NB, NB)]).then_inc(sm(f"w_loaded{j % 2}"), 16)

        @block.tensor
        def _(pe):
            pe.sem_inc(sm("y_done"), START["y_done"])
            pe.sem_inc(sm("s_done"), START["s_done"])

            def x_transposes(i, s):
                pe.wait_ge(sm("xn_ready"), i + 1)
                for kb in range(4):
                    b = kb % 2
                    n = 2 * i + kb // 2
                    if n > 0:
                        pe.wait_ge(sm(f"tr_evicted{b}"), n)
                    for r in range(4):
                        k = 4 * kb + r
                        mm = pe.transpose(ps[:, 2 + b, 128 * r:128 * (r + 1)], x_tile[s][:, 128 * k:128 * (k + 1)], ident[:, :])
                    mm.then_inc(sm(f"tr_done{b}"), 1)

            def ada_matmuls(n, k, piece, s, first, last):
                pe.wait_ge(sm(f"ada_loaded{s}"), 16 * (n // 4 + 1))
                for q in range(4):
                    mm = pe.matmul(ps[32 * q:32 * q + 2, piece, :], cs[:, k, :], ada_buf[s][:, NB * q:NB * (q + 1)],
                                   start=first, stop=last)
                mm.then_inc(sm("ada_used"), 1)

            pe.wait_ge(sm("ident_ready"), 2)
            pe.wait_ge(sm("vecs_loaded"), 16 * len(vec_src))
            pe.transpose(ps[:, 7, 0:128], vecs[:, :], ident[:, :]).then_inc(sm("vT_done"), 1)
            pe.wait_ge(sm("cs_ready"), 1)
            for n in range(32):
                ada_matmuls(n, n // 2, n % 2, n % 4, n < 2, n >= 30)
                if n % 2 == 1 and n // 2 < 10:
                    x_transposes(n // 2, (n // 2) % 2)
                if n == 21:
                    pe.wait_ge(sm("pw_ready"), 1)
                    blocks = [pw_[:, j, ri, :] for j in range(L + 1) for ri in range(2)]
                    blocks += [b_bar[:, h, ri, :] for h in range(SH) for ri in range(2)]
                    blocks += [pp[w][:, :] for w in ("wr", "wi", "r8")]
                    rounds = [blocks[0:8], blocks[8:16], blocks[16:18]] + [blocks[18 + 8 * r:26 + 8 * r] for r in range(4)] + [blocks[50:53]]
                    for r, blk in enumerate(rounds):
                        if r > 0:
                            pe.wait_ge(sm("pf_evicted"), r)
                            pe.wait_ge(sm("pbk_evicted"), r)
                        for i_, src in enumerate(blk):
                            for d_ in range(2):
                                lo_ = 64 * d_
                                mm = pe.matmul(ps[lo_:lo_ + 64, 4 + d_, 64 * i_:64 * i_ + 64], src[lo_:lo_ + 64, :],
                                               ident[lo_:lo_ + 64, lo_:lo_ + 64], start=True, stop=True)
                        mm.then_inc(sm("pt_done"), 1)
                if n == 27:
                    pe.wait_ge(sm("c_ready"), 1)
                    for oc in range(8):
                        if oc > 0:
                            pe.wait_ge(sm("ct_evicted"), oc)
                        for e in range(3):
                            mm = pe.transpose(ps[:, 6, 128 * e:128 * (e + 1)],
                                              c_nat[:, oc, e, :, :].rearrange("p d n -> p (d n)"), ident[:, :])
                        mm.then_inc(sm("ct_done"), 1)
            pe.wait_ge(sm("ada_row_ready"), 1)
            pe.wait_ge(sm("tr_evicted0"), 20)
            pe.wait_ge(sm("tr_evicted1"), 20)
            pe.wait_ge(sm("pf_evicted"), 8)
            pe.wait_ge(sm("pbk_evicted"), 8)
            for q in range(4):
                for h in range(2):
                    for r in range(4):
                        mm = pe.matmul(ps[:, 2 + q, (4 * h + r) * 2:(4 * h + r) * 2 + 2],
                                       ada_row[32 * q:32 * q + 2, h, 128 * r:128 * (r + 1)],
                                       ident[32 * q:32 * q + 2, 32 * q:32 * q + 2], start=True, stop=True)
            mm.then_inc(sm("mod_done"), 1)
            pe.wait_ge(sm("mod_evicted"), 1)

            def three(bank, cols, w, a, start, stop):
                (wh, wl), (ah, al) = w, a
                pe.matmul(ps[:, bank, 0:cols], wh, ah, start=start, stop=False)
                pe.matmul(ps[:, bank, 0:cols], wh, al, start=False, stop=False)
                return pe.matmul(ps[:, bank, 0:cols], wl, ah, start=False, stop=stop)

            def in_tile(t, s, j, g, ctx):
                pe.wait_ge(sm("w_lo_ready"), t + 1)
                for kk in range(4):
                    k = 4 * j + kk
                    if ctx:
                        pe.wait_ge(sm("h_ready"), k + 1)
                        if kk == 0:
                            pe.wait_ge(sm("hc_ready"), j + 1)
                    for m in range(2):
                        cut = slice(256 * kk + 128 * m, 256 * kk + 128 * (m + 1))
                        w = (w_hi[s][:, cut], w_lo[s][:, cut])
                        if k == 0:
                            pe.wait_ge(*past(f"bank_free{m}", g))
                        for n in range(2):
                            a = (act_hi[:, k, NB * n:NB * (n + 1)], act_lo[:, k, NB * n:NB * (n + 1)])
                            mm = three(2 * m + n, NB, w, a, k == 0, k == KT - 1)
                        if ctx:
                            mm = three(4 + m, TC, w, (c_hi[:, k, :], c_lo[:, k, :]), k == 0, k == KT - 1)
                        if k == KT - 1 and m == 0:
                            mm.then_inc(sm("m0_done"), 1)
                mm.then_inc(sm("w_used"), 1)

            with pe.Fori(0, 4) as i:
                for j in range(4):
                    in_tile(i * 4 + (T_SSM + j), j % 2, j, i + G_SSM, True)
            with pe.Fori(0, 8) as i:
                for j in range(4):
                    in_tile(i * 4 + (T_Z + j), j % 2, j, i + G_Z, False)
            with pe.Fori(0, 4) as i:
                for j in range(4):
                    in_tile(i * 4 + (T_POOL + j), j % 2, j, i + G_POOL, False)

            pe.wait_ge(*past("bank_free0", G_GLU))
            for n in range(16):
                pe.wait_ge(sm(f"ada_loaded{n % 4}"), 16 * (8 + n // 4 + 1))
                for q in range(4):
                    mm = pe.matmul(ps[32 * q:32 * q + 1, 0, :], cs[:, n, 0:1], ada_buf[n % 4][:, NB * q:NB * (q + 1)],
                                   start=n == 0, stop=n == 15)
                mm.then_inc(sm("ada_used"), 1)

            def ssm_quad(q):
                pe.wait_ge(sm("f_ready"), q + 1)
                pe.wait_ge(sm("bz_loaded"), q * 32 + 32)
                for r in range(2):
                    pe.wait_ge(*past("strip_evicted", q * 2 + r))
                    for gg in range(2):
                        g = 2 * r + gg
                        o_ = LANES * SH * gg
                        for d_, lo_, j0 in ((1, 0, 2), (0, (L - 1) * SH, 0)):
                            for ri in range(2):
                                mm = pe.matmul(ps[0:SH, 6, o_ + lo_:o_ + lo_ + L * SH], BZ[:, d_, g, ri, :],
                                               F[:, g, ri, j0:j0 + L, :].rearrange("p j h -> p (j h)"),
                                               start=(d_ == 1 and ri == 0), stop=(d_ == 0 and ri == 1), skip_group_check=True)
                    mm.then_inc(sm("strip_done"), 1)
                pe.wait_ge(sm("xq_loaded"), q * 128 + 128)
                pe.wait_ge(sm("e_ready"), q + 1)
                for r in range(2):
                    pe.wait_ge(*past("s_read", q * 2 + r))
                    for gg in range(2):
                        g = 2 * r + gg
                        for ri in range(2):
                            for d_, rhs in ((0, X[:, g, 0:SEQC]), (1, X[:, g, XC - 1:CC - 1:-1])):
                                mm = pe.matmul(ps[64 * d_:64 * d_ + 64, 4 + gg, ri * SEQC:(ri + 1) * SEQC],
                                               E[:, d_, ri, SN * g:SN * (g + 1)], rhs, start=True, stop=True)
                    mm.then_inc(sm("s_done"), 1)
                pe.wait_ge(sm("m_loaded"), q * 128 + 128)
                pe.wait_ge(*past("hs_ready", q + 1))
                pe.wait_ge(*past("y_evicted", q))
                for g in range(GQ):
                    o_ = ps[:, 7, CX * g:CX * (g + 1)]
                    pe.matmul(o_, M[:, g, :], X[:, g, CC:CC + CX], start=True, stop=False)
                    pe.matmul(o_, F[:, g, 0, 1:L + 1, :].rearrange("p j h -> p (j h)"), H[:, g, 0, :], start=False, stop=False)
                    mm = pe.matmul(o_, F[:, g, 1, 1:L + 1, :].rearrange("p j h -> p (j h)"), H[:, g, 1, :], start=False, stop=True)
                mm.then_inc(sm("y_done"), 1)

            pe.wait_ge(*past("bank_free1", G_SSM + 4))
            with pe.Fori(0, NQ) as q:
                ssm_quad(q)

            def pool_matmuls(g):
                pe.wait_ge(sm("diff_ready"), g * 2 + 2)
                pe.wait_ge(sm("pw_loaded"), g * 16 + 16)
                pe.wait_ge(*past("pool_evicted", g * 2))
                for mo in range(2):
                    for n in range(2):
                        for k in range(2):
                            mm = pe.matmul(ps[:, 4 + 2 * mo + n, :], pw_in[:, k, 128 * mo:128 * (mo + 1)],
                                           up_in[:, k, NB * n:NB * (n + 1)], start=k == 0, stop=k == 1)
                    mm.then_inc(sm("pool_done"), 1)

            pe.wait_ge(sm("gate_row_ready"), 1)
            pe.wait_ge(*past("y_evicted", NQ))
            with pe.Fori(0, 4) as i2:
                for sub in range(2):
                    for half in range(2):
                        pe.wait_ge(sm("w_lo_ready"), i2 * 4 + (T_GLU + 2 * sub + half + 1))
                        pe.wait_ge(*past(f"bank_free{half}", i2 * 2 + (G_GLU + sub)))
                        for k in range(8):
                            if half == 0:
                                pe.wait_ge(*past("y_ready", k + 1))
                            w = (w_hi[half][:, 128 * k:128 * (k + 1)], w_lo[half][:, 128 * k:128 * (k + 1)])
                            for n in range(2):
                                a = (act_hi[:, k, NB * n:NB * (n + 1)], act_lo[:, k, NB * n:NB * (n + 1)])
                                mm = three(2 * half + n, NB, w, a, k == 0, k == 7)
                        mm.then_inc(sm("w_used"), 1)
                pool_matmuls(i2)

            pe.wait_ge(*past("pool_evicted", 8))
            for q in range(4):
                mm = pe.matmul(ps[:, 4 + q, :], ones[32 * q:32 * q + 1, :], gate_row[32 * q:32 * q + 1, :], start=True, stop=True)
            mm.then_inc(sm("gate_done"), 1)
            pe.wait_ge(sm("gate_bc_ready"), 1)

            with pe.Fori(0, 4) as i:
                for j, a_ in enumerate(OUT_ORDER):
                    pe.wait_ge(sm("w_lo_ready"), i * 8 + (T_OUT + j + 1))
                    s = j % 2
                    for kk in range(2):
                        k = 2 * a_ + kk
                        if k >= 8:
                            pe.wait_ge(sm("br_ready"), k - 8 + 1)
                        else:
                            pe.wait_ge(sm("pbr_ready"), k + 1)
                        for tok in range(8):
                            first, last = (j == 0 and kk == 0), (j == 7 and kk == 1)
                            if first:
                                pe.wait_ge(sm("out_free"), i * 8 + tok + 1)
                            cols = slice(128 * tok, 128 * (tok + 1))
                            ah, al = act_hi[:, k, cols], act_lo[:, k, cols]
                            wh, wl = w_hi[s][:, NB * kk:NB * (kk + 1)], w_lo[s][:, NB * kk:NB * (kk + 1)]
                            pe.matmul(ps[:, tok, :], ah, wh, start=first, stop=False)
                            pe.matmul(ps[:, tok, :], ah, wl, start=False, stop=False)
                            mm = pe.matmul(ps[:, tok, :], al, wh, start=False, stop=last)
                            if last and tok < 7:
                                mm.then_inc(sm("tok_done"), 1)
                    mm.then_inc(sm("w_used"), 1)

        @block.scalar
        def _(act):
            act.sem_inc(sm("bank_free0"), START["bank_free0"])
            act.sem_inc(sm("bank_free1"), START["bank_free1"])
            act.sem_inc(sm("strip_evicted"), START["strip_evicted"])
            act.sem_inc(sm("y_evicted"), START["y_evicted"])
            act.sem_inc(sm("zst_stored0"), START["zst_stored0"])
            act.sem_inc(sm("zst_stored1"), START["zst_stored1"])
            act.sem_inc(sm("yst_stored"), START["yst_stored"])

            def split_hi(t, s, n_loaded):
                act.wait_ge(sm(f"w_loaded{s}"), n_loaded)
                if not isinstance(t, int) or t >= 2:
                    act.wait_ge(sm("w_used"), t - 1)
                act.activation(w_hi[s][:, :], w_raw[s][:, :], ACT.Copy).then_inc(sm("w_hi_ready"), 1)

            def tiles(base, per, i, js):
                for j in js:
                    t = (i * per + (base + j))
                    split_hi(t, (base + j) % 2, i * (16 * per // 2) + 16 * ((base + j) // 2 + 1))

            act.wait_ge(sm("vT_ready"), 1)
            act.activation(cs[:, :, :].rearrange("p k v -> p v k"), vT[:, V_C:V_C + 32].rearrange("p (v k) -> p v k", v=2),
                           ACT.Silu).then_inc(sm("cs_ready"), 1)

            def x_norm(i, s, n_sq, n_ld):
                act.wait_ge(sm(f"xt_loaded{s}"), n_ld)
                for h in range(4):
                    if not isinstance(n_sq, int) or n_sq > 0 or h > 0:
                        act.wait_ge(sm("sq_chain"), n_sq + h)
                    act.activation(sq_junk[:, :], x_tile[s][:, NB * h:NB * (h + 1)], ACT.Square,
                                   accum_out=ssq[:, s, h:h + 1]).then_inc(sm("sq_chain"), 1)

            def x_evict(i, dst, col):
                for kb in (0, 2):
                    act.wait_ge(sm("tr_done0"), 2 * i + kb // 2 + 1)
                    act.activation(dst[:, 4 * kb:4 * kb + 4, ds(col, 128)],
                                   ps[:, 2, :].rearrange("p (r n) -> p r n", r=4), ACT.Copy).then_inc(sm("tr_evicted0"), 1)

            for s in range(2):
                x_norm(s, s, 4 * s, 16)
            for s in range(2):
                x_evict(s, cT, 128 * s)
                x_norm(2 + s, s, 8 + 4 * s, 32)
            with act.Fori(0, 3) as i:
                for s in range(2):
                    x_evict(i * 2 + (2 + s), xT, i * 256 + 128 * s)
                    x_norm(i * 2 + (4 + s), s, i * 8 + (16 + 4 * s), i * 16 + 48)
            for s in range(2):
                x_evict(8 + s, xT, 768 + 128 * s)

            for n_, (dst, src, scale) in enumerate((("sh", "y", 0.5), ("s1", "y", 1.0), ("wi", "y8", 1.0), ("wr", "y8", 0.5))):
                act.wait_ge(sm("y_reduced"), 1 if src == "y" else 2)
                act.activation(pp[dst][:, :], pp[src][:, :], ACT.Sin, scale=scale).then_inc(sm("sin_done"), 1)
            nb = [8, 8, 2] + [8] * 4 + [3]
            for r in range(8):
                act.wait_ge(sm("pt_done"), r + 1)
                src = ps[0:64, 4, 0:64 * nb[r]]
                if r < 3:
                    dst = q_st[0:64, :, :, 4 * r:4 * r + nb[r] // 2].rearrange("p g ri j -> p j ri g")
                    src = src.rearrange("p (j ri g) -> p j ri g", ri=2, g=SG)
                    for ri in range(2):
                        e_ = act.activation(dst[:, :, ri, :], src[:, :, ri, :], ACT.Copy)
                elif r < 7:
                    dst = b_st[0:64, :, :, 4 * (r - 3):4 * (r - 3) + 4].rearrange("p g ri h -> p h ri g")
                    src = src.rearrange("p (h ri g) -> p h ri g", ri=2, g=SG)
                    for ri in range(2):
                        e_ = act.activation(dst[:, :, ri, :], src[:, :, ri, :], ACT.Copy)
                else:
                    e_ = act.activation(wT[0:64, :, :].rearrange("p w g -> p (w g)"), src, ACT.Copy)
                e_.then_inc(sm("pf_evicted"), 1)
            for oc in range(8):
                act.wait_ge(sm("ct_done"), oc + 1)
                act.activation(c_st[:, 8 * oc:8 * oc + 8, :, :].rearrange("p g e h -> p e g h"),
                               ps[:, 6, 0:384].rearrange("p (e g h) -> p e g h", e=3, g=8), ACT.Copy).then_inc(sm("ct_evicted"), 1)
            act.wait_ge(sm("pf_evicted"), 8)
            act.wait_ge(sm("pbk_evicted"), 8)
            act.wait_ge(sm("q_zeroed"), 1)
            act.wait_ge(sm("ct_evicted"), 8)
            act.dma_start(qtab, q_st[:, :, :, :]).then_inc(sm("params_stored"), 16)
            act.dma_start(btab, b_st[:, :, :, :]).then_inc(sm("params_stored"), 16)
            act.dma_start(ctab, c_st[:, :, :, :]).then_inc(sm("params_stored"), 16)

            act.wait_ge(sm("ada_used"), 32)
            for q in range(4):
                e_ = act.activation(ada_row[32 * q:32 * q + 2, :, :], ps[32 * q:32 * q + 2, 0:2, :], ACT.Copy)
            e_.then_inc(sm("ada_row_ready"), 1)

            def h_split(ks):
                with act.Fori(*ks) as k:
                    act.wait_ge(sm("h_scaled"), k + 1)
                    act.activation(act_hi[:, ds(k, 1), :], xT[:, ds(k, 1), :], ACT.Copy).then_inc(sm("h_hi_ready"), 1)

            def u_evict(i):
                act.wait_ge(sm("u_stored"), i * 16)
                for m in range(2):
                    if m == 0:
                        act.wait_ge(sm("m0_done"), i + (G_SSM + 1))
                    else:
                        act.wait_ge(sm("w_used"), i * 4 + (T_SSM + 4))
                    for n in range(2):
                        act.activation(ust[:, m, :, CC + 64 * n:CC + 64 * (n + 1)],
                                       ps[:, 2 * m + n, :].rearrange("p (c t) -> p t c", t=L), ACT.Copy)
                    for c0 in (0, SEQC):
                        e_ = act.activation(ust[:, m, :, c0:c0 + CC],
                                            ps[:, 4 + m, 0:TC].rearrange("p (c t) -> p t c", t=L), ACT.Copy)
                    e_.then_inc(sm(f"bank_free{m}"), 1)
                act.wait_ge(*past("bank_free1", i + 1))
                act.dma_start(u_scr.rearrange("(a m p) t c -> p a m (t c)", m=2, p=128)[:, ds(i, 1), :, :].rearrange("p o m f -> p (o m) f"),
                              ust[:, :, :, :].rearrange("p m t c -> p m (t c)")).then_inc(sm("u_stored"), 16)

            split_hi(0, 0, 16)
            split_hi(1, 1, 16)
            for j in range(4):
                act.wait_ge(sm("hc_scaled"), 4 * (j + 1))
                act.activation(c_hi[:, 4 * j:4 * j + 4, :], cT[:, 4 * j:4 * j + 4, :], ACT.Copy).then_inc(sm("hc_hi_ready"), 1)
            h_split((0, 8))
            split_hi(2, 0, 32)
            h_split((8, 12))
            split_hi(3, 1, 32)
            h_split((12, 16))
            split_hi(4, 0, 48)
            act.wait_ge(sm("tabs_free"), 1)
            u_evict(0)
            with act.Fori(1, 4) as i:
                tiles(T_SSM, 4, i, (1, 2, 3, 4))
                u_evict(i)

            def evict_store(i, g0, t0, u0, func, dst, rows):
                for m in range(2):
                    if m == 0:
                        act.wait_ge(sm("m0_done"), i + (g0 + 1))
                    else:
                        act.wait_ge(sm("w_used"), i * 4 + (t0 + 4))
                    for n in range(2):
                        act.wait_ge(*past(f"zst_stored{n}", i * 32 + 16 * (u0 + m)))
                        e_ = act.activation(z_st[n][:, :], ps[:, 2 * m + n, :], func)
                        e_.then_inc(sm(f"zst_ready{n}"), 1)
                        act.wait_ge(sm(f"zst_ready{n}"), i * 2 + (u0 + m + 1))
                        act.dma_start(dst.rearrange("(a m p) t -> p a m t", m=2, p=128)[:, ds(i, 1), m, NB * n:NB * (n + 1)],
                                      z_st[n][:, :].unsqueeze(1)).then_inc(sm(f"zst_stored{n}"), 16)
                    act.wait_ge(sm("zst_ready1"), i * 2 + (u0 + m + 1))
                    act.sem_inc(sm(f"bank_free{m}"), 1)

            with act.Fori(0, 8) as i:
                tiles(T_Z, 4, i, (1, 2, 3, 4))
                evict_store(i, G_Z, T_Z, 0, ACT.Silu, z_scr, D)
            with act.Fori(0, 4) as i:
                tiles(T_POOL, 4, i, (1, 2, 3, 4))
                evict_store(i, G_POOL, T_POOL, 16, ACT.Copy, up_scr, PW)

            act.wait_ge(sm("ada_used"), 48)
            act.wait_ge(*past("zst_stored0", 16 * 24))
            act.wait_ge(*past("zst_stored1", 16 * 24))
            for q in range(4):
                e_ = act.activation(gate_row[32 * q:32 * q + 1, :], ps[32 * q:32 * q + 1, 0, :], ACT.Copy)
            e_.then_inc(sm("gate_row_ready"), 1)

            def load_quad(q):
                u_q = u_scr.rearrange("(q g h) t c -> q t h g c", g=GQ, h=SH)
                for t_ in range(L):
                    act.dma_start(X[SH * t_:SH * (t_ + 1), :, :], u_q[ds(q, 1), t_, :, :, :].rearrange("o h g c -> (o h) g c")) \
                        .then_inc(sm("xq_loaded"), 16)
                for d_ in range(2):
                    for t_ in range(L):
                        src = p_scr.rearrange("q d t ri g n -> q d t (ri g n)")[ds(q, 1), d_, t_, :]
                        act.dma_start(PT[SH * t_:SH * (t_ + 1), d_, :, :].rearrange("p a b -> p (a b)"), src.partition_broadcast(SH) if False else src.to_broadcast([SH, 1024 // 2])) \
                            .then_inc(sm("ptab_loaded"), 16)
                        src = b_scr.rearrange("q d h ri g n -> q d h (ri g n)")[ds(q, 1), d_, :, :].rearrange("o h f -> (o h) f")
                        act.dma_start(BT[SH * t_:SH * (t_ + 1), d_, :, :].rearrange("p a b -> p (a b)"), src).then_inc(sm("ptab_loaded"), 16)
                act.dma_start(CQ[:, :, :, :], ctab[:, ds(q * GQ, GQ), :, :]).then_inc(sm("cq_loaded"), 16)
                act.dma_start(QQ[:, :, :, :], qtab[:, ds(q * GQ, GQ), :, :]).then_inc(sm("cq_loaded"), 16)
                for d_ in range(2):
                    rows = slice(64 * d_, 64 * d_ + 64)
                    act.dma_start(BZ[rows, d_, :, :, :], btab[rows, ds(q * GQ, GQ), :, :]).then_inc(sm("bz_loaded"), 16)

            act.wait_ge(sm("bz_zeroed"), 1)
            act.wait_ge(sm("p_stored"), 16 * 24)
            act.wait_ge(sm("u_stored"), 16 * 4)
            with act.Fori(0, NQ) as q:
                act.wait_ge(*past("y_done", q))
                act.wait_ge(*past("yst_stored", q * 128))
                load_quad(q)
                for r in range(2):
                    act.wait_ge(sm("strip_done"), q * 2 + r + 1)
                    act.activation(strip[:, 2 * r:2 * r + 2, :, :].rearrange("p g a b -> p g (a b)"),
                                   ps[0:SH, 6, 0:2 * LANES * SH].rearrange("p (g f) -> p g f", g=2), ACT.Copy) \
                        .then_inc(sm("strip_evicted"), 1)
                act.wait_ge(*past("strip_evicted", q * 2 + 2))
                act.wait_ge(sm("e_ready"), q + 1)
                for t_ in range(L):
                    act.dma_start(M[SH * t_:SH * (t_ + 1), :, :],
                                  strip[:, :, L - 1 - t_:2 * L - 1 - t_, :].rearrange("p g a b -> p g (a b)")).then_inc(sm("m_loaded"), 16)
                act.wait_ge(*past("y_done", q + 1))
                act.activation(yst[:, :, :].rearrange("p g c -> p (g c)"), ps[:, 7, :], ACT.Copy).then_inc(sm("y_evicted"), 1)
                act.wait_ge(*past("y_evicted", q + 1))
                y_q = y_scr.rearrange("(q g h) t c -> q t h g c", g=GQ, h=SH)
                for t_ in range(L):
                    act.dma_start(y_q[ds(q, 1), t_, :, :, :].rearrange("o h g c -> (o h) g c"), yst[SH * t_:SH * (t_ + 1), :, :]) \
                        .then_inc(sm("yst_stored"), 16)

            with act.Fori(0, 8) as k:
                act.wait_ge(sm("skip_ready"), k + 1)
                act.activation(y_in[:, :], y_in[:, :], ACT.Gelu_apprx_tanh).then_inc(sm("gelu_ready"), 1)
                act.wait_ge(sm("gelu_ready"), k + 1)
                act.activation(act_hi[:, ds(k, 1), :], y_in[:, :].unsqueeze(1), ACT.Copy).then_inc(sm("y_hi_ready"), 1)

            with act.Fori(0, 8) as i:
                tiles(T_GLU, 2, i, (1, 2))
                act.wait_ge(sm("w_used"), i * 2 + (T_GLU + 2))
                act.wait_ge(sm("sg_used"), i + 1)
                for n in range(2):
                    act.activation(sg[:, NB * n:NB * (n + 1)], ps[:, 2 + n, :], ACT.Sigmoid,
                                   bias=b2col[:, ds(i, 1)]).then_inc(sm("sg_ready"), 1)
                act.wait_ge(sm("sg_ready"), i * 2 + 2)
                act.sem_inc(sm("bank_free1"), 1)
                act.wait_ge(sm("bf_ready"), i + 1)
                act.activation(act_hi[:, ds(i + 8, 1), :], bf[:, :].unsqueeze(1), ACT.Copy).then_inc(sm("br_hi_ready"), 1)

            split_hi(T_OUT + 1, 1, 16 * (T_OUT // 2 + 1))
            for k in range(8):
                act.wait_ge(sm(f"pb_loaded{k % 2}"), 16 * (k // 2 + 1))
                act.activation(act_hi[:, k, :], pb_in[k % 2][:, :], ACT.Copy).then_inc(sm("pbr_hi_ready"), 1)

            def square_sums(i, n_):
                for tok in range(8):
                    act.wait_ge(*past("y_added", i * 8 + tok + 1))
                    if not isinstance(n_, int) or n_ + tok > 0:
                        act.wait_ge(sm("ysq_chain"), n_ + tok)
                    act.activation(sq_junk2[:, :], yb[:, tok, :], ACT.Square, accum_out=ysq[:, tok, ds(i, 1)]) \
                        .then_inc(sm("ysq_chain"), 1)

            tiles(T_OUT, 8, 0, range(2, 9))
            square_sums(0, 0)
            with act.Fori(1, 3) as i:
                tiles(T_OUT, 8, i, range(1, 9))
                square_sums(i, i * 8)
            tiles(T_OUT, 8, 3, range(1, 8))
            square_sums(3, 24)

            for tok in range(8):
                act.wait_ge(sm("out_ready"), tok + 1)
                act.dma_start(out[0, 128 * tok:128 * (tok + 1), 0:3 * NB], yfin[tok // 4][:, tok % 4, :]).then_inc(sm("stored"), 16)
                act.dma_start(out[0, 128 * tok:128 * (tok + 1), 3 * NB:], yb[:, tok, :]).then_inc(sm("stored"), 16)
            act.wait_ge(sm("stored"), 16 * 16)

        @block.vector
        def _(dve):
            dve.sem_inc(sm("s_read"), START["s_read"])
            dve.sem_inc(sm("pool_evicted"), START["pool_evicted"])
            dve.sem_inc(sm("hs_ready"), START["hs_ready"])
            dve.sem_inc(sm("y_ready"), START["y_ready"])
            dve.sem_inc(sm("y_added"), START["y_added"])

            chained = [0, 0]

            def link(ins):
                chained[0] += 1
                ins.then_inc(sm("dve_chain"), 1)
                dve.wait_ge(sm("dve_chain"), chained[1] + chained[0])

            class repeat:
                def __init__(self, lo, hi, per):
                    self.lo, self.hi, self.per, self.f = lo, hi, per, dve.Fori(lo, hi)

                def __enter__(self):
                    i = self.f.__enter__()
                    self.base = chained[0]
                    chained[1] = i * self.per
                    chained[0] -= self.per * self.lo
                    return i

                def __exit__(self, *a):
                    chained[0] += self.per * self.lo
                    assert chained[0] - self.base == self.per, chained[0] - self.base
                    chained[0], chained[1] = self.base + self.per * (self.hi - self.lo), 0
                    return self.f.__exit__(*a)

            TT, TS, STT = dve.tensor_tensor, dve.tensor_scalar, dve.scalar_tensor_tensor

            def rsqrt(r, v, tmp):
                link(TS(r.bitcast(i32), v.bitcast(i32), -0.5, 1597463007.0, ALU.mult, ALU.add))
                for _ in range(3):
                    link(STT(tmp, r, v, r, ALU.mult, ALU.mult))
                    link(TS(tmp, tmp, -0.5, 1.5, ALU.mult, ALU.add))
                    link(TT(r, r, tmp, ALU.mult))

            dve.wait_ge(sm("vT_done"), 1)
            dve.tensor_copy(vT[:, :], ps[:, 7, 0:128]).then_inc(sm("vT_ready"), 1)
            dve.wait_ge(sm("vT_ready"), 1)
            dve.tensor_copy(b2col[:, :], vT[:, V_GLUB + 8:V_GLUB + 16]).then_inc(sm("b2_ready"), 1)

            def x_scale(i, s):
                dve.wait_ge(sm("sq_chain"), i * 4 + 4)
                link(dve.tensor_reduce(rs[:, 0:1], ssq[:, s, :], mybir.AxisListType.X, ALU.add))
                link(TS(rs[:, 1:2], rs[:, 0:1], 1.0 / D, EPS, ALU.mult, ALU.add))
                rsqrt(rs[:, 2:3], rs[:, 1:2], rs[:, 3:4])
                TS(x_tile[s][:, :], x_tile[s][:, :], rs[:, 2:3], None, ALU.mult).then_inc(sm("xn_ready"), 1)

            def x_evict(i, dst, col):
                for kb in (1, 3):
                    dve.wait_ge(sm("tr_done1"), 2 * i + kb // 2 + 1)
                    dve.tensor_copy(dst[:, 4 * kb:4 * kb + 4, ds(col, 128)],
                                    ps[:, 3, :].rearrange("p (r n) -> p r n", r=4)).then_inc(sm("tr_evicted1"), 1)

            for s in range(2):
                x_scale(s, s)
                x_evict(s, cT, 128 * s)
            with repeat(1, 5, 2 * 12) as i:
                for s in range(2):
                    x_scale(i * 2 + s, s)
                    x_evict(i * 2 + s, xT, i * 256 + (128 * s - 256))

            P = {n_: t[:, :] for n_, t in pp.items()}

            def exp(dst, x_, n_, r_, p_, bits):
                MAGIC = 12582912.0
                link(TS(r_, x_, -88.0, 89.0, ALU.max, ALU.min))
                link(TS(n_, r_, 1.0 / math.log(2.0), MAGIC, ALU.mult, ALU.add))
                link(TS(n_, n_, MAGIC, None, ALU.subtract))
                link(STT(r_, n_, -0.693359375, r_, ALU.mult, ALU.add))
                link(STT(r_, n_, 2.12194440e-4, r_, ALU.mult, ALU.add))
                link(TS(p_, r_, 1.0 / 5040, None, ALU.mult))
                for k in (720, 120, 24, 6, 2, 1):
                    link(STT(p_, p_, 1.0 / k, r_, ALU.add, ALU.mult))
                link(TS(bits, n_, 127.0, 8388608.0, ALU.add, ALU.mult))
                link(STT(dst, p_, 1.0, bits.bitcast(f32), ALU.add, ALU.mult))

            def reduce_angle(dst, x_, n_):
                MAGIC = 12582912.0
                link(TS(n_, x_, 1.0 / (2 * math.pi), MAGIC, ALU.mult, ALU.add))
                link(TS(n_, n_, MAGIC, None, ALU.subtract))
                c1 = 6.28125
                c2 = float(np.float32(np.floor((2 * math.pi - c1) * 2 ** 21) / 2 ** 21))
                c3 = 2 * math.pi - c1 - c2
                link(STT(dst, n_, -c1, x_, ALU.mult, ALU.add))
                link(STT(dst, n_, -c2, dst, ALU.mult, ALU.add))
                link(STT(dst, n_, -c3, dst, ALU.mult, ALU.add))
                return TS(dst, dst, -math.pi, math.pi, ALU.max, ALU.min)

            dve.wait_ge(sm("lam_loaded"), 16 * 3)
            col = lambda i_: dt_col[:, i_:i_ + 1]
            exp(col(4), col(0), col(1), col(2), col(3), dt_bits[:, :])
            link(TS(P["zr"], P["lre"], col(4), None, ALU.mult))
            link(TS(P["zi"], P["lim"], col(4), None, ALU.mult))
            link(reduce_angle(P["y"], P["zi"], P["n"]))
            dve.sem_inc(sm("y_reduced"), 1)
            link(TS(P["t"], P["y"], 8.0, None, ALU.mult))
            link(reduce_angle(P["y8"], P["t"], P["n"]))
            dve.sem_inc(sm("y_reduced"), 1)
            exp(P["e"], P["zr"], P["n"], P["r"], P["p"], e_bits[:, :])
            link(TT(P["r8"], P["e"], P["e"], ALU.mult))
            link(TT(P["r8"], P["r8"], P["r8"], ALU.mult))
            link(TT(P["r8"], P["r8"], P["r8"], ALU.mult))
            dve.wait_ge(sm("sin_done"), 4)
            link(STT(P["cm"], P["sh"], -2.0, P["sh"], ALU.mult, ALU.mult))
            link(STT(P["t"], P["wr"], -2.0, P["wr"], ALU.mult, ALU.mult))
            link(TS(P["wr"], P["t"], 1.0, None, ALU.add))
            link(TS(P["wi"], P["wi"], -1.0, None, ALU.mult))
            a_r, a_i = pw_[:, 1, 0, :], pw_[:, 1, 1, :]
            link(TT(P["t"], P["e"], P["cm"], ALU.mult))
            link(STT(P["t2"], P["e"], -1.0, P["t"], ALU.add, ALU.add))
            link(TT(a_r, P["t"], P["e"], ALU.add))
            link(TT(a_i, P["e"], P["s1"], ALU.mult))
            link(TT(P["t"], P["lre"], P["lre"], ALU.mult))
            link(TT(P["t3"], P["lim"], P["lim"], ALU.mult))
            link(TT(P["t"], P["t"], P["t3"], ALU.add))
            link(dve.reciprocal(P["inv"], P["t"]))
            link(TT(P["kr"], P["t2"], P["lre"], ALU.mult))
            link(TT(P["t"], a_i, P["lim"], ALU.mult))
            link(TT(P["kr"], P["kr"], P["t"], ALU.add))
            link(TT(P["kr"], P["kr"], P["inv"], ALU.mult))
            link(TT(P["ki"], a_i, P["lre"], ALU.mult))
            link(TT(P["t"], P["t2"], P["lim"], ALU.mult))
            link(TT(P["ki"], P["ki"], P["t"], ALU.subtract))
            link(TT(P["ki"], P["ki"], P["inv"], ALU.mult))
            dve.memset(pw_[:, 0, 0, :], 1.0)
            dve.memset(pw_[:, 0, 1, :], 0.0)
            for m in (1, 2, 4):
                src = pw_[:, 1:m + 1, :, :]
                link(TT(ptmp[:, 0, 0:m, :, :], src, pw_[:, m:m + 1, 0:1, :].broadcast_to([128, m, 2, SN]), ALU.mult))
                link(TT(ptmp[:, 1, 0:m, :, :], src, pw_[:, m:m + 1, 1:2, :].broadcast_to([128, m, 2, SN]), ALU.mult))
                link(TT(pw_[:, m + 1:2 * m + 1, 0, :], ptmp[:, 0, 0:m, 0, :], ptmp[:, 1, 0:m, 1, :], ALU.subtract))
                link(TT(pw_[:, m + 1:2 * m + 1, 1, :], ptmp[:, 0, 0:m, 1, :], ptmp[:, 1, 0:m, 0, :], ALU.add))
            dve.wait_ge(sm("b_loaded"), 32)
            br_, bi_ = (b_nat[:, i_, :, :].rearrange("p n h -> p h n") for i_ in range(2))
            kr_, ki_ = (P[n_].unsqueeze(1).broadcast_to([128, SH, SN]) for n_ in ("kr", "ki"))
            for o_, (u0, v0), (u1, v1), op in ((0, (br_, kr_), (bi_, ki_), ALU.subtract), (1, (bi_, kr_), (br_, ki_), ALU.add)):
                link(TT(b_tmp[:, 0, :, :], u0, v0, ALU.mult))
                link(TT(b_tmp[:, 1, :, :], u1, v1, ALU.mult))
                link(TT(b_bar[:, :, o_, :], b_tmp[:, 0, :, :], b_tmp[:, 1, :, :], op))
            dve.sem_inc(sm("pw_ready"), 1)
            link(dve.memset(q_st[0:64, :, :, JP - 1], 0.0))
            link(dve.memset(q_st[64:128, :, :, 0], 0.0))
            dve.sem_inc(sm("q_zeroed"), 1)
            nb = [8, 8, 2] + [8] * 4 + [3]
            for r in range(8):
                dve.wait_ge(sm("pt_done"), r + 1)
                src = ps[64:128, 5, 0:64 * nb[r]]
                if r < 3:
                    src = src.rearrange("p (j ri g) -> p j ri g", ri=2, g=SG)
                    n_, top = nb[r] // 2, L + 1 - 4 * r
                    dst = q_st[64:128, :, :, top:(top - n_ if top - n_ >= 0 else None):-1].rearrange("p g ri j -> p j ri g")
                    for ri in range(2):
                        e_ = dve.tensor_copy(dst[:, :, ri, :], src[:, :, ri, :])
                elif r < 7:
                    dst = b_st[64:128, :, :, 4 * (r - 3):4 * (r - 3) + 4].rearrange("p g ri h -> p h ri g")
                    src = src.rearrange("p (h ri g) -> p h ri g", ri=2, g=SG)
                    for ri in range(2):
                        e_ = dve.tensor_copy(dst[:, :, ri, :], src[:, :, ri, :])
                else:
                    e_ = dve.tensor_copy(wT[64:128, :, :].rearrange("p w g -> p (w g)"), src)
                e_.then_inc(sm("pbk_evicted"), 1)
            dve.wait_ge(sm("c_loaded"), 64)
            link(TS(c_nat[:, :, 1, :, :], c_nat[:, :, 1, :, :], -1.0, None, ALU.mult))
            link(TS(c_nat[:, :, 2, :, :], c_nat[:, :, 0, :, :], -1.0, None, ALU.mult))
            dve.sem_inc(sm("c_ready"), 1)

            dve.wait_ge(sm("mod_done"), 1)
            for q in range(4):
                e_ = TT(modT[:, :, 4 * q:4 * q + 4, :], ps[:, 2 + q, 0:16].rearrange("p (h r v) -> p h r v", h=2, r=4),
                        vT[:, V_ADAB:V_ADAB + 32].rearrange("p (h k) -> p h k", h=2)[:, :, 4 * q:4 * q + 4].unsqueeze(3)
                        .broadcast_to([128, 2, 4, 2]), ALU.add)
            link(e_)
            dve.sem_inc(sm("mod_evicted"), 1)
            link(STT(gmul[:, :, :], modT[:, 1, :, :], 1.0, vT[:, V_NG:V_NG + 16].unsqueeze(2).broadcast_to([128, KT, 2]),
                     ALU.add, ALU.mult))

            def split_lo(t, s):
                dve.wait_ge(sm("w_hi_ready"), t + 1)
                TT(w_lo[s][:, :], w_raw[s][:, :], w_hi[s][:, :].bitcast(f32), ALU.subtract).then_inc(sm("w_lo_ready"), 1)

            def tiles(base, per, i, js):
                for j in js:
                    split_lo(i * per + (base + j), (base + j) % 2)

            def h_split(lo_, hi_):
                with dve.Fori(lo_, hi_) as k:
                    TS(xT[:, ds(k, 1), :], xT[:, ds(k, 1), :], gmul[:, ds(k, 1), 0], modT[:, 0, ds(k, 1), 0],
                       ALU.mult, ALU.add).then_inc(sm("h_scaled"), 1)
                    dve.wait_ge(sm("h_hi_ready"), k + 1)
                    TT(act_lo[:, ds(k, 1), :], xT[:, ds(k, 1), :], act_hi[:, ds(k, 1), :].bitcast(f32), ALU.subtract) \
                        .then_inc(sm("h_ready"), 1)

            split_lo(0, 0)
            split_lo(1, 1)
            for k in range(KT):
                TS(cT[:, k, :], cT[:, k, :], gmul[:, k, 1:2], modT[:, 0, k, 1:2], ALU.mult, ALU.add).then_inc(sm("hc_scaled"), 1)
            for j in range(4):
                dve.wait_ge(sm("hc_hi_ready"), j + 1)
                TT(c_lo[:, 4 * j:4 * j + 4, :], cT[:, 4 * j:4 * j + 4, :], c_hi[:, 4 * j:4 * j + 4, :].bitcast(f32), ALU.subtract) \
                    .then_inc(sm("hc_ready"), 1)
            h_split(0, 8)
            split_lo(2, 0)
            h_split(8, 12)
            split_lo(3, 1)
            h_split(12, 16)
            split_lo(4, 0)
            dve.wait_ge(sm("params_stored"), 48)
            dve.sem_inc(sm("tabs_free"), 1)
            with dve.Fori(1, 4) as i:
                tiles(T_SSM, 4, i, (1, 2, 3, 4))
            with dve.Fori(0, 8) as i:
                tiles(T_Z, 4, i, (1, 2, 3, 4))
            with dve.Fori(0, 4) as i:
                tiles(T_POOL, 4, i, (1, 2, 3, 4))

            dve.wait_ge(sm("w_used"), T_Z)
            link(dve.memset(BZ[0:64, 1, :, :, :], 0.0))
            link(dve.memset(BZ[64:128, 0, :, :, :], 0.0))
            dve.sem_inc(sm("bz_zeroed"), 1)

            def ssm_quad(q):
                dve.wait_ge(sm("cq_loaded"), q * 32 + 32)
                dve.wait_ge(*past("y_done", q))
                t0, t1 = (TV[:, i_, 0:GQ * JP * SH].rearrange("p (g j h) -> p g j h", g=GQ, j=JP) for i_ in range(2))

                def cb(e):
                    return CQ[:, :, e:e + 1, :].broadcast_to([128, GQ, JP, SH])

                def qb(ri):
                    return QQ[:, :, ri, :].unsqueeze(3).broadcast_to([128, GQ, JP, SH])
                for ri, e0, e1 in ((0, 0, 1), (1, 1, 2)):
                    link(TT(t0, cb(e0), qb(0), ALU.mult))
                    link(TT(t1, cb(e1), qb(1), ALU.mult))
                    e_ = TT(F[:, :, ri, :, :], t0, t1, ALU.add)
                    link(e_)
                dve.sem_inc(sm("f_ready"), 1)
                dve.wait_ge(sm("r_ready"), q + 1)
                for r in range(2):
                    dve.wait_ge(*past("s_done", q * 2 + r + 1))
                    src = ps[:, 4:6, 0:2 * SEQC].rearrange("p g (ri c) -> p g ri c", ri=2)
                    t0, t1 = (TV[:, i_, 0:4 * SEQC].rearrange("p (g ri c) -> p g ri c", g=2, ri=2) for i_ in range(2))
                    rr, ri_ = (R[:, 2 * r:2 * r + 2, i_:i_ + 1, :].broadcast_to([128, 2, 2, SEQC]) for i_ in range(2))
                    link(TT(t0, src, rr, ALU.mult))
                    link(TT(t1, src, ri_, ALU.mult))
                    dve.sem_inc(sm("s_read"), 1)
                    link(TT(G[:, 2 * r:2 * r + 2, 0, :], t0[:, :, 0, :], t1[:, :, 1, :], ALU.subtract))
                    link(TT(G[:, 2 * r:2 * r + 2, 1, :], t0[:, :, 1, :], t1[:, :, 0, :], ALU.add))
                for g in range(GQ):
                    for ri in range(2):
                        e_ = dve.tensor_tensor_scan(G[:, g, ri, :], wT[:, 2, ds(q * GQ + g, 1)].broadcast_to([128, SEQC]),
                                                    G[:, g, ri, :], 0.0, ALU.mult, ALU.add)
                link(e_)
                src = G[:, :, :, CC - 1:SEQC - 1]
                t0, t1 = (TV[:, i_, :].rearrange("p (g ri c) -> p g ri c", g=GQ, ri=2) for i_ in range(2))
                rr, ri_ = (R[:, :, i_:i_ + 1, CC - 1:SEQC - 1].broadcast_to([128, GQ, 2, CX]) for i_ in range(2))
                link(TT(t0, src, rr, ALU.mult))
                link(TT(t1, src, ri_, ALU.mult))
                for rows, way in ((slice(0, 64), slice(None)), (slice(64, 128), slice(None, None, -1))):
                    TT(H[rows, :, 0, :], t0[rows, :, 0, way], t1[rows, :, 1, way], ALU.add)
                    e_ = TT(H[rows, :, 1, :], t0[rows, :, 1, way], t1[rows, :, 0, way], ALU.subtract)
                link(e_)
                dve.sem_inc(sm("hs_ready"), 1)

            with repeat(0, NQ, 6 + 8 + 1 + 3) as q:
                ssm_quad(q)

            with dve.Fori(0, 8) as k:
                dve.wait_ge(sm("yu_loaded"), k * 32 + 32)
                STT(y_in[:, :], u_in[:, :, :].rearrange("p t c -> p (t c)"), vT[:, ds(k + V_D, 1)], y_in[:, :], ALU.mult, ALU.add) \
                    .then_inc(sm("skip_ready"), 1)
                dve.wait_ge(sm("y_hi_ready"), k + 1)
                TT(act_lo[:, ds(k, 1), :], y_in[:, :].unsqueeze(1), act_hi[:, ds(k, 1), :].bitcast(f32), ALU.subtract) \
                    .then_inc(sm("y_ready"), 1)

            dve.wait_ge(*past("y_ready", 8))
            dve.sem_inc(sm("sg_used"), 1)

            def glu_group(i):
                tiles(T_GLU, 2, i, (1,))
                dve.wait_ge(sm("w_used"), i * 2 + (T_GLU + 1))
                for n in range(2):
                    e_ = TS(br[:, NB * n:NB * (n + 1)], ps[:, n, :], vT[:, ds(i + V_GLUB, 1)], None, ALU.add)
                e_.then_inc(sm("bank_free0"), 1)
                tiles(T_GLU, 2, i, (2,))
                dve.wait_ge(sm("sg_ready"), i * 2 + 2)
                dve.wait_ge(*past("bank_free0", i + (G_GLU + 1)))
                TT(br[:, :], br[:, :], sg[:, :], ALU.mult).then_inc(sm("sg_used"), 1)
                dve.wait_ge(sm("sg_used"), i + 2)
                dve.wait_ge(sm("zb_loaded"), i * 16 + 16)
                TT(bf[:, :].rearrange("p (c t) -> p t c", t=L), br[:, :].rearrange("p (t c) -> p t c", t=L),
                   z_in[:, :].rearrange("p (c t) -> p t c", t=L), ALU.mult).then_inc(sm("bf_ready"), 1)
                dve.wait_ge(sm("br_hi_ready"), i + 1)
                TT(act_lo[:, ds(i + 8, 1), :], bf[:, :].unsqueeze(1), act_hi[:, ds(i + 8, 1), :].bitcast(f32), ALU.subtract) \
                    .then_inc(sm("br_ready"), 1)

            with dve.Fori(0, 4) as g:
                for sub in range(2):
                    glu_group(g * 2 + sub)
                for mo in range(2):
                    dve.wait_ge(sm("pool_done"), g * 2 + mo + 1)
                    dve.wait_ge(sm("zp_loaded"), g * 32 + 16 * (mo + 1))
                    dve.wait_ge(sm("bp_free"), g + 1)
                    for n in range(2):
                        e_ = STT(bp[:, mo, NB * n:NB * (n + 1)], ps[:, 4 + 2 * mo + n, :], vT[:, ds(g * 2 + (V_PS + mo), 1)],
                                 zp_in[:, NB * n:NB * (n + 1)], ALU.mult, ALU.mult)
                    e_.then_inc(sm("pool_evicted"), 1)

            tiles(T_OUT, 8, 0, (1,))
            dve.wait_ge(sm("gate_done"), 1)
            dve.wait_ge(sm("adab_loaded"), 16)
            for q in range(4):
                e_ = TT(gate_bc[:, NB * q:NB * (q + 1)], ps[:, 4 + q, :], adab_bc[:, NB * q:NB * (q + 1)], ALU.add)
            e_.then_inc(sm("gate_bc_ready"), 1)
            dve.wait_ge(sm("gate_bc_ready"), 1)
            dve.sem_inc(sm("out_free"), 8)
            for k in range(8):
                dve.wait_ge(sm("pbr_hi_ready"), k + 1)
                TT(act_lo[:, k, :], pb_in[k % 2][:, :], act_hi[:, k, :].bitcast(f32), ALU.subtract).then_inc(sm("pbr_ready"), 1)

            def out_evict(i):
                dve.wait_ge(sm("yb_stored"), i * 16)
                if not isinstance(i, int) or i > 0:
                    dve.wait_ge(sm("ysq_chain"), i * 8)
                for tok in range(8):
                    if tok < 7:
                        dve.wait_ge(sm("tok_done"), i * 7 + tok + 1)
                    else:
                        dve.wait_ge(sm("w_used"), i * 8 + (T_OUT + 8))
                    TT(yb[:, tok, :], ps[:, tok, :], gate_bc[:, ds(i * NB, NB)], ALU.mult).then_inc(sm("out_free"), 1)
                dve.wait_ge(sm("xb_loaded"), i * 16 + 16)
                dve.wait_ge(sm("out_free"), i * 8 + 16)
                for tok in range(8):
                    TT(yb[:, tok, :], yb[:, tok, :], xb[:, tok, :], ALU.add).then_inc(sm("y_added"), 1)

            tiles(T_OUT, 8, 0, range(2, 9))
            out_evict(0)
            with dve.Fori(1, 3) as i:
                tiles(T_OUT, 8, i, range(1, 9))
                out_evict(i)
            tiles(T_OUT, 8, 3, range(1, 8))
            out_evict(3)

            dve.wait_ge(sm("fg_loaded"), 16)
            for tok in range(8):
                dve.wait_ge(sm("ysq_chain"), 24 + tok + 1)
                link(dve.tensor_reduce(rs[:, 0:1], ysq[:, tok, :], mybir.AxisListType.X, ALU.add))
                link(TS(rs[:, 1:2], rs[:, 0:1], 1.0 / D, EPS, ALU.mult, ALU.add))
                rsqrt(rs[:, 2:3], rs[:, 1:2], rs[:, 3:4])
                dve.wait_ge(sm(f"yfin_loaded{tok}"), 16)
                STT(yfin[tok // 4][:, tok % 4, :], yfin[tok // 4][:, tok % 4, :], rs[:, 2:3], fg_bc[:, 0:3 * NB], ALU.mult, ALU.mult)
                link(STT(yb[:, tok, :], yb[:, tok, :], rs[:, 2:3], fg_bc[:, 3 * NB:], ALU.mult, ALU.mult))
                dve.sem_inc(sm("out_ready"), 1)

        @block.gpsimd
        def _(gp):
            TT = gp.tensor_tensor
            chained = [0, 0]

            def link(ins):
                chained[0] += 1
                ins.then_inc(sm("gp_chain"), 1)
                gp.wait_ge(sm("gp_chain"), chained[1] + chained[0])

            class repeat:
                def __init__(self, lo, hi, per):
                    self.lo, self.hi, self.per, self.f = lo, hi, per, gp.Fori(lo, hi)

                def __enter__(self):
                    i = self.f.__enter__()
                    self.base = chained[0]
                    chained[1] = i * self.per
                    return i

                def __exit__(self, *a):
                    assert self.lo == 0 and chained[0] - self.base == self.per, chained[0] - self.base
                    chained[0], chained[1] = self.base + self.per * self.hi, 0
                    return self.f.__exit__(*a)

            gp.memset(ident[:, :], 0.0).then_inc(sm("ident_ready"), 1)
            gp.memset(ones[:, :], 1.0).then_inc(sm("ones_ready"), 1)
            gp.wait_ge(sm("ident_ready"), 1)
            gp.affine_select(out=ident[:, :], in_=ident[:, :], compare_op=ALU.not_equal, fill=1.0, base=0,
                             pattern=[[-1, 128]], channel_multiplier=1).then_inc(sm("ident_ready"), 1)

            def apart(semaphore, value):
                gp.wait_ge(semaphore, value)
                gp.sem_inc(sm("gp_passed"), 1)

            for s in range(2):
                gp.dma_start(x_tile[s][:, :], ctx_in[0, 128 * s:128 * (s + 1), :]).then_inc(sm(f"xt_loaded{s}"), 16)
            with gp.Fori(0, 4) as i:
                for s in range(2):
                    gp.wait_ge(sm("tr_done0"), i * 4 + 2 * s + 2)
                    apart(sm("tr_done1"), i * 4 + 2 * s + 2)
                    gp.dma_start(x_tile[s][:, :], x[0, ds(i * 256 + 128 * s, 128), :]).then_inc(sm(f"xt_loaded{s}"), 16)

            gp.dma_start(pp["lre"][:, :], lam_re.rearrange("o d g n -> (o d g) n")).then_inc(sm("lam_loaded"), 16)
            gp.dma_start(pp["lim"][:, :], lam_im.rearrange("o d g n -> (o d g) n")).then_inc(sm("lam_loaded"), 16)
            gp.dma_start(dt_col[:, 0:1], log_dt.rearrange("o d (g u) -> (o d g) u", u=1)).then_inc(sm("lam_loaded"), 16)
            for ri, b_ in enumerate((b_re, b_im)):
                gp.dma_start(b_nat[:, ri, :, :], b_.rearrange("o d g n h -> (o d g) n h")).then_inc(sm("b_loaded"), 16)
            gp.wait_ge(sm("pw_ready"), 1)
            for d_ in range(2):
                for g in range(GQ):
                    rows = slice(64 * d_ + g, 64 * d_ + 64, GQ)
                    src = pw_[rows, 0:L, :, :] if d_ == 1 else pw_[rows, L - 1::-1, :, :]
                    for ri in range(2):
                        gp.dma_start(p_scr[:, d_, :, ri, g, :], src[:, :, ri, :]).then_inc(sm("p_stored"), 16)
                    gp.dma_start(b_scr[:, d_, :, :, g, :].rearrange("q h ri n -> q (h ri) n"),
                                 b_bar[rows, :, :, :].rearrange("p h ri n -> p (h ri) n")).then_inc(sm("p_stored"), 16)
            gp.wait_ge(sm("p_stored"), 16 * 24)
            gp.wait_ge(sm("pt_done"), 8)
            for ri, c_ in enumerate((c_re, c_im)):
                for d_ in range(2):
                    gp.dma_start(c_nat[:, :, ri, d_, :], c_[0, d_].rearrange("(oc g) h n -> (g h) oc n", g=8)).then_inc(sm("c_loaded"), 16)

            gp.wait_ge(sm("w_used"), T_Z)
            gp.wait_ge(sm("bz_zeroed"), 1)
            link(gp.memset(R[:, :, 0, 0], 1.0))
            link(gp.memset(R[:, :, 1, 0], 0.0))
            spans = [(1, 1), (2, 2), (4, 4), (8, 8), (16, 16), (32, 32), (64, 64), (128, SEQC - 1 - 128)]
            with repeat(0, NQ, 4 * len(spans) + 1 + 8) as q:
                gp.wait_ge(*past("hs_ready", q))
                link(gp.tensor_copy(R[:, :, :, 1], wT[:, 0:2, ds(q * GQ, GQ)].rearrange("p w g -> p g w")))
                for m, n in spans:
                    src = R[:, :, :, 1:n + 1]
                    t0, t1 = (TG[:, i_, 0:GQ * 2 * n].rearrange("p (g ri n) -> p g ri n", g=GQ, ri=2) for i_ in range(2))
                    link(TT(t0, src, R[:, :, 0:1, m:m + 1].broadcast_to([128, GQ, 2, n]), ALU.mult))
                    link(TT(t1, src, R[:, :, 1:2, m:m + 1].broadcast_to([128, GQ, 2, n]), ALU.mult))
                    link(TT(R[:, :, 0, m + 1:m + 1 + n], t0[:, :, 0, :], t1[:, :, 1, :], ALU.subtract))
                    link(TT(R[:, :, 1, m + 1:m + 1 + n], t0[:, :, 1, :], t1[:, :, 0, :], ALU.add))
                gp.sem_inc(sm("r_ready"), 1)
                gp.wait_ge(sm("ptab_loaded"), q * 512 + 512)
                gp.wait_ge(*past("s_done", q * 2))
                for d_ in range(2):
                    t0, t1 = (TG[:, i_, :].rearrange("p (ri f) -> p ri f", ri=2) for i_ in range(2))
                    link(TT(t0, BT[:, d_, :, :], PT[:, d_, 0:1, :].broadcast_to([128, 2, GQ * SN]), ALU.mult))
                    link(TT(t1, BT[:, d_, :, :], PT[:, d_, 1:2, :].broadcast_to([128, 2, GQ * SN]), ALU.mult))
                    link(TT(E[:, d_, 0, :], t0[:, 0, :], t1[:, 1, :], ALU.subtract))
                    link(TT(E[:, d_, 1, :], t0[:, 1, :], t1[:, 0, :], ALU.add))
                gp.sem_inc(sm("e_ready"), 1)

            gp.wait_ge(*past("yst_stored", NQ * 128))
            gp.wait_ge(*past("hs_ready", NQ))
            with gp.Fori(0, 8) as k:
                apart(*past("y_ready", k))
                gp.dma_start(y_in[:, :], y_scr.rearrange("(k p) t c -> k p (t c)", p=128)[ds(k, 1), :, :].rearrange("o p f -> (o p) f")) \
                    .then_inc(sm("yu_loaded"), 16)
                gp.dma_start(u_in[:, :, :], u_scr.rearrange("(k p) t c -> k p t c", p=128)[ds(k, 1), :, :, CC:CC + CX]
                             .rearrange("o p t c -> (o p) t c")).then_inc(sm("yu_loaded"), 16)

            z_rows = z_scr.rearrange("(k p) t -> k p t", p=128)
            up_rows = up_scr.rearrange("(g m p) t -> g p m t", m=2, p=128)
            gp.wait_ge(*past("zst_stored0", 16 * 24))
            gp.wait_ge(*past("zst_stored1", 16 * 24))

            def load_z(i):
                gp.wait_ge(sm("bf_ready"), i)
                gp.dma_start(z_in[:, :], z_rows[ds(i + 8, 1), :, :].rearrange("o p t -> (o p) t")).then_inc(sm("zb_loaded"), 16)

            load_z(0)
            for g, w in enumerate(WINDOWS):
                if g > 0:
                    gp.wait_ge(sm("bp_stored"), 32 * g)
                gp.sem_inc(sm("bp_free"), 1)
                gp.dma_start(up_in[:, :, :], up_rows[g]).then_inc(sm("up_loaded"), 16)
                gp.dma_start(inv_in[:, :], inv_count[g:g + 1, :].to_broadcast([128, T])).then_inc(sm("up_loaded"), 16)
                gp.wait_ge(sm("up_loaded"), 32 * (g + 1))
                for m in range(2):
                    half = w // 2
                    rows = GR + w
                    cur, oth = PA, PB
                    gp.memset(cur[:, 0:half * GW], 0.0)
                    gp.memset(cur[:, (half + GR) * GW:rows * GW], 0.0)
                    link(gp.tensor_copy(cur[:, half * GW:(half + GR) * GW], up_in[:, m, :]))
                    d_, n = 1, rows
                    cols = GW + w
                    while d_ < w:
                        n -= d_
                        lastlevel = 2 * d_ == w
                        if lastlevel:
                            pad = oth[:, 0:GR * cols].rearrange("p (r c) -> p r c", c=cols)
                            gp.memset(pad[:, :, 0:half], 0.0)
                            gp.memset(pad[:, :, half + GW:], 0.0)
                            c3 = cur[:, :].rearrange("p (r c) -> p r c", c=GW)
                            link(TT(pad[:, :, half:half + GW], c3[:, 0:GR, :], c3[:, d_:d_ + GR, :], ALU.add))
                        else:
                            link(TT(oth[:, 0:n * GW], cur[:, 0:n * GW], cur[:, d_ * GW:(d_ + n) * GW], ALU.add))
                        cur, oth = oth, cur
                        d_ *= 2
                    d_, n = 1, cols
                    cv = cur[:, 0:GR * cols].rearrange("p (r c) -> p r c", c=cols)
                    while d_ < w:
                        n = GW if 2 * d_ == w else n - d_
                        ov = oth[:, 0:GR * n].rearrange("p (r c) -> p r c", c=n)
                        link(TT(ov, cv[:, :, 0:n], cv[:, :, d_:d_ + n], ALU.add))
                        cur, oth = oth, cur
                        cv = ov
                        d_ *= 2
                    link(TT(cur[:, 0:T], cur[:, 0:T], inv_in[:, :], ALU.mult))
                    link(TT(up_in[:, m, :], cur[:, 0:T], up_in[:, m, :], ALU.subtract))
                    gp.sem_inc(sm("diff_ready"), 1)
                gp.dma_start(pw_in[:, :, :], pool_w[0, g].rearrange("(k p) n -> p k n", p=128)).then_inc(sm("pw_loaded"), 16)
                load_z(2 * g + 1)
                for mo in range(2):
                    if mo == 1:
                        gp.wait_ge(*past("pool_evicted", 2 * g + 1))
                    gp.dma_start(zp_in[:, :], z_rows[2 * g + mo]).then_inc(sm("zp_loaded"), 16)
                if g < 3:
                    load_z(2 * g + 2)
                for mo in range(2):
                    gp.wait_ge(*past("pool_evicted", 2 * g + mo + 1))
                    gp.dma_start(pb_scr[256 * g + 128 * mo:256 * g + 128 * (mo + 1), :], bp[:, mo, :]).then_inc(sm("bp_stored"), 16)

            gp.wait_ge(sm("bp_stored"), 128)
            gp.wait_ge(sm("br_ready"), 8)
            gp.dma_start(adab_bc[:, :], ada_b[0:1, 2 * D:3 * D].to_broadcast([128, D])).then_inc(sm("adab_loaded"), 16)
            gp.wait_ge(sm("w_used"), T_OUT)
            for k in range(8):
                if k >= 2:
                    gp.wait_ge(sm("pbr_ready"), k - 1)
                gp.dma_start(pb_in[k % 2][:, :], pb_scr[128 * k:128 * (k + 1), :]).then_inc(sm(f"pb_loaded{k % 2}"), 16)
            gp.wait_ge(sm("gate_bc_ready"), 1)
            gp.dma_start(fg_bc[:, :], final_g.unsqueeze(0).to_broadcast([128, D])).then_inc(sm("fg_loaded"), 16)
            gp.wait_ge(sm("pbr_ready"), 8)
            x_v = x[0].rearrange("(a p) n -> p a n", p=128)
            yo_v = yo_scr.rearrange("(a p) n -> p a n", p=128)
            with gp.Fori(0, 4) as i:
                apart(*past("y_added", i * 8))
                gp.dma_start(xb[:, :, :], x_v[:, :, ds(i * NB, NB)]).then_inc(sm("xb_loaded"), 16)
                apart(*past("y_added", i * 8 + 8))
                gp.dma_start(yo_v[:, :, ds(i * NB, NB)], yb[:, :, :]).then_inc(sm("yb_stored"), 16)
            gp.wait_ge(sm("yb_stored"), 64)
            gp.wait_ge(sm("w_used"), T_END)
            for tok in range(8):
                gp.dma_start(yfin[tok // 4][:, tok % 4, :], yo_v[:, tok, 0:3 * NB]).then_inc(sm(f"yfin_loaded{tok}"), 16)


_INS = ["x", "c", "ctx", "c_ctx", "ada_w", "ada_b", "norm_g", "in_w", "pool_w", "pool_scale", "s5_lam_re", "s5_lam_im",
        "s5_log_dt", "s5_b_re", "s5_b_im", "s5_c_re", "s5_c_im", "s5_d", "glu_w", "glu_b", "out_w", "final_g"]
_OUTS = [((1, T, D), "float32")]


def _inv_counts():
    def counts(n, w):
        t = np.arange(n)
        return np.clip(t + w - w // 2, 0, n) - np.clip(t - w // 2, 0, n)
    return np.stack([(1.0 / np.outer(counts(GR, w), counts(GW, w))).reshape(T) for w in WINDOWS]).astype(np.float32)


def kernel(**inputs):
    import numpy as _np
    import concourse.bacc as _bacc
    from concourse import mybir as _mybir
    from concourse.bass_utils import run_bass_kernel_spmd as _run

    nc = _bacc.Bacc("TRN2", target_bir_lowering=False, num_devices=1)
    arrays, args = {}, []
    for name in _INS:
        a = _np.ascontiguousarray(inputs[name])
        arrays[f"in_{name}_dram"] = a
        args.append(nc.dram_tensor(f"in_{name}_dram", a.shape, _mybir.dt.from_np(a.dtype), kind="ExternalInput").ap())
    a = _inv_counts()
    arrays["inv_count_dram"] = a
    args.append(nc.dram_tensor("inv_count_dram", a.shape, _mybir.dt.from_np(a.dtype), kind="ExternalInput").ap())
    for i, (shape, dtype) in enumerate(_OUTS):
        dt = _mybir.dt.from_np(_np.dtype(dtype))
        args.append(nc.dram_tensor(f"out_{i}_dram", shape, dt, kind="ExternalOutput").ap())
    hybrid_block(nc, *args)
    r = _run(nc, [arrays], core_ids=[0])
    return r.results[0]["out_0_dram"]
```

```python
import math
from contextlib import ExitStack

import numpy as np

import concourse.bass as bass
from concourse import mybir

D = 2048
T = 1024
TC = 256
GW = 64
GR = T // GW
PW = D // 2
SW = D // 2
WINDOWS = (2, 4, 8, 16)
PGW = PW // len(WINDOWS)
SG, SH, SN = 64, 16, 64
KT = D // 128
L = 8
CX, CC = T // L, TC // L
SEQC = CX + CC
XC = SEQC + CC
GQ = 4
NQ = SG // GQ
EPS = 1e-6
NB = 512
LANES = 2 * L - 1
JP = L + 2

V_C, V_CC, V_ADAB, V_NG, V_D, V_GLUB, V_PS = 0, 16, 32, 80, 96, 104, 120


def hybrid_block(nc, x, c, ctx_in, c_ctx, ada_w, ada_b, norm_g, in_w, pool_w, pool_scale,
                 lam_re, lam_im, log_dt, b_re, b_im, c_re, c_im, d_skip, glu_w, glu_b, out_w, final_g,
                 inv_count, out, debug=None):
    f32, f32r, i32, bf16 = mybir.dt.float32, mybir.dt.float32r, mybir.dt.int32, mybir.dt.bfloat16
    ALU = mybir.AluOpType
    ACT = mybir.ActivationFunctionType
    ds = bass.ds
    es = ExitStack()
    with es:
        def sem(name):
            return es.enter_context(nc.semaphore(name))

        def scratch(name, shape):
            kind = "ExternalOutput" if debug else "Internal"
            return nc.dram_tensor(name, shape, f32, kind=kind).ap()

        u_scr = scratch("u_scr", [SW, L, XC])
        y_scr = scratch("y_scr", [SW, L, CX])
        z_scr = scratch("z_scr", [D, T])
        up_scr = scratch("up_scr", [PW, T])
        pb_scr = scratch("pb_scr", [PW, T])
        yo_scr = scratch("yo_scr", [T, D])
        p_scr = scratch("p_scr", [NQ, 2, L, 2, GQ, SN])
        b_scr = scratch("b_scr", [NQ, 2, SH, 2, GQ, SN])
        ctab = scratch("ctab", [128, SG, 3, SH])
        qtab = scratch("qtab", [128, SG, 2, JP])
        btab = scratch("btab", [128, SG, 2, SH])

        BASE = 16512
        HI, LO, RAW = BASE, BASE + 65536, BASE + 131072
        WHI, WLO = RAW + 8192, RAW + 16384
        SMALL = RAW + 24576
        WK = SMALL + 2144

        def at(name, shape, offset, dt=f32):
            return nc.alloc_sbuf_tensor_at(name, shape, dt, offset=offset)

        act_hi = at("act_hi", [128, KT, T], HI, f32r)
        act_lo = at("act_lo", [128, KT, T], LO, f32r)
        w_raw = [at(f"w_raw{s}", [128, 1024], RAW + 4096 * s) for s in range(2)]
        w_hi = [at(f"w_hi{s}", [128, 1024], WHI + 4096 * s, f32r) for s in range(2)]
        w_lo = [at(f"w_lo{s}", [128, 1024], WLO + 4096 * s, f32r) for s in range(2)]

        o = [SMALL]

        def small(name, shape, dt=f32):
            t = at(name, shape, o[0], dt)
            o[0] += (4 * int(np.prod(shape[1:])) + 31) // 32 * 32
            assert o[0] <= WK
            return t

        ident = small("ident", [128, 128])
        vT = small("vT", [128, 128])
        cs = small("cs", [128, KT, 2])
        wT = small("wT", [128, 3, SG])
        ssq = small("ssq", [128, 2, 4])
        b2col = small("b2col", [128, 8])
        rs = small("rs", [128, 4])
        ysq = small("ysq", [128, 8, 4])

        modT = at("modT", [128, 2, KT, 2], WK + 51712)
        gmul = at("gmul", [128, KT, 2], WK + 51968)
        ada_buf = [at(f"ada_buf{s}", [128, D], HI + 8192 * s) for s in range(4)]
        x_tile = [at(f"x_tile{s}", [128, D], HI + 32768 + 8192 * s) for s in range(2)]
        xT = at("xT", [128, KT, T], LO)
        cT = at("cT", [128, KT, TC], WK)
        c_lo = at("c_lo", [128, KT, TC], WK, f32r)
        c_hi = at("c_hi", [128, KT, TC], WK + 16384, f32r)
        ust = at("ust", [128, 2, L, XC], WK + 32768)
        vecs = at("vecs", [128, 128], WK + 32768)
        ada_row = at("ada_row", [128, 2, NB], WK + 32768 + 512)
        sq_junk = at("sq_junk", [128, NB], WK + 32768 + 4608 + 5120 + 8192, bf16)
        SA, SB = HI + 49152, RAW
        pp = {}
        names = ["lre", "lim", "zr", "zi", "n", "t", "r", "p", "e", "y", "sh", "s1", "cm", "inv", "t2", "t3",
                 "kr", "ki", "y8", "wr", "wi", "r8"]
        for i, n_ in enumerate(names):
            pp[n_] = at(f"p_{n_}", [128, SN], SA + 256 * i)
        e_bits = at("e_bits", [128, SN], SA + 256 * len(names), i32)
        dt_col = at("dt_col", [128, 8], SA + 256 * (len(names) + 1))
        dt_bits = at("dt_bits", [128, 1], SA + 256 * (len(names) + 1) + 64, i32)
        pw_ = at("pw", [128, L + 1, 2, SN], SA + 256 * (len(names) + 2))
        ptmp = at("ptmp", [128, 2, 4, 2, SN], SA + 256 * (len(names) + 2) + 4608)
        assert 256 * (len(names) + 2) + 4608 + 4096 <= 16384
        b_nat = at("b_nat", [128, 2, SN, SH], SB)
        b_bar = at("b_bar", [128, SH, 2, SN], SB + 8192)
        b_tmp = at("b_tmp", [128, 2, SH, SN], SB + 16384)
        c_nat = at("c_nat", [128, 8, 3, 2, SN], SB)
        c_st = at("c_st", [128, SG, 3, SH], SB + 12288)
        q_st = at("q_st", [128, SG, 2, JP], WK + 32768 + 4608)
        b_st = at("b_st", [128, SG, 2, SH], WK + 32768 + 4608 + 5120)
        assert WK + 32768 + 4608 + 5120 + 8192 <= 229368

        WORK_BYTES = 50944
        assert WK + WORK_BYTES + 4096 <= 229376
        z_st = [at(f"z_st{s}", [128, NB], WK + WORK_BYTES + 2048 * s) for s in range(2)]

        w_ = [WK]

        def work(name, shape):
            t = at(name, shape, w_[0])
            w_[0] += 4 * int(np.prod(shape[1:]))
            assert w_[0] <= WK + WORK_BYTES
            return t

        X = work("X", [128, GQ, XC])
        PT = work("PT", [128, 2, 2, GQ * SN])
        BT = work("BT", [128, 2, 2, GQ * SN])
        H = work("H", [128, GQ, 2, CX])
        M = work("M", [128, GQ, L * SH])
        CQ = work("CQ", [128, GQ, 3, SH])
        QQ = work("QQ", [128, GQ, 2, JP])
        BZ = work("BZ", [128, 2, GQ, 2, SH])
        E = work("E", [128, 2, 2, GQ * SN])
        TG = work("TG", [128, 2, 256])
        F = work("F", [128, GQ, 2, JP, SH])
        yst = at("yst", [128, GQ, CX], w_[0])
        strip = work("strip", [SH, GQ, LANES, SH])
        R = work("R", [128, GQ, 2, SEQC])
        TV = work("TV", [128, 2, GQ * JP * SH])
        G = work("G", [128, GQ, 2, SEQC])

        y_in = at("y_in", [128, T], WK)
        u_in = at("u_in", [128, L, CX], WK + 4096)
        sg = at("sg", [128, T], WK)
        br = at("br", [128, T], WK + 4096)
        z_in = at("z_in", [128, T], WK + 8192)
        bf = at("bf", [128, T], WK + 12288)
        up_in = at("up_in", [128, 2, T], WK + 16384)
        inv_in = at("inv_in", [128, T], WK + 24576)
        PA = at("PA", [128, 2048], WK + 28672)
        PB = at("PB", [128, 2048], WK + 36864)
        bp = at("bp", [128, 2, T], WK + 28672)
        zp_in = at("zp_in", [128, T], WK + 36864)
        pw_in = at("pw_in", [128, 2, PGW], WK + 40960)
        ones = at("ones", [128, 128], WK + 49152)
        gate_row = at("gate_row", [128, NB], WK + 51200)

        yb = at("yb", [128, 8, NB], WK)
        adab_bc = at("adab_bc", [128, D], WK)
        xb = at("xb", [128, 8, NB], WK + 16384)
        pb_in = [at(f"pb_in{s}", [128, T], WK + 16384 + 4096 * s) for s in range(2)]
        gate_bc = at("gate_bc", [128, D], WK + 32768)
        fg_bc = at("fg_bc", [128, D], WK + 40960)
        yfin = [at(f"yfin{s}", [128, 4, 3 * NB], (HI, LO)[s] + 32768) for s in range(2)]
        sq_junk2 = at("sq_junk2", [128, NB], WK + 49152)

        S = {}

        def sm(name):
            if name not in S:
                S[name] = es.enter_context(nc.semaphore(name))
            return S[name]

        START = {"bank_free0": 1, "bank_free1": 1, "strip_evicted": 1, "s_read": 1, "y_evicted": 1, "pool_evicted": 1,
                 "zst_stored0": 16, "zst_stored1": 16, "y_done": 1, "yst_stored": 16, "hs_ready": 1,
                 "s_done": 1, "y_ready": 1, "y_added": 1}

        def past(name, n):
            return sm(name), n + START[name]

        ps = es.enter_context(nc.psum_tensor("ps", [128, 8, NB], f32))
        block = es.enter_context(nc.Block())

        PROJ = 12
        T_SSM, T_Z, T_POOL, T_GLU, T_OUT, T_END = 0, 16, 48, 64, 80, 112
        G_SSM, G_Z, G_POOL, G_GLU = 0, 4, 12, 16
        OUT_ORDER = (4, 5, 6, 0, 1, 2, 3, 7)

        vec_src = [(c, V_C, 16), (c_ctx, V_CC, 16), (ada_b, V_ADAB, 48), (norm_g, V_NG, 16), (d_skip, V_D, 8),
                   (glu_b, V_GLUB, 16), (pool_scale, V_PS, 8)]

        in_tiles = in_w.rearrange("o (a b p) n -> p (o a) b n", p=128, b=4)
        glu_tiles = glu_w.rearrange("o (b p) n -> p (o b) n", p=128)
        out_tiles = out_w.rearrange("o (a b p) n -> p (o a) b n", p=128, b=2)
        ada_rows = ada_w.rearrange("o (k p) n -> p (o k) n", p=128)

        @block.sync
        def _(sp):
            for v, row, n in vec_src:
                flat = v.rearrange("o (r q) -> (o r) q", q=128) if len(v.shape) == 2 else v.rearrange("(r q) -> r q", q=128)
                sp.dma_start(vecs[row:row + n, :], flat).then_inc(sm("vecs_loaded"), 16)

            def apart(semaphore, value):
                sp.wait_ge(semaphore, value)
                sp.sem_inc(sm("sp_passed"), 1)

            def ada_load(k, piece, s):
                sp.dma_start(ada_buf[s][:, :].unsqueeze(1), ada_rows[:, ds(k, 1), piece * D:(piece + 1) * D]) \
                    .then_inc(sm(f"ada_loaded{s}"), 16)

            for s in range(4):
                ada_load(s // 2, s % 2, s)
            with sp.Fori(1, 8) as i:
                for s in range(4):
                    apart(sm("ada_used"), i * 4 + (s - 3))
                    ada_load(i * 2 + s // 2, s % 2, s)

            def raw_free(t):
                apart(sm("w_lo_ready"), t - 1)

            def in_tile(col, a, s):
                sp.dma_start(w_raw[s][:, :].rearrange("p (b n) -> p b n", b=4),
                             in_tiles[:, a, :, ds(col, 256)]).then_inc(sm(f"w_loaded{s}"), 16)

            for j in range(4):
                if j < 2:
                    sp.wait_ge(sm("params_stored"), 16 * 3)
                else:
                    raw_free(T_SSM + j)
                in_tile(PW, j, j % 2)
            with sp.Fori(1, 4) as i:
                for j in range(4):
                    raw_free(i * 4 + (T_SSM + j))
                    in_tile(i * 256 + PW, j, j % 2)
            def proj_tile(i, j):
                raw_free(i * PROJ + (T_Z + j))
                i_, part = i + j // PROJ, j % PROJ // 4
                in_tile(*(((i_ * 512 + (D + 256 * part)),) if part < 2 else (i_ * 256,)), j % 4, j % 2)

            p_q = p_scr.rearrange("q d t ri g n -> q d t (ri g n)")
            b_q = b_scr.rearrange("q d h ri g n -> q d h (ri g n)")
            u_q = u_scr.rearrange("(q g h) t c -> q t h g c", g=GQ, h=SH)

            def load_u(q):
                for t_ in range(L):
                    sp.dma_start(X[SH * t_:SH * (t_ + 1), :, :], u_q[ds(q, 1), t_, :, :, :].rearrange("o h g c -> (o h) g c")) \
                        .then_inc(sm("xq_loaded"), 16)

            def load_powers(q):
                for d_ in range(2):
                    sp.dma_start(PT[:, d_, :, :].rearrange("p a b -> p (a b)"),
                                 p_q[ds(q, 1), d_, :, :].rearrange("o t f -> (o t) f").unsqueeze(1).broadcast_to([L, SH, 2 * GQ * SN])) \
                        .then_inc(sm("ptab_loaded"), 16)
                    sp.dma_start(BT[:, d_, :, :].rearrange("p a b -> p (a b)"),
                                 b_q[ds(q, 1), d_, :, :].broadcast_to([L, SH, 2 * GQ * SN])) \
                        .then_inc(sm("ptab_loaded"), 16)

            def load_c(q):
                sp.dma_start(CQ[:, :, :, :], ctab[:, ds(q * GQ, GQ), :, :]).then_inc(sm("cq_loaded"), 16)
                sp.dma_start(QQ[:, :, :, :], qtab[:, ds(q * GQ, GQ), :, :]).then_inc(sm("cq_loaded"), 16)

            def load_b(q):
                for d_ in range(2):
                    rows = slice(64 * d_, 64 * d_ + 64)
                    sp.dma_start(BZ[rows, d_, :, :, :], btab[rows, ds(q * GQ, GQ), :, :]).then_inc(sm("bz_loaded"), 16)

            for j in range(3):
                proj_tile(0, j)
            sp.wait_ge(sm("w_used"), T_Z)
            sp.wait_ge(sm("u_stored"), 16 * 4)
            sp.wait_ge(sm("p_stored"), 16 * 24)
            load_powers(0)
            load_c(0)
            sp.wait_ge(sm("bz_zeroed"), 1)
            load_b(0)

            def proj_block(i, last):
                for j in range(PROJ):
                    a, r = divmod(j, 3)
                    if not last or j < 9:
                        proj_tile(i, j + 3)
                    elif j == 9:
                        glu_tile_pair(0)
                    q = i * 4 + a
                    more = not last or a < 3
                    if r == 0:
                        apart(*past("y_done", q))
                        load_u(q)
                        if more:
                            apart(sm("e_ready"), q + 1)
                            load_powers(q + 1)
                    if r == 1 and more:
                        apart(sm("f_ready"), q + 1)
                        load_c(q + 1)
                    if r == 2 and more:
                        apart(sm("strip_done"), q + 1)
                        load_b(q + 1)

            def glu_tile_pair(i):
                for half in range(2):
                    raw_free(i * 2 + (T_GLU + half))
                    sp.dma_start(w_raw[half][:, :].rearrange("p (b n) -> p b n", b=8),
                                 glu_tiles[:, :, ds(i * 128 + half * SW, 128)]).then_inc(sm(f"w_loaded{half}"), 16)

            with sp.Fori(0, 3) as i:
                proj_block(i, False)
            proj_block(3, True)
            sp.wait_ge(sm("w_used"), T_GLU)
            for s in range(4):
                ada_load(s, 2, s)
            with sp.Fori(1, 4) as i:
                for s in range(4):
                    apart(sm("ada_used"), i * 4 + (32 - 3 + s))
                    ada_load(i * 4 + s, 2, s)
            with sp.Fori(1, 8) as i:
                glu_tile_pair(i)
            with sp.Fori(0, 4) as i:
                for j, a in enumerate(OUT_ORDER):
                    raw_free(i * 8 + (T_OUT + j))
                    sp.dma_start(w_raw[j % 2][:, :].rearrange("p (b n) -> p b n", b=2),
                                 out_tiles[:, a, :, ds(i * NB, NB)]).then_inc(sm(f"w_loaded{j % 2}"), 16)

        @block.tensor
        def _(pe):
            pe.sem_inc(sm("y_done"), START["y_done"])
            pe.sem_inc(sm("s_done"), START["s_done"])

            def x_transposes(i, s):
                pe.wait_ge(sm("xn_ready"), i + 1)
                for kb in range(4):
                    b = kb % 2
                    n = 2 * i + kb // 2
                    if n > 0:
                        pe.wait_ge(sm(f"tr_evicted{b}"), n)
                    for r in range(4):
                        k = 4 * kb + r
                        mm = pe.transpose(ps[:, 2 + b, 128 * r:128 * (r + 1)], x_tile[s][:, 128 * k:128 * (k + 1)], ident[:, :])
                    mm.then_inc(sm(f"tr_done{b}"), 1)

            def ada_matmuls(n, k, piece, s, first, last):
                pe.wait_ge(sm(f"ada_loaded{s}"), 16 * (n // 4 + 1))
                for q in range(4):
                    mm = pe.matmul(ps[32 * q:32 * q + 2, piece, :], cs[:, k, :], ada_buf[s][:, NB * q:NB * (q + 1)],
                                   start=first, stop=last)
                mm.then_inc(sm("ada_used"), 1)

            pe.wait_ge(sm("ident_ready"), 2)
            pe.wait_ge(sm("vecs_loaded"), 16 * len(vec_src))
            pe.transpose(ps[:, 7, 0:128], vecs[:, :], ident[:, :]).then_inc(sm("vT_done"), 1)
            pe.wait_ge(sm("cs_ready"), 1)
            for n in range(32):
                ada_matmuls(n, n // 2, n % 2, n % 4, n < 2, n >= 30)
                if n % 2 == 1 and n // 2 < 10:
                    x_transposes(n // 2, (n // 2) % 2)
                if n == 21:
                    pe.wait_ge(sm("pw_ready"), 1)
                    blocks = [pw_[:, j, ri, :] for j in range(L + 1) for ri in range(2)]
                    blocks += [b_bar[:, h, ri, :] for h in range(SH) for ri in range(2)]
                    blocks += [pp[w][:, :] for w in ("wr", "wi", "r8")]
                    rounds = [blocks[0:8], blocks[8:16], blocks[16:18]] + [blocks[18 + 8 * r:26 + 8 * r] for r in range(4)] + [blocks[50:53]]
                    for r, blk in enumerate(rounds):
                        if r > 0:
                            pe.wait_ge(sm("pf_evicted"), r)
                            pe.wait_ge(sm("pbk_evicted"), r)
                        for i_, src in enumerate(blk):
                            for d_ in range(2):
                                lo_ = 64 * d_
                                mm = pe.matmul(ps[lo_:lo_ + 64, 4 + d_, 64 * i_:64 * i_ + 64], src[lo_:lo_ + 64, :],
                                               ident[lo_:lo_ + 64, lo_:lo_ + 64], start=True, stop=True)
                        mm.then_inc(sm("pt_done"), 1)
                if n == 27:
                    pe.wait_ge(sm("c_ready"), 1)
                    for oc in range(8):
                        if oc > 0:
                            pe.wait_ge(sm("ct_evicted"), oc)
                        for e in range(3):
                            mm = pe.transpose(ps[:, 6, 128 * e:128 * (e + 1)],
                                              c_nat[:, oc, e, :, :].rearrange("p d n -> p (d n)"), ident[:, :])
                        mm.then_inc(sm("ct_done"), 1)
            pe.wait_ge(sm("ada_row_ready"), 1)
            pe.wait_ge(sm("tr_evicted0"), 20)
            pe.wait_ge(sm("tr_evicted1"), 20)
            pe.wait_ge(sm("pf_evicted"), 8)
            pe.wait_ge(sm("pbk_evicted"), 8)
            for q in range(4):
                for h in range(2):
                    for r in range(4):
                        mm = pe.matmul(ps[:, 2 + q, (4 * h + r) * 2:(4 * h + r) * 2 + 2],
                                       ada_row[32 * q:32 * q + 2, h, 128 * r:128 * (r + 1)],
                                       ident[32 * q:32 * q + 2, 32 * q:32 * q + 2], start=True, stop=True)
            mm.then_inc(sm("mod_done"), 1)
            pe.wait_ge(sm("mod_evicted"), 1)

            def three(bank, cols, w, a, start, stop):
                (wh, wl), (ah, al) = w, a
                pe.matmul(ps[:, bank, 0:cols], wh, ah, start=start, stop=False)
                pe.matmul(ps[:, bank, 0:cols], wh, al, start=False, stop=False)
                return pe.matmul(ps[:, bank, 0:cols], wl, ah, start=False, stop=stop)

            def in_tile(t, s, j, g, ctx):
                pe.wait_ge(sm("w_lo_ready"), t + 1)
                for kk in range(4):
                    k = 4 * j + kk
                    if ctx:
                        pe.wait_ge(sm("h_ready"), k + 1)
                        if kk == 0:
                            pe.wait_ge(sm("hc_ready"), j + 1)
                    for m in range(2):
                        cut = slice(256 * kk + 128 * m, 256 * kk + 128 * (m + 1))
                        w = (w_hi[s][:, cut], w_lo[s][:, cut])
                        if k == 0:
                            pe.wait_ge(*past(f"bank_free{m}", g))
                        for n in range(2):
                            a = (act_hi[:, k, NB * n:NB * (n + 1)], act_lo[:, k, NB * n:NB * (n + 1)])
                            mm = three(2 * m + n, NB, w, a, k == 0, k == KT - 1)
                        if ctx:
                            mm = three(4 + m, TC, w, (c_hi[:, k, :], c_lo[:, k, :]), k == 0, k == KT - 1)
                        if k == KT - 1 and m == 0:
                            mm.then_inc(sm("m0_done"), 1)
                mm.then_inc(sm("w_used"), 1)

            with pe.Fori(0, 4) as i:
                for j in range(4):
                    in_tile(i * 4 + (T_SSM + j), j % 2, j, i + G_SSM, True)
            def ssm_states(q):
                pe.wait_ge(sm("xq_loaded"), q * 128 + 128)
                pe.wait_ge(sm("e_ready"), q + 1)
                pe.wait_ge(*past("strip_evicted", q))
                pe.wait_ge(*past("y_evicted", q))
                for g in range(GQ):
                    for ri in range(2):
                        for d_, rhs in ((0, X[:, g, 0:SEQC]), (1, X[:, g, XC - 1:CC - 1:-1])):
                            mm = pe.matmul(ps[64 * d_:64 * d_ + 64, 4 + g, ri * SEQC:(ri + 1) * SEQC],
                                           E[:, d_, ri, SN * g:SN * (g + 1)], rhs, start=True, stop=True)
                mm.then_inc(sm("s_done"), 1)

            def ssm_strips(q):
                pe.wait_ge(sm("f_ready"), q + 1)
                pe.wait_ge(sm("bz_loaded"), q * 32 + 32)
                pe.wait_ge(*past("s_read", q + 1))
                for g in range(GQ):
                    o_ = LANES * SH * (g % 2)
                    for d_, lo_, j0 in ((1, 0, 2), (0, (L - 1) * SH, 0)):
                        for ri in range(2):
                            mm = pe.matmul(ps[0:SH, 4 + g // 2, o_ + lo_:o_ + lo_ + L * SH], BZ[:, d_, g, ri, :],
                                           F[:, g, ri, j0:j0 + L, :].rearrange("p j h -> p (j h)"),
                                           start=(d_ == 1 and ri == 0), stop=(d_ == 0 and ri == 1), skip_group_check=True)
                mm.then_inc(sm("strip_done"), 1)

            def ssm_readout(q):
                pe.wait_ge(sm("m_loaded"), q * 128 + 128)
                pe.wait_ge(*past("hs_ready", q + 1))
                for g in range(GQ):
                    o_ = ps[:, 6, CX * g:CX * (g + 1)]
                    pe.matmul(o_, M[:, g, :], X[:, g, CC:CC + CX], start=True, stop=False)
                    pe.matmul(o_, F[:, g, 0, 1:L + 1, :].rearrange("p j h -> p (j h)"), H[:, g, 0, :], start=False, stop=False)
                    mm = pe.matmul(o_, F[:, g, 1, 1:L + 1, :].rearrange("p j h -> p (j h)"), H[:, g, 1, :], start=False, stop=True)
                mm.then_inc(sm("y_done"), 1)

            pe.wait_ge(*past("bank_free1", G_Z))
            with pe.Fori(0, 4) as i:
                for j in range(PROJ):
                    in_tile(i * PROJ + (T_Z + j), j % 2, j % 4, i * 3 + (G_Z + j // 4), False)
                    (ssm_states, ssm_strips, ssm_readout)[j % 3](i * 4 + j // 3)

            pe.wait_ge(*past("bank_free0", G_GLU))
            for n in range(16):
                pe.wait_ge(sm(f"ada_loaded{n % 4}"), 16 * (8 + n // 4 + 1))
                for q in range(4):
                    mm = pe.matmul(ps[32 * q:32 * q + 1, 0, :], cs[:, n, 0:1], ada_buf[n % 4][:, NB * q:NB * (q + 1)],
                                   start=n == 0, stop=n == 15)
                mm.then_inc(sm("ada_used"), 1)

            def pool_matmuls(g):
                pe.wait_ge(sm("diff_ready"), g * 2 + 2)
                pe.wait_ge(sm("pw_loaded"), g * 16 + 16)
                pe.wait_ge(*past("pool_evicted", g * 2))
                for mo in range(2):
                    for n in range(2):
                        for k in range(2):
                            mm = pe.matmul(ps[:, 4 + 2 * mo + n, :], pw_in[:, k, 128 * mo:128 * (mo + 1)],
                                           up_in[:, k, NB * n:NB * (n + 1)], start=k == 0, stop=k == 1)
                    mm.then_inc(sm("pool_done"), 1)

            pe.wait_ge(sm("gate_row_ready"), 1)
            pe.wait_ge(*past("y_evicted", NQ))
            with pe.Fori(0, 4) as i2:
                for sub in range(2):
                    for half in range(2):
                        pe.wait_ge(sm("w_lo_ready"), i2 * 4 + (T_GLU + 2 * sub + half + 1))
                        pe.wait_ge(*past(f"bank_free{half}", i2 * 2 + (G_GLU + sub)))
                        for k in range(8):
                            if half == 0:
                                pe.wait_ge(*past("y_ready", k + 1))
                            w = (w_hi[half][:, 128 * k:128 * (k + 1)], w_lo[half][:, 128 * k:128 * (k + 1)])
                            for n in range(2):
                                a = (act_hi[:, k, NB * n:NB * (n + 1)], act_lo[:, k, NB * n:NB * (n + 1)])
                                mm = three(2 * half + n, NB, w, a, k == 0, k == 7)
                        mm.then_inc(sm("w_used"), 1)
                pool_matmuls(i2)

            pe.wait_ge(*past("pool_evicted", 8))
            pe.wait_ge(sm("ones_ready"), 1)
            for q in range(4):
                mm = pe.matmul(ps[:, 4 + q, :], ones[32 * q:32 * q + 1, :], gate_row[32 * q:32 * q + 1, :], start=True, stop=True)
            mm.then_inc(sm("gate_done"), 1)
            pe.wait_ge(sm("gate_bc_ready"), 1)

            with pe.Fori(0, 4) as i:
                for j, a_ in enumerate(OUT_ORDER):
                    pe.wait_ge(sm("w_lo_ready"), i * 8 + (T_OUT + j + 1))
                    s = j % 2
                    for kk in range(2):
                        k = 2 * a_ + kk
                        if k >= 8:
                            pe.wait_ge(sm("br_ready"), k - 8 + 1)
                        else:
                            pe.wait_ge(sm("pbr_ready"), k + 1)
                        for tok in range(8):
                            first, last = (j == 0 and kk == 0), (j == 7 and kk == 1)
                            if first:
                                pe.wait_ge(sm("out_free"), i * 8 + tok + 1)
                            cols = slice(128 * tok, 128 * (tok + 1))
                            ah, al = act_hi[:, k, cols], act_lo[:, k, cols]
                            wh, wl = w_hi[s][:, NB * kk:NB * (kk + 1)], w_lo[s][:, NB * kk:NB * (kk + 1)]
                            pe.matmul(ps[:, tok, :], ah, wh, start=first, stop=False)
                            pe.matmul(ps[:, tok, :], ah, wl, start=False, stop=False)
                            mm = pe.matmul(ps[:, tok, :], al, wh, start=False, stop=last)
                            if last and tok < 7:
                                mm.then_inc(sm("tok_done"), 1)
                    mm.then_inc(sm("w_used"), 1)

        @block.scalar
        def _(act):
            act.sem_inc(sm("bank_free0"), START["bank_free0"])
            act.sem_inc(sm("bank_free1"), START["bank_free1"])
            act.sem_inc(sm("strip_evicted"), START["strip_evicted"])
            act.sem_inc(sm("y_evicted"), START["y_evicted"])
            act.sem_inc(sm("zst_stored0"), START["zst_stored0"])
            act.sem_inc(sm("zst_stored1"), START["zst_stored1"])
            act.sem_inc(sm("yst_stored"), START["yst_stored"])

            def split_hi(t, s, n_loaded):
                act.wait_ge(sm(f"w_loaded{s}"), n_loaded)
                if not isinstance(t, int) or t >= 2:
                    act.wait_ge(sm("w_used"), t - 1)
                act.activation(w_hi[s][:, :], w_raw[s][:, :], ACT.Copy).then_inc(sm("w_hi_ready"), 1)

            def tiles(base, per, i, js):
                for j in js:
                    t = (i * per + (base + j))
                    split_hi(t, (base + j) % 2, i * (16 * per // 2) + 16 * ((base + j) // 2 + 1))

            act.wait_ge(sm("vT_ready"), 1)
            act.activation(cs[:, :, :].rearrange("p k v -> p v k"), vT[:, V_C:V_C + 32].rearrange("p (v k) -> p v k", v=2),
                           ACT.Silu).then_inc(sm("cs_ready"), 1)

            def x_norm(i, s, n_sq, n_ld):
                act.wait_ge(sm(f"xt_loaded{s}"), n_ld)
                for h in range(4):
                    if not isinstance(n_sq, int) or n_sq > 0 or h > 0:
                        act.wait_ge(sm("sq_chain"), n_sq + h)
                    act.activation(sq_junk[:, :], x_tile[s][:, NB * h:NB * (h + 1)], ACT.Square,
                                   accum_out=ssq[:, s, h:h + 1]).then_inc(sm("sq_chain"), 1)

            def x_evict(i, dst, col):
                for kb in (0, 2):
                    act.wait_ge(sm("tr_done0"), 2 * i + kb // 2 + 1)
                    act.activation(dst[:, 4 * kb:4 * kb + 4, ds(col, 128)],
                                   ps[:, 2, :].rearrange("p (r n) -> p r n", r=4), ACT.Copy).then_inc(sm("tr_evicted0"), 1)

            for s in range(2):
                x_norm(s, s, 4 * s, 16)
            for s in range(2):
                x_evict(s, cT, 128 * s)
                x_norm(2 + s, s, 8 + 4 * s, 32)
            with act.Fori(0, 3) as i:
                for s in range(2):
                    x_evict(i * 2 + (2 + s), xT, i * 256 + 128 * s)
                    x_norm(i * 2 + (4 + s), s, i * 8 + (16 + 4 * s), i * 16 + 48)
            for s in range(2):
                x_evict(8 + s, xT, 768 + 128 * s)

            for n_, (dst, src, scale) in enumerate((("sh", "y", 0.5), ("s1", "y", 1.0), ("wi", "y8", 1.0), ("wr", "y8", 0.5))):
                act.wait_ge(sm("y_reduced"), 1 if src == "y" else 2)
                act.activation(pp[dst][:, :], pp[src][:, :], ACT.Sin, scale=scale).then_inc(sm("sin_done"), 1)
            nb = [8, 8, 2] + [8] * 4 + [3]
            for r in range(8):
                act.wait_ge(sm("pt_done"), r + 1)
                src = ps[0:64, 4, 0:64 * nb[r]]
                if r < 3:
                    dst = q_st[0:64, :, :, 4 * r:4 * r + nb[r] // 2].rearrange("p g ri j -> p j ri g")
                    src = src.rearrange("p (j ri g) -> p j ri g", ri=2, g=SG)
                    for ri in range(2):
                        e_ = act.activation(dst[:, :, ri, :], src[:, :, ri, :], ACT.Copy)
                elif r < 7:
                    dst = b_st[0:64, :, :, 4 * (r - 3):4 * (r - 3) + 4].rearrange("p g ri h -> p h ri g")
                    src = src.rearrange("p (h ri g) -> p h ri g", ri=2, g=SG)
                    for ri in range(2):
                        e_ = act.activation(dst[:, :, ri, :], src[:, :, ri, :], ACT.Copy)
                else:
                    e_ = act.activation(wT[0:64, :, :].rearrange("p w g -> p (w g)"), src, ACT.Copy)
                e_.then_inc(sm("pf_evicted"), 1)
            for oc in range(8):
                act.wait_ge(sm("ct_done"), oc + 1)
                act.activation(c_st[:, 8 * oc:8 * oc + 8, :, :].rearrange("p g e h -> p e g h"),
                               ps[:, 6, 0:384].rearrange("p (e g h) -> p e g h", e=3, g=8), ACT.Copy).then_inc(sm("ct_evicted"), 1)
            act.wait_ge(sm("pf_evicted"), 8)
            act.wait_ge(sm("pbk_evicted"), 8)
            act.wait_ge(sm("q_zeroed"), 1)
            act.wait_ge(sm("ct_evicted"), 8)
            act.dma_start(qtab, q_st[:, :, :, :]).then_inc(sm("params_stored"), 16)
            act.dma_start(btab, b_st[:, :, :, :]).then_inc(sm("params_stored"), 16)
            act.dma_start(ctab, c_st[:, :, :, :]).then_inc(sm("params_stored"), 16)

            act.wait_ge(sm("ada_used"), 32)
            for q in range(4):
                e_ = act.activation(ada_row[32 * q:32 * q + 2, :, :], ps[32 * q:32 * q + 2, 0:2, :], ACT.Copy)
            e_.then_inc(sm("ada_row_ready"), 1)

            def h_split(ks):
                with act.Fori(*ks) as k:
                    act.wait_ge(sm("h_scaled"), k + 1)
                    act.activation(act_hi[:, ds(k, 1), :], xT[:, ds(k, 1), :], ACT.Copy).then_inc(sm("h_hi_ready"), 1)

            def u_evict(i):
                act.wait_ge(sm("u_stored"), i * 16)
                for m in range(2):
                    if m == 0:
                        act.wait_ge(sm("m0_done"), i + (G_SSM + 1))
                    else:
                        act.wait_ge(sm("w_used"), i * 4 + (T_SSM + 4))
                    for n in range(2):
                        act.activation(ust[:, m, :, CC + 64 * n:CC + 64 * (n + 1)],
                                       ps[:, 2 * m + n, :].rearrange("p (c t) -> p t c", t=L), ACT.Copy)
                    for c0 in (0, SEQC):
                        e_ = act.activation(ust[:, m, :, c0:c0 + CC],
                                            ps[:, 4 + m, 0:TC].rearrange("p (c t) -> p t c", t=L), ACT.Copy)
                    e_.then_inc(sm(f"bank_free{m}"), 1)
                act.wait_ge(*past("bank_free1", i + 1))
                act.dma_start(u_scr.rearrange("(a m p) t c -> p a m (t c)", m=2, p=128)[:, ds(i, 1), :, :].rearrange("p o m f -> p (o m) f"),
                              ust[:, :, :, :].rearrange("p m t c -> p m (t c)")).then_inc(sm("u_stored"), 16)

            split_hi(0, 0, 16)
            split_hi(1, 1, 16)
            for j in range(4):
                act.wait_ge(sm("hc_scaled"), 4 * (j + 1))
                act.activation(c_hi[:, 4 * j:4 * j + 4, :], cT[:, 4 * j:4 * j + 4, :], ACT.Copy).then_inc(sm("hc_hi_ready"), 1)
            h_split((0, 8))
            split_hi(2, 0, 32)
            h_split((8, 12))
            split_hi(3, 1, 32)
            h_split((12, 16))
            split_hi(4, 0, 48)
            act.wait_ge(sm("tabs_free"), 1)
            u_evict(0)
            with act.Fori(1, 4) as i:
                tiles(T_SSM, 4, i, (1, 2, 3, 4))
                u_evict(i)

            def evict_store(i, sub):
                func = ACT.Silu if sub < 2 else ACT.Copy
                for m in range(2):
                    if m == 0:
                        act.wait_ge(sm("m0_done"), i * 3 + (G_Z + sub + 1))
                    else:
                        act.wait_ge(sm("w_used"), i * PROJ + (T_Z + 4 * sub + 4))
                    for n in range(2):
                        act.wait_ge(*past(f"zst_stored{n}", i * 96 + 16 * (2 * sub + m)))
                        act.activation(z_st[n][:, :], ps[:, 2 * m + n, :], func).then_inc(sm(f"zst_ready{n}"), 1)
                        act.wait_ge(sm(f"zst_ready{n}"), i * 6 + (2 * sub + m + 1))
                        if sub < 2:
                            dst = z_scr.rearrange("(a s m p) t -> p a s m t", s=2, m=2, p=128)[:, ds(i, 1), sub, m, NB * n:NB * (n + 1)]
                        else:
                            dst = up_scr.rearrange("(a m p) t -> p a m t", m=2, p=128)[:, ds(i, 1), m, NB * n:NB * (n + 1)]
                        act.dma_start(dst, z_st[n][:, :].unsqueeze(1)).then_inc(sm(f"zst_stored{n}"), 16)
                    act.wait_ge(sm("zst_ready1"), i * 6 + (2 * sub + m + 1))
                    act.sem_inc(sm(f"bank_free{m}"), 1)

            def taps(q):
                act.wait_ge(sm("strip_done"), q + 1)
                act.wait_ge(*past("yst_stored", q * 128))
                act.activation(strip[:, :, :, :].rearrange("p (b g) a c -> p b (g a c)", b=2),
                               ps[0:SH, 4:6, 0:2 * LANES * SH], ACT.Copy).then_inc(sm("strip_evicted"), 1)
                act.wait_ge(*past("strip_evicted", q + 1))
                for t_ in range(L):
                    act.dma_start(M[SH * t_:SH * (t_ + 1), :, :],
                                  strip[:, :, L - 1 - t_:2 * L - 1 - t_, :].rearrange("p g a b -> p g (a b)")).then_inc(sm("m_loaded"), 16)

            y_q = y_scr.rearrange("(q g h) t c -> q t h g c", g=GQ, h=SH)

            def readout(q):
                act.wait_ge(*past("y_done", q + 1))
                act.activation(yst[:, :, :].rearrange("p g c -> p (g c)"), ps[:, 6, :], ACT.Copy).then_inc(sm("y_evicted"), 1)
                act.wait_ge(*past("y_evicted", q + 1))
                for t_ in range(L):
                    act.dma_start(y_q[ds(q, 1), t_, :, :, :].rearrange("o h g c -> (o h) g c"), yst[SH * t_:SH * (t_ + 1), :, :]) \
                        .then_inc(sm("yst_stored"), 16)

            with act.Fori(0, 4) as i:
                for j in range(PROJ):
                    q = i * 4 + j // 3
                    if j % 3 == 2:
                        taps(q)
                    tiles(T_Z, PROJ, i, (j + 1,))
                    if j % 4 == 3:
                        evict_store(i, j // 4)
                    if j % 3 == 2:
                        readout(q)

            act.wait_ge(sm("ada_used"), 48)
            act.wait_ge(*past("zst_stored0", 16 * 24))
            act.wait_ge(*past("zst_stored1", 16 * 24))
            for q in range(4):
                e_ = act.activation(gate_row[32 * q:32 * q + 1, :], ps[32 * q:32 * q + 1, 0, :], ACT.Copy)
            e_.then_inc(sm("gate_row_ready"), 1)

            with act.Fori(0, 8) as k:
                act.wait_ge(sm("skip_ready"), k + 1)
                act.activation(y_in[:, :], y_in[:, :], ACT.Gelu_apprx_tanh).then_inc(sm("gelu_ready"), 1)
                act.wait_ge(sm("gelu_ready"), k + 1)
                act.activation(act_hi[:, ds(k, 1), :], y_in[:, :].unsqueeze(1), ACT.Copy).then_inc(sm("y_hi_ready"), 1)

            with act.Fori(0, 8) as i:
                tiles(T_GLU, 2, i, (1, 2))
                act.wait_ge(sm("w_used"), i * 2 + (T_GLU + 2))
                act.wait_ge(sm("sg_used"), i + 1)
                for n in range(2):
                    act.activation(sg[:, NB * n:NB * (n + 1)], ps[:, 2 + n, :], ACT.Sigmoid,
                                   bias=b2col[:, ds(i, 1)]).then_inc(sm("sg_ready"), 1)
                act.wait_ge(sm("sg_ready"), i * 2 + 2)
                act.sem_inc(sm("bank_free1"), 1)
                act.wait_ge(sm("bf_ready"), i + 1)
                act.activation(act_hi[:, ds(i + 8, 1), :], bf[:, :].unsqueeze(1), ACT.Copy).then_inc(sm("br_hi_ready"), 1)

            split_hi(T_OUT + 1, 1, 16 * (T_OUT // 2 + 1))
            for k in range(8):
                act.wait_ge(sm(f"pb_loaded{k % 2}"), 16 * (k // 2 + 1))
                act.activation(act_hi[:, k, :], pb_in[k % 2][:, :], ACT.Copy).then_inc(sm("pbr_hi_ready"), 1)

            def square_sums(i, n_):
                for tok in range(8):
                    act.wait_ge(*past("y_added", i * 8 + tok + 1))
                    if not isinstance(n_, int) or n_ + tok > 0:
                        act.wait_ge(sm("ysq_chain"), n_ + tok)
                    act.activation(sq_junk2[:, :], yb[:, tok, :], ACT.Square, accum_out=ysq[:, tok, ds(i, 1)]) \
                        .then_inc(sm("ysq_chain"), 1)

            tiles(T_OUT, 8, 0, range(2, 9))
            square_sums(0, 0)
            with act.Fori(1, 3) as i:
                tiles(T_OUT, 8, i, range(1, 9))
                square_sums(i, i * 8)
            tiles(T_OUT, 8, 3, range(1, 8))
            square_sums(3, 24)

            for tok in range(8):
                act.wait_ge(sm("out_ready"), tok + 1)
                act.dma_start(out[0, 128 * tok:128 * (tok + 1), 0:3 * NB], yfin[tok // 4][:, tok % 4, :]).then_inc(sm("stored"), 16)
                act.dma_start(out[0, 128 * tok:128 * (tok + 1), 3 * NB:], yb[:, tok, :]).then_inc(sm("stored"), 16)
            act.wait_ge(sm("stored"), 16 * 16)

        @block.vector
        def _(dve):
            dve.sem_inc(sm("s_read"), START["s_read"])
            dve.sem_inc(sm("pool_evicted"), START["pool_evicted"])
            dve.sem_inc(sm("hs_ready"), START["hs_ready"])
            dve.sem_inc(sm("y_ready"), START["y_ready"])
            dve.sem_inc(sm("y_added"), START["y_added"])

            chained = [0, 0]

            def link(ins):
                chained[0] += 1
                ins.then_inc(sm("dve_chain"), 1)
                dve.wait_ge(sm("dve_chain"), chained[1] + chained[0])

            class repeat:
                def __init__(self, lo, hi, per):
                    self.lo, self.hi, self.per, self.f = lo, hi, per, dve.Fori(lo, hi)

                def __enter__(self):
                    i = self.f.__enter__()
                    self.base = chained[0]
                    chained[1] = i * self.per
                    chained[0] -= self.per * self.lo
                    return i

                def __exit__(self, *a):
                    chained[0] += self.per * self.lo
                    assert chained[0] - self.base == self.per, chained[0] - self.base
                    chained[0], chained[1] = self.base + self.per * (self.hi - self.lo), 0
                    return self.f.__exit__(*a)

            TT, TS, STT = dve.tensor_tensor, dve.tensor_scalar, dve.scalar_tensor_tensor

            def rsqrt(r, v, tmp):
                link(TS(r.bitcast(i32), v.bitcast(i32), -0.5, 1597463007.0, ALU.mult, ALU.add))
                for _ in range(3):
                    link(STT(tmp, r, v, r, ALU.mult, ALU.mult))
                    link(TS(tmp, tmp, -0.5, 1.5, ALU.mult, ALU.add))
                    link(TT(r, r, tmp, ALU.mult))

            dve.wait_ge(sm("vT_done"), 1)
            dve.tensor_copy(vT[:, :], ps[:, 7, 0:128]).then_inc(sm("vT_ready"), 1)
            dve.wait_ge(sm("vT_ready"), 1)
            dve.tensor_copy(b2col[:, :], vT[:, V_GLUB + 8:V_GLUB + 16]).then_inc(sm("b2_ready"), 1)

            def x_scale(i, s):
                dve.wait_ge(sm("sq_chain"), i * 4 + 4)
                link(dve.tensor_reduce(rs[:, 0:1], ssq[:, s, :], mybir.AxisListType.X, ALU.add))
                link(TS(rs[:, 1:2], rs[:, 0:1], 1.0 / D, EPS, ALU.mult, ALU.add))
                rsqrt(rs[:, 2:3], rs[:, 1:2], rs[:, 3:4])
                TS(x_tile[s][:, :], x_tile[s][:, :], rs[:, 2:3], None, ALU.mult).then_inc(sm("xn_ready"), 1)

            def x_evict(i, dst, col):
                for kb in (1, 3):
                    dve.wait_ge(sm("tr_done1"), 2 * i + kb // 2 + 1)
                    dve.tensor_copy(dst[:, 4 * kb:4 * kb + 4, ds(col, 128)],
                                    ps[:, 3, :].rearrange("p (r n) -> p r n", r=4)).then_inc(sm("tr_evicted1"), 1)

            for s in range(2):
                x_scale(s, s)
                x_evict(s, cT, 128 * s)
            with repeat(1, 5, 2 * 12) as i:
                for s in range(2):
                    x_scale(i * 2 + s, s)
                    x_evict(i * 2 + s, xT, i * 256 + (128 * s - 256))

            P = {n_: t[:, :] for n_, t in pp.items()}

            def exp(dst, x_, n_, r_, p_, bits):
                MAGIC = 12582912.0
                link(TS(r_, x_, -88.0, 89.0, ALU.max, ALU.min))
                link(TS(n_, r_, 1.0 / math.log(2.0), MAGIC, ALU.mult, ALU.add))
                link(TS(n_, n_, MAGIC, None, ALU.subtract))
                link(STT(r_, n_, -0.693359375, r_, ALU.mult, ALU.add))
                link(STT(r_, n_, 2.12194440e-4, r_, ALU.mult, ALU.add))
                link(TS(p_, r_, 1.0 / 5040, None, ALU.mult))
                for k in (720, 120, 24, 6, 2, 1):
                    link(STT(p_, p_, 1.0 / k, r_, ALU.add, ALU.mult))
                link(TS(bits, n_, 127.0, 8388608.0, ALU.add, ALU.mult))
                link(STT(dst, p_, 1.0, bits.bitcast(f32), ALU.add, ALU.mult))

            def reduce_angle(dst, x_, n_):
                MAGIC = 12582912.0
                link(TS(n_, x_, 1.0 / (2 * math.pi), MAGIC, ALU.mult, ALU.add))
                link(TS(n_, n_, MAGIC, None, ALU.subtract))
                c1 = 6.28125
                c2 = float(np.float32(np.floor((2 * math.pi - c1) * 2 ** 21) / 2 ** 21))
                c3 = 2 * math.pi - c1 - c2
                link(STT(dst, n_, -c1, x_, ALU.mult, ALU.add))
                link(STT(dst, n_, -c2, dst, ALU.mult, ALU.add))
                link(STT(dst, n_, -c3, dst, ALU.mult, ALU.add))
                return TS(dst, dst, -math.pi, math.pi, ALU.max, ALU.min)

            dve.wait_ge(sm("lam_loaded"), 16 * 3)
            col = lambda i_: dt_col[:, i_:i_ + 1]
            exp(col(4), col(0), col(1), col(2), col(3), dt_bits[:, :])
            link(TS(P["zr"], P["lre"], col(4), None, ALU.mult))
            link(TS(P["zi"], P["lim"], col(4), None, ALU.mult))
            link(reduce_angle(P["y"], P["zi"], P["n"]))
            dve.sem_inc(sm("y_reduced"), 1)
            link(TS(P["t"], P["y"], 8.0, None, ALU.mult))
            link(reduce_angle(P["y8"], P["t"], P["n"]))
            dve.sem_inc(sm("y_reduced"), 1)
            exp(P["e"], P["zr"], P["n"], P["r"], P["p"], e_bits[:, :])
            link(TT(P["r8"], P["e"], P["e"], ALU.mult))
            link(TT(P["r8"], P["r8"], P["r8"], ALU.mult))
            link(TT(P["r8"], P["r8"], P["r8"], ALU.mult))
            dve.wait_ge(sm("sin_done"), 4)
            link(STT(P["cm"], P["sh"], -2.0, P["sh"], ALU.mult, ALU.mult))
            link(STT(P["t"], P["wr"], -2.0, P["wr"], ALU.mult, ALU.mult))
            link(TS(P["wr"], P["t"], 1.0, None, ALU.add))
            link(TS(P["wi"], P["wi"], -1.0, None, ALU.mult))
            a_r, a_i = pw_[:, 1, 0, :], pw_[:, 1, 1, :]
            link(TT(P["t"], P["e"], P["cm"], ALU.mult))
            link(STT(P["t2"], P["e"], -1.0, P["t"], ALU.add, ALU.add))
            link(TT(a_r, P["t"], P["e"], ALU.add))
            link(TT(a_i, P["e"], P["s1"], ALU.mult))
            link(TT(P["t"], P["lre"], P["lre"], ALU.mult))
            link(TT(P["t3"], P["lim"], P["lim"], ALU.mult))
            link(TT(P["t"], P["t"], P["t3"], ALU.add))
            link(dve.reciprocal(P["inv"], P["t"]))
            link(TT(P["kr"], P["t2"], P["lre"], ALU.mult))
            link(TT(P["t"], a_i, P["lim"], ALU.mult))
            link(TT(P["kr"], P["kr"], P["t"], ALU.add))
            link(TT(P["kr"], P["kr"], P["inv"], ALU.mult))
            link(TT(P["ki"], a_i, P["lre"], ALU.mult))
            link(TT(P["t"], P["t2"], P["lim"], ALU.mult))
            link(TT(P["ki"], P["ki"], P["t"], ALU.subtract))
            link(TT(P["ki"], P["ki"], P["inv"], ALU.mult))
            dve.memset(pw_[:, 0, 0, :], 1.0)
            dve.memset(pw_[:, 0, 1, :], 0.0)
            for m in (1, 2, 4):
                src = pw_[:, 1:m + 1, :, :]
                link(TT(ptmp[:, 0, 0:m, :, :], src, pw_[:, m:m + 1, 0:1, :].broadcast_to([128, m, 2, SN]), ALU.mult))
                link(TT(ptmp[:, 1, 0:m, :, :], src, pw_[:, m:m + 1, 1:2, :].broadcast_to([128, m, 2, SN]), ALU.mult))
                link(TT(pw_[:, m + 1:2 * m + 1, 0, :], ptmp[:, 0, 0:m, 0, :], ptmp[:, 1, 0:m, 1, :], ALU.subtract))
                link(TT(pw_[:, m + 1:2 * m + 1, 1, :], ptmp[:, 0, 0:m, 1, :], ptmp[:, 1, 0:m, 0, :], ALU.add))
            dve.wait_ge(sm("b_loaded"), 32)
            br_, bi_ = (b_nat[:, i_, :, :].rearrange("p n h -> p h n") for i_ in range(2))
            kr_, ki_ = (P[n_].unsqueeze(1).broadcast_to([128, SH, SN]) for n_ in ("kr", "ki"))
            for o_, (u0, v0), (u1, v1), op in ((0, (br_, kr_), (bi_, ki_), ALU.subtract), (1, (bi_, kr_), (br_, ki_), ALU.add)):
                link(TT(b_tmp[:, 0, :, :], u0, v0, ALU.mult))
                link(TT(b_tmp[:, 1, :, :], u1, v1, ALU.mult))
                link(TT(b_bar[:, :, o_, :], b_tmp[:, 0, :, :], b_tmp[:, 1, :, :], op))
            dve.sem_inc(sm("pw_ready"), 1)
            link(dve.memset(q_st[0:64, :, :, JP - 1], 0.0))
            link(dve.memset(q_st[64:128, :, :, 0], 0.0))
            dve.sem_inc(sm("q_zeroed"), 1)
            nb = [8, 8, 2] + [8] * 4 + [3]
            for r in range(8):
                dve.wait_ge(sm("pt_done"), r + 1)
                src = ps[64:128, 5, 0:64 * nb[r]]
                if r < 3:
                    src = src.rearrange("p (j ri g) -> p j ri g", ri=2, g=SG)
                    n_, top = nb[r] // 2, L + 1 - 4 * r
                    dst = q_st[64:128, :, :, top:(top - n_ if top - n_ >= 0 else None):-1].rearrange("p g ri j -> p j ri g")
                    for ri in range(2):
                        e_ = dve.tensor_copy(dst[:, :, ri, :], src[:, :, ri, :])
                elif r < 7:
                    dst = b_st[64:128, :, :, 4 * (r - 3):4 * (r - 3) + 4].rearrange("p g ri h -> p h ri g")
                    src = src.rearrange("p (h ri g) -> p h ri g", ri=2, g=SG)
                    for ri in range(2):
                        e_ = dve.tensor_copy(dst[:, :, ri, :], src[:, :, ri, :])
                else:
                    e_ = dve.tensor_copy(wT[64:128, :, :].rearrange("p w g -> p (w g)"), src)
                e_.then_inc(sm("pbk_evicted"), 1)
            dve.wait_ge(sm("c_loaded"), 64)
            link(TS(c_nat[:, :, 1, :, :], c_nat[:, :, 1, :, :], -1.0, None, ALU.mult))
            link(TS(c_nat[:, :, 2, :, :], c_nat[:, :, 0, :, :], -1.0, None, ALU.mult))
            dve.sem_inc(sm("c_ready"), 1)

            dve.wait_ge(sm("mod_done"), 1)
            for q in range(4):
                e_ = TT(modT[:, :, 4 * q:4 * q + 4, :], ps[:, 2 + q, 0:16].rearrange("p (h r v) -> p h r v", h=2, r=4),
                        vT[:, V_ADAB:V_ADAB + 32].rearrange("p (h k) -> p h k", h=2)[:, :, 4 * q:4 * q + 4].unsqueeze(3)
                        .broadcast_to([128, 2, 4, 2]), ALU.add)
            link(e_)
            dve.sem_inc(sm("mod_evicted"), 1)
            link(STT(gmul[:, :, :], modT[:, 1, :, :], 1.0, vT[:, V_NG:V_NG + 16].unsqueeze(2).broadcast_to([128, KT, 2]),
                     ALU.add, ALU.mult))

            def split_lo(t, s):
                dve.wait_ge(sm("w_hi_ready"), t + 1)
                TT(w_lo[s][:, :], w_raw[s][:, :], w_hi[s][:, :].bitcast(f32), ALU.subtract).then_inc(sm("w_lo_ready"), 1)

            def tiles(base, per, i, js):
                for j in js:
                    split_lo(i * per + (base + j), (base + j) % 2)

            def h_split(lo_, hi_):
                with dve.Fori(lo_, hi_) as k:
                    TS(xT[:, ds(k, 1), :], xT[:, ds(k, 1), :], gmul[:, ds(k, 1), 0], modT[:, 0, ds(k, 1), 0],
                       ALU.mult, ALU.add).then_inc(sm("h_scaled"), 1)
                    dve.wait_ge(sm("h_hi_ready"), k + 1)
                    TT(act_lo[:, ds(k, 1), :], xT[:, ds(k, 1), :], act_hi[:, ds(k, 1), :].bitcast(f32), ALU.subtract) \
                        .then_inc(sm("h_ready"), 1)

            split_lo(0, 0)
            split_lo(1, 1)
            for k in range(KT):
                TS(cT[:, k, :], cT[:, k, :], gmul[:, k, 1:2], modT[:, 0, k, 1:2], ALU.mult, ALU.add).then_inc(sm("hc_scaled"), 1)
            for j in range(4):
                dve.wait_ge(sm("hc_hi_ready"), j + 1)
                TT(c_lo[:, 4 * j:4 * j + 4, :], cT[:, 4 * j:4 * j + 4, :], c_hi[:, 4 * j:4 * j + 4, :].bitcast(f32), ALU.subtract) \
                    .then_inc(sm("hc_ready"), 1)
            h_split(0, 8)
            split_lo(2, 0)
            h_split(8, 12)
            split_lo(3, 1)
            h_split(12, 16)
            split_lo(4, 0)
            dve.wait_ge(sm("params_stored"), 48)
            dve.sem_inc(sm("tabs_free"), 1)
            with dve.Fori(1, 4) as i:
                tiles(T_SSM, 4, i, (1, 2, 3, 4))

            dve.wait_ge(sm("w_used"), T_Z)
            dve.wait_ge(sm("u_stored"), 16 * 4)
            link(dve.memset(BZ[0:64, 1, :, :, :], 0.0))
            link(dve.memset(BZ[64:128, 0, :, :, :], 0.0))
            dve.sem_inc(sm("bz_zeroed"), 1)

            def c_powers(q):
                dve.wait_ge(sm("cq_loaded"), q * 32 + 32)
                dve.wait_ge(*past("y_done", q))
                t0, t1 = (TV[:, i_, :].rearrange("p (g j h) -> p g j h", g=GQ, j=JP) for i_ in range(2))

                def cb(e):
                    return CQ[:, :, e:e + 1, :].broadcast_to([128, GQ, JP, SH])

                def qb(ri):
                    return QQ[:, :, ri, :].unsqueeze(3).broadcast_to([128, GQ, JP, SH])
                for ri, e0, e1 in ((0, 0, 1), (1, 1, 2)):
                    link(TT(t0, cb(e0), qb(0), ALU.mult))
                    link(TT(t1, cb(e1), qb(1), ALU.mult))
                    link(TT(F[:, :, ri, :, :], t0, t1, ALU.add))
                dve.sem_inc(sm("f_ready"), 1)

            def recurrence(q):
                dve.wait_ge(sm("r_ready"), q + 1)
                dve.wait_ge(*past("s_done", q + 1))
                for r in range(2):
                    src = ps[:, 4 + 2 * r:6 + 2 * r, 0:2 * SEQC].rearrange("p g (ri c) -> p g ri c", ri=2)
                    t0, t1 = (TV[:, i_, 0:4 * SEQC].rearrange("p (g ri c) -> p g ri c", g=2, ri=2) for i_ in range(2))
                    rr, ri_ = (R[:, 2 * r:2 * r + 2, i_:i_ + 1, :].broadcast_to([128, 2, 2, SEQC]) for i_ in range(2))
                    link(TT(t0, src, rr, ALU.mult))
                    link(TT(t1, src, ri_, ALU.mult))
                    link(TT(G[:, 2 * r:2 * r + 2, 0, :], t0[:, :, 0, :], t1[:, :, 1, :], ALU.subtract))
                    link(TT(G[:, 2 * r:2 * r + 2, 1, :], t0[:, :, 1, :], t1[:, :, 0, :], ALU.add))
                dve.sem_inc(sm("s_read"), 1)
                for g in range(GQ):
                    for ri in range(2):
                        e_ = dve.tensor_tensor_scan(G[:, g, ri, :], wT[:, 2, ds(q * GQ + g, 1)].broadcast_to([128, SEQC]),
                                                    G[:, g, ri, :], 0.0, ALU.mult, ALU.add)
                link(e_)

            def states(q):
                for r in range(2):
                    gs = slice(2 * r, 2 * r + 2)
                    src = G[:, gs, :, CC - 1:SEQC - 1]
                    t0, t1 = (TV[:, i_, 0:4 * CX].rearrange("p (g ri c) -> p g ri c", g=2, ri=2) for i_ in range(2))
                    rr, ri_ = (R[:, gs, i_:i_ + 1, CC - 1:SEQC - 1].broadcast_to([128, 2, 2, CX]) for i_ in range(2))
                    link(TT(t0, src, rr, ALU.mult))
                    link(TT(t1, src, ri_, ALU.mult))
                    for rows, way in ((slice(0, 64), slice(None)), (slice(64, 128), slice(None, None, -1))):
                        TT(H[rows, gs, 0, :], t0[rows, :, 0, way], t1[rows, :, 1, way], ALU.add)
                        e_ = TT(H[rows, gs, 1, :], t0[rows, :, 1, way], t1[rows, :, 0, way], ALU.subtract)
                    link(e_)
                dve.sem_inc(sm("hs_ready"), 1)

            with repeat(0, 4, 4 * (6 + 9 + 6)) as i:
                for j in range(PROJ):
                    tiles(T_Z, PROJ, i, (j + 1,))
                    (c_powers, recurrence, states)[j % 3](i * 4 + j // 3)

            with dve.Fori(0, 8) as k:
                dve.wait_ge(sm("yu_loaded"), k * 32 + 32)
                STT(y_in[:, :], u_in[:, :, :].rearrange("p t c -> p (t c)"), vT[:, ds(k + V_D, 1)], y_in[:, :], ALU.mult, ALU.add) \
                    .then_inc(sm("skip_ready"), 1)
                dve.wait_ge(sm("y_hi_ready"), k + 1)
                TT(act_lo[:, ds(k, 1), :], y_in[:, :].unsqueeze(1), act_hi[:, ds(k, 1), :].bitcast(f32), ALU.subtract) \
                    .then_inc(sm("y_ready"), 1)

            dve.wait_ge(*past("y_ready", 8))
            dve.sem_inc(sm("sg_used"), 1)

            def glu_group(i):
                tiles(T_GLU, 2, i, (1,))
                dve.wait_ge(sm("w_used"), i * 2 + (T_GLU + 1))
                for n in range(2):
                    e_ = TS(br[:, NB * n:NB * (n + 1)], ps[:, n, :], vT[:, ds(i + V_GLUB, 1)], None, ALU.add)
                e_.then_inc(sm("bank_free0"), 1)
                tiles(T_GLU, 2, i, (2,))
                dve.wait_ge(sm("sg_ready"), i * 2 + 2)
                dve.wait_ge(*past("bank_free0", i + (G_GLU + 1)))
                TT(br[:, :], br[:, :], sg[:, :], ALU.mult).then_inc(sm("sg_used"), 1)
                dve.wait_ge(sm("sg_used"), i + 2)
                dve.wait_ge(sm("zb_loaded"), i * 16 + 16)
                TT(bf[:, :].rearrange("p (c t) -> p t c", t=L), br[:, :].rearrange("p (t c) -> p t c", t=L),
                   z_in[:, :].rearrange("p (c t) -> p t c", t=L), ALU.mult).then_inc(sm("bf_ready"), 1)
                dve.wait_ge(sm("br_hi_ready"), i + 1)
                TT(act_lo[:, ds(i + 8, 1), :], bf[:, :].unsqueeze(1), act_hi[:, ds(i + 8, 1), :].bitcast(f32), ALU.subtract) \
                    .then_inc(sm("br_ready"), 1)

            with dve.Fori(0, 4) as g:
                for sub in range(2):
                    glu_group(g * 2 + sub)
                for mo in range(2):
                    dve.wait_ge(sm("pool_done"), g * 2 + mo + 1)
                    dve.wait_ge(sm("zp_loaded"), g * 32 + 16 * (mo + 1))
                    dve.wait_ge(sm("bp_free"), g + 1)
                    for n in range(2):
                        e_ = STT(bp[:, mo, NB * n:NB * (n + 1)], ps[:, 4 + 2 * mo + n, :], vT[:, ds(g * 2 + (V_PS + mo), 1)],
                                 zp_in[:, NB * n:NB * (n + 1)], ALU.mult, ALU.mult)
                    e_.then_inc(sm("pool_evicted"), 1)

            tiles(T_OUT, 8, 0, (1,))
            dve.wait_ge(sm("gate_done"), 1)
            dve.wait_ge(sm("adab_loaded"), 16)
            for q in range(4):
                e_ = TT(gate_bc[:, NB * q:NB * (q + 1)], ps[:, 4 + q, :], adab_bc[:, NB * q:NB * (q + 1)], ALU.add)
            e_.then_inc(sm("gate_bc_ready"), 1)
            dve.wait_ge(sm("gate_bc_ready"), 1)
            dve.sem_inc(sm("out_free"), 8)
            for k in range(8):
                dve.wait_ge(sm("pbr_hi_ready"), k + 1)
                TT(act_lo[:, k, :], pb_in[k % 2][:, :], act_hi[:, k, :].bitcast(f32), ALU.subtract).then_inc(sm("pbr_ready"), 1)

            def out_evict(i):
                dve.wait_ge(sm("yb_stored"), i * 16)
                if not isinstance(i, int) or i > 0:
                    dve.wait_ge(sm("ysq_chain"), i * 8)
                for tok in range(8):
                    if tok < 7:
                        dve.wait_ge(sm("tok_done"), i * 7 + tok + 1)
                    else:
                        dve.wait_ge(sm("w_used"), i * 8 + (T_OUT + 8))
                    TT(yb[:, tok, :], ps[:, tok, :], gate_bc[:, ds(i * NB, NB)], ALU.mult).then_inc(sm("out_free"), 1)
                dve.wait_ge(sm("xb_loaded"), i * 16 + 16)
                dve.wait_ge(sm("out_free"), i * 8 + 16)
                for tok in range(8):
                    TT(yb[:, tok, :], yb[:, tok, :], xb[:, tok, :], ALU.add).then_inc(sm("y_added"), 1)

            tiles(T_OUT, 8, 0, range(2, 9))
            out_evict(0)
            with dve.Fori(1, 3) as i:
                tiles(T_OUT, 8, i, range(1, 9))
                out_evict(i)
            tiles(T_OUT, 8, 3, range(1, 8))
            out_evict(3)

            dve.wait_ge(sm("fg_loaded"), 16)
            for tok in range(8):
                dve.wait_ge(sm("ysq_chain"), 24 + tok + 1)
                link(dve.tensor_reduce(rs[:, 0:1], ysq[:, tok, :], mybir.AxisListType.X, ALU.add))
                link(TS(rs[:, 1:2], rs[:, 0:1], 1.0 / D, EPS, ALU.mult, ALU.add))
                rsqrt(rs[:, 2:3], rs[:, 1:2], rs[:, 3:4])
                dve.wait_ge(sm(f"yfin_loaded{tok}"), 16)
                STT(yfin[tok // 4][:, tok % 4, :], yfin[tok // 4][:, tok % 4, :], rs[:, 2:3], fg_bc[:, 0:3 * NB], ALU.mult, ALU.mult)
                link(STT(yb[:, tok, :], yb[:, tok, :], rs[:, 2:3], fg_bc[:, 3 * NB:], ALU.mult, ALU.mult))
                dve.sem_inc(sm("out_ready"), 1)

        @block.gpsimd
        def _(gp):
            TT = gp.tensor_tensor
            chained = [0, 0]

            def link(ins):
                chained[0] += 1
                ins.then_inc(sm("gp_chain"), 1)
                gp.wait_ge(sm("gp_chain"), chained[1] + chained[0])

            class repeat:
                def __init__(self, lo, hi, per):
                    self.lo, self.hi, self.per, self.f = lo, hi, per, gp.Fori(lo, hi)

                def __enter__(self):
                    i = self.f.__enter__()
                    self.base = chained[0]
                    chained[1] = i * self.per
                    return i

                def __exit__(self, *a):
                    assert self.lo == 0 and chained[0] - self.base == self.per, chained[0] - self.base
                    chained[0], chained[1] = self.base + self.per * self.hi, 0
                    return self.f.__exit__(*a)

            gp.memset(ident[:, :], 0.0).then_inc(sm("ident_ready"), 1)
            gp.wait_ge(sm("ident_ready"), 1)
            gp.affine_select(out=ident[:, :], in_=ident[:, :], compare_op=ALU.not_equal, fill=1.0, base=0,
                             pattern=[[-1, 128]], channel_multiplier=1).then_inc(sm("ident_ready"), 1)

            def apart(semaphore, value):
                gp.wait_ge(semaphore, value)
                gp.sem_inc(sm("gp_passed"), 1)

            for s in range(2):
                gp.dma_start(x_tile[s][:, :], ctx_in[0, 128 * s:128 * (s + 1), :]).then_inc(sm(f"xt_loaded{s}"), 16)
            with gp.Fori(0, 4) as i:
                for s in range(2):
                    gp.wait_ge(sm("tr_done0"), i * 4 + 2 * s + 2)
                    apart(sm("tr_done1"), i * 4 + 2 * s + 2)
                    gp.dma_start(x_tile[s][:, :], x[0, ds(i * 256 + 128 * s, 128), :]).then_inc(sm(f"xt_loaded{s}"), 16)

            gp.dma_start(pp["lre"][:, :], lam_re.rearrange("o d g n -> (o d g) n")).then_inc(sm("lam_loaded"), 16)
            gp.dma_start(pp["lim"][:, :], lam_im.rearrange("o d g n -> (o d g) n")).then_inc(sm("lam_loaded"), 16)
            gp.dma_start(dt_col[:, 0:1], log_dt.rearrange("o d (g u) -> (o d g) u", u=1)).then_inc(sm("lam_loaded"), 16)
            for ri, b_ in enumerate((b_re, b_im)):
                gp.dma_start(b_nat[:, ri, :, :], b_.rearrange("o d g n h -> (o d g) n h")).then_inc(sm("b_loaded"), 16)
            gp.wait_ge(sm("pw_ready"), 1)
            for d_ in range(2):
                for g in range(GQ):
                    rows = slice(64 * d_ + g, 64 * d_ + 64, GQ)
                    src = pw_[rows, 0:L, :, :] if d_ == 1 else pw_[rows, L - 1::-1, :, :]
                    for ri in range(2):
                        gp.dma_start(p_scr[:, d_, :, ri, g, :], src[:, :, ri, :]).then_inc(sm("p_stored"), 16)
                    gp.dma_start(b_scr[:, d_, :, :, g, :].rearrange("q h ri n -> q (h ri) n"),
                                 b_bar[rows, :, :, :].rearrange("p h ri n -> p (h ri) n")).then_inc(sm("p_stored"), 16)
            gp.wait_ge(sm("p_stored"), 16 * 24)
            gp.wait_ge(sm("pt_done"), 8)
            for ri, c_ in enumerate((c_re, c_im)):
                for d_ in range(2):
                    gp.dma_start(c_nat[:, :, ri, d_, :], c_[0, d_].rearrange("(oc g) h n -> (g h) oc n", g=8)).then_inc(sm("c_loaded"), 16)

            gp.wait_ge(sm("w_used"), T_Z)
            gp.wait_ge(sm("u_stored"), 16 * 4)
            gp.wait_ge(sm("bz_zeroed"), 1)
            link(gp.memset(R[:, :, 0, 0], 1.0))
            link(gp.memset(R[:, :, 1, 0], 0.0))
            spans = [(0, 1, 1), (0, 2, 2), (0, 4, 4), (0, 8, 8), (0, 16, 16), (0, 32, 32), (0, 64, 32), (32, 64, 32),
                     (0, 128, SEQC - 1 - 128)]
            with repeat(0, NQ, 16 + 1 + 4 * len(spans)) as q:
                gp.wait_ge(sm("ptab_loaded"), q * 64 + 64)
                gp.wait_ge(*past("s_done", q))
                for d_ in range(2):
                    for half in range(2):
                        cols = slice(2 * SN * half, 2 * SN * (half + 1))
                        t0, t1 = (TG[:, i_, :].rearrange("p (ri f) -> p ri f", ri=2) for i_ in range(2))
                        link(TT(t0, BT[:, d_, :, cols], PT[:, d_, 0:1, cols].broadcast_to([128, 2, 2 * SN]), ALU.mult))
                        link(TT(t1, BT[:, d_, :, cols], PT[:, d_, 1:2, cols].broadcast_to([128, 2, 2 * SN]), ALU.mult))
                        link(TT(E[:, d_, 0, cols], t0[:, 0, :], t1[:, 1, :], ALU.subtract))
                        link(TT(E[:, d_, 1, cols], t0[:, 1, :], t1[:, 0, :], ALU.add))
                gp.sem_inc(sm("e_ready"), 1)
                gp.wait_ge(*past("hs_ready", q))
                link(gp.tensor_copy(R[:, :, :, 1], wT[:, 0:2, ds(q * GQ, GQ)].rearrange("p w g -> p g w")))
                for s0, m, n in spans:
                    src = R[:, :, :, s0 + 1:s0 + n + 1]
                    t0, t1 = (TG[:, i_, 0:GQ * 2 * n].rearrange("p (g ri n) -> p g ri n", g=GQ, ri=2) for i_ in range(2))
                    link(TT(t0, src, R[:, :, 0:1, m:m + 1].broadcast_to([128, GQ, 2, n]), ALU.mult))
                    link(TT(t1, src, R[:, :, 1:2, m:m + 1].broadcast_to([128, GQ, 2, n]), ALU.mult))
                    o_ = slice(m + s0 + 1, m + s0 + 1 + n)
                    link(TT(R[:, :, 0, o_], t0[:, :, 0, :], t1[:, :, 1, :], ALU.subtract))
                    link(TT(R[:, :, 1, o_], t0[:, :, 1, :], t1[:, :, 0, :], ALU.add))
                gp.sem_inc(sm("r_ready"), 1)

            gp.wait_ge(*past("yst_stored", NQ * 128))
            gp.wait_ge(*past("hs_ready", NQ))
            with gp.Fori(0, 8) as k:
                apart(*past("y_ready", k))
                gp.dma_start(y_in[:, :], y_scr.rearrange("(k p) t c -> k p (t c)", p=128)[ds(k, 1), :, :].rearrange("o p f -> (o p) f")) \
                    .then_inc(sm("yu_loaded"), 16)
                gp.dma_start(u_in[:, :, :], u_scr.rearrange("(k p) t c -> k p t c", p=128)[ds(k, 1), :, :, CC:CC + CX]
                             .rearrange("o p t c -> (o p) t c")).then_inc(sm("yu_loaded"), 16)

            gp.memset(ones[:, :], 1.0).then_inc(sm("ones_ready"), 1)
            z_rows = z_scr.rearrange("(k p) t -> k p t", p=128)
            up_rows = up_scr.rearrange("(g m p) t -> g p m t", m=2, p=128)
            gp.wait_ge(*past("zst_stored0", 16 * 24))
            gp.wait_ge(*past("zst_stored1", 16 * 24))

            def load_z(i):
                gp.wait_ge(sm("bf_ready"), i)
                gp.dma_start(z_in[:, :], z_rows[ds(i + 8, 1), :, :].rearrange("o p t -> (o p) t")).then_inc(sm("zb_loaded"), 16)

            load_z(0)
            for g, w in enumerate(WINDOWS):
                if g > 0:
                    gp.wait_ge(sm("bp_stored"), 32 * g)
                gp.sem_inc(sm("bp_free"), 1)
                gp.dma_start(up_in[:, :, :], up_rows[g]).then_inc(sm("up_loaded"), 16)
                gp.dma_start(inv_in[:, :], inv_count[g:g + 1, :].to_broadcast([128, T])).then_inc(sm("up_loaded"), 16)
                gp.wait_ge(sm("up_loaded"), 32 * (g + 1))
                for m in range(2):
                    half = w // 2
                    rows = GR + w
                    cur, oth = PA, PB
                    gp.memset(cur[:, 0:half * GW], 0.0)
                    gp.memset(cur[:, (half + GR) * GW:rows * GW], 0.0)
                    link(gp.tensor_copy(cur[:, half * GW:(half + GR) * GW], up_in[:, m, :]))
                    d_, n = 1, rows
                    cols = GW + w
                    while d_ < w:
                        n -= d_
                        lastlevel = 2 * d_ == w
                        if lastlevel:
                            pad = oth[:, 0:GR * cols].rearrange("p (r c) -> p r c", c=cols)
                            gp.memset(pad[:, :, 0:half], 0.0)
                            gp.memset(pad[:, :, half + GW:], 0.0)
                            c3 = cur[:, :].rearrange("p (r c) -> p r c", c=GW)
                            link(TT(pad[:, :, half:half + GW], c3[:, 0:GR, :], c3[:, d_:d_ + GR, :], ALU.add))
                        else:
                            link(TT(oth[:, 0:n * GW], cur[:, 0:n * GW], cur[:, d_ * GW:(d_ + n) * GW], ALU.add))
                        cur, oth = oth, cur
                        d_ *= 2
                    d_, n = 1, cols
                    cv = cur[:, 0:GR * cols].rearrange("p (r c) -> p r c", c=cols)
                    while d_ < w:
                        n = GW if 2 * d_ == w else n - d_
                        ov = oth[:, 0:GR * n].rearrange("p (r c) -> p r c", c=n)
                        link(TT(ov, cv[:, :, 0:n], cv[:, :, d_:d_ + n], ALU.add))
                        cur, oth = oth, cur
                        cv = ov
                        d_ *= 2
                    link(TT(cur[:, 0:T], cur[:, 0:T], inv_in[:, :], ALU.mult))
                    link(TT(up_in[:, m, :], cur[:, 0:T], up_in[:, m, :], ALU.subtract))
                    gp.sem_inc(sm("diff_ready"), 1)
                gp.dma_start(pw_in[:, :, :], pool_w[0, g].rearrange("(k p) n -> p k n", p=128)).then_inc(sm("pw_loaded"), 16)
                load_z(2 * g + 1)
                for mo in range(2):
                    if mo == 1:
                        gp.wait_ge(*past("pool_evicted", 2 * g + 1))
                    gp.dma_start(zp_in[:, :], z_rows[2 * g + mo]).then_inc(sm("zp_loaded"), 16)
                if g < 3:
                    load_z(2 * g + 2)
                for mo in range(2):
                    gp.wait_ge(*past("pool_evicted", 2 * g + mo + 1))
                    gp.dma_start(pb_scr[256 * g + 128 * mo:256 * g + 128 * (mo + 1), :], bp[:, mo, :]).then_inc(sm("bp_stored"), 16)

            gp.wait_ge(sm("bp_stored"), 128)
            gp.wait_ge(sm("br_ready"), 8)
            gp.dma_start(adab_bc[:, :], ada_b[0:1, 2 * D:3 * D].to_broadcast([128, D])).then_inc(sm("adab_loaded"), 16)
            gp.wait_ge(sm("w_used"), T_OUT)
            for k in range(8):
                if k >= 2:
                    gp.wait_ge(sm("pbr_ready"), k - 1)
                gp.dma_start(pb_in[k % 2][:, :], pb_scr[128 * k:128 * (k + 1), :]).then_inc(sm(f"pb_loaded{k % 2}"), 16)
            gp.wait_ge(sm("gate_bc_ready"), 1)
            gp.dma_start(fg_bc[:, :], final_g.unsqueeze(0).to_broadcast([128, D])).then_inc(sm("fg_loaded"), 16)
            gp.wait_ge(sm("pbr_ready"), 8)
            x_v = x[0].rearrange("(a p) n -> p a n", p=128)
            yo_v = yo_scr.rearrange("(a p) n -> p a n", p=128)
            with gp.Fori(0, 4) as i:
                apart(*past("y_added", i * 8))
                gp.dma_start(xb[:, :, :], x_v[:, :, ds(i * NB, NB)]).then_inc(sm("xb_loaded"), 16)
                apart(*past("y_added", i * 8 + 8))
                gp.dma_start(yo_v[:, :, ds(i * NB, NB)], yb[:, :, :]).then_inc(sm("yb_stored"), 16)
            gp.wait_ge(sm("yb_stored"), 64)
            gp.wait_ge(sm("w_used"), T_END)
            for tok in range(8):
                gp.dma_start(yfin[tok // 4][:, tok % 4, :], yo_v[:, tok, 0:3 * NB]).then_inc(sm(f"yfin_loaded{tok}"), 16)


_INS = ["x", "c", "ctx", "c_ctx", "ada_w", "ada_b", "norm_g", "in_w", "pool_w", "pool_scale", "s5_lam_re", "s5_lam_im",
        "s5_log_dt", "s5_b_re", "s5_b_im", "s5_c_re", "s5_c_im", "s5_d", "glu_w", "glu_b", "out_w", "final_g"]
_OUTS = [((1, T, D), "float32")]


def _inv_counts():
    def counts(n, w):
        t = np.arange(n)
        return np.clip(t + w - w // 2, 0, n) - np.clip(t - w // 2, 0, n)
    return np.stack([(1.0 / np.outer(counts(GR, w), counts(GW, w))).reshape(T) for w in WINDOWS]).astype(np.float32)


def kernel(**inputs):
    import numpy as _np
    import concourse.bacc as _bacc
    from concourse import mybir as _mybir
    from concourse.bass_utils import run_bass_kernel_spmd as _run

    nc = _bacc.Bacc("TRN2", target_bir_lowering=False, num_devices=1)
    arrays, args = {}, []
    for name in _INS:
        a = _np.ascontiguousarray(inputs[name])
        arrays[f"in_{name}_dram"] = a
        args.append(nc.dram_tensor(f"in_{name}_dram", a.shape, _mybir.dt.from_np(a.dtype), kind="ExternalInput").ap())
    a = _inv_counts()
    arrays["inv_count_dram"] = a
    args.append(nc.dram_tensor("inv_count_dram", a.shape, _mybir.dt.from_np(a.dtype), kind="ExternalInput").ap())
    for i, (shape, dtype) in enumerate(_OUTS):
        dt = _mybir.dt.from_np(_np.dtype(dtype))
        args.append(nc.dram_tensor(f"out_{i}_dram", shape, dt, kind="ExternalOutput").ap())
    hybrid_block(nc, *args)
    r = _run(nc, [arrays], core_ids=[0])
    return r.results[0]["out_0_dram"]
```

```python
import math
from contextlib import ExitStack

import numpy as np

import concourse.bass as bass
from concourse import mybir

D = 2048
T = 1024
TC = 256
GW = 64
GR = T // GW
PW = D // 2
SW = D // 2
WINDOWS = (2, 4, 8, 16)
PGW = PW // len(WINDOWS)
SG, SH, SN = 64, 16, 64
KT = D // 128
L = 8
CX, CC = T // L, TC // L
SEQC = CX + CC
XC = SEQC + CC
GQ = 4
NQ = SG // GQ
EPS = 1e-6
NB = 512
LANES = 2 * L - 1
JP = L + 2

V_C, V_CC, V_ADAB, V_NG, V_GLUB, V_PS, V_END = 0, 16, 32, 80, 96, 112, 120


def hybrid_block(nc, x, c, ctx_in, c_ctx, ada_w, ada_b, norm_g, in_w, pool_w, pool_scale,
                 lam_re, lam_im, log_dt, b_re, b_im, c_re, c_im, d_skip, glu_w, glu_b, out_w, final_g,
                 inv_count, out, debug=None):
    f32, f32r, i32, bf16 = mybir.dt.float32, mybir.dt.float32r, mybir.dt.int32, mybir.dt.bfloat16
    ALU = mybir.AluOpType
    ACT = mybir.ActivationFunctionType
    ds = bass.ds
    es = ExitStack()
    with es:
        def sem(name):
            return es.enter_context(nc.semaphore(name))

        def scratch(name, shape):
            kind = "ExternalOutput" if debug else "Internal"
            return nc.dram_tensor(name, shape, f32, kind=kind).ap()

        u_scr = scratch("u_scr", [SW, L, XC])
        y_scr = scratch("y_scr", [SW, L, CX])
        z_scr = scratch("z_scr", [D, T])
        up_scr = scratch("up_scr", [PW, T])
        pb_scr = scratch("pb_scr", [PW, T])
        yo_scr = scratch("yo_scr", [T, D])
        p_scr = scratch("p_scr", [NQ, 2, L, 2, GQ, SN])
        b_scr = scratch("b_scr", [NQ, 2, SH, 2, GQ, SN])
        ctab = scratch("ctab", [128, SG, 3, SH])
        qtab = scratch("qtab", [128, SG, 2, JP])
        btab = scratch("btab", [128, SG, 2, SH])

        BASE = 16512
        HI, LO, RAW = BASE, BASE + 65536, BASE + 131072
        WHI, WLO = RAW + 8192, RAW + 16384
        SMALL = RAW + 24576
        WK = SMALL + 2528

        def at(name, shape, offset, dt=f32):
            return nc.alloc_sbuf_tensor_at(name, shape, dt, offset=offset)

        act_hi = at("act_hi", [128, KT, T], HI, f32r)
        act_lo = at("act_lo", [128, KT, T], LO, f32r)
        w_raw = [at(f"w_raw{s}", [128, 1024], RAW + 4096 * s) for s in range(2)]
        w_hi = [at(f"w_hi{s}", [128, 1024], WHI + 4096 * s, f32r) for s in range(2)]
        w_lo = [at(f"w_lo{s}", [128, 1024], WLO + 4096 * s, f32r) for s in range(2)]

        o = [SMALL]

        def small(name, shape, dt=f32):
            t = at(name, shape, o[0], dt)
            o[0] += (4 * int(np.prod(shape[1:])) + 31) // 32 * 32
            assert o[0] <= WK
            return t

        ident = small("ident", [128, 128])
        vT = small("vT", [128, V_END])
        cs = small("cs", [128, KT, 2])
        wT = small("wT", [128, 3, SG])
        ssq = small("ssq", [128, 2, 4])
        b2col = small("b2col", [128, 8])
        rs = small("rs", [128, 4])
        ysq = small("ysq", [128, 8, 4])
        dT = small("dT", [128, SG])
        rsq = small("rsq", [128, 4, 8])

        modT = at("modT", [128, 2, KT, 2], WK + 51712)
        gmul = at("gmul", [128, KT, 2], WK + 51968)
        ada_buf = [at(f"ada_buf{s}", [128, D], HI + 8192 * s) for s in range(4)]
        x_tile = [at(f"x_tile{s}", [128, D], HI + 32768 + 8192 * s) for s in range(2)]
        xT = at("xT", [128, KT, T], LO)
        cT = at("cT", [128, KT, TC], WK)
        c_lo = at("c_lo", [128, KT, TC], WK, f32r)
        c_hi = at("c_hi", [128, KT, TC], WK + 16384, f32r)
        ust = at("ust", [128, 2, L, XC], WK + 32768)
        vecs = at("vecs", [V_END, 128], WK + 32768)
        d_nat = at("d_nat", [SG, SH], WK + 32768 + 512)
        d_rep = at("d_rep", [SG, L, SH], WK + 32768 + 1024)
        ada_row = at("ada_row", [128, 2, NB], WK + 32768 + 512)
        sq_junk = at("sq_junk", [128, NB], WK + 32768 + 4608 + 5120 + 8192, bf16)
        SA, SB = HI + 49152, RAW
        pp = {}
        names = ["lre", "lim", "zr", "zi", "n", "t", "r", "p", "e", "y", "sh", "s1", "cm", "inv", "den", "t2", "t3",
                 "kr", "ki", "y8", "wr", "wi", "r8", "step"]
        for i, n_ in enumerate(names):
            pp[n_] = at(f"p_{n_}", [128, SN], SA + 256 * i)
        e_bits = at("e_bits", [128, SN], SA + 256 * len(names), i32)
        dt_col = at("dt_col", [128, 8], SA + 256 * (len(names) + 1))
        dt_bits = at("dt_bits", [128, 1], SA + 256 * (len(names) + 1) + 64, i32)
        pw_ = at("pw", [128, L + 1, 2, SN], SA + 256 * (len(names) + 2))
        ptmp = at("ptmp", [128, 2, 4, 2, SN], SA + 256 * (len(names) + 2) + 4608)
        assert 256 * (len(names) + 2) + 4608 + 4096 <= 16384
        b_nat = at("b_nat", [128, 2, SN, SH], SB)
        b_bar = at("b_bar", [128, SH, 2, SN], SB + 16384)
        b_tmp = at("b_tmp", [128, 2, SH, SN], SB + 8192)
        c_nat = at("c_nat", [128, 8, 3, 2, SN], WK + 16384)
        c_st = at("c_st", [128, SG, 3, SH], SB)
        q_st = at("q_st", [128, SG, 2, JP], WK + 32768 + 4608)
        b_st = at("b_st", [128, SG, 2, SH], WK + 32768 + 4608 + 5120)
        assert WK + 32768 + 4608 + 5120 + 8192 <= 229368

        WORK_BYTES = 46464
        assert WK + WORK_BYTES + 8192 <= 229376
        z_st = [at(f"z_st{s}", [128, NB], WK + WORK_BYTES + 2048 * s) for s in range(4)]

        w_ = [WK]

        def work(name, shape):
            t = at(name, shape, w_[0])
            w_[0] += 4 * int(np.prod(shape[1:]))
            assert w_[0] <= WK + WORK_BYTES
            return t

        X = work("X", [128, GQ, XC])
        PT = work("PT", [128, 2, GQ * SN])
        BT = work("BT", [128, 2, GQ * SN])
        E = work("E", [128, 2, 2, GQ * SN])
        BZ = work("BZ", [128, 2, GQ, 2, SH])
        M = work("M", [128, GQ, L * SH])
        CQ = work("CQ", [128, GQ, 3, SH])
        QQ = work("QQ", [128, GQ, 2, JP])
        H = work("H", [128, GQ, 2, CX])
        TG = work("TG", [128, 2, 256])
        F = work("F", [128, GQ, 2, JP, SH])
        yst = at("yst", [128, GQ, CX], w_[0])
        strip = work("strip", [SH, GQ, LANES, SH])
        R = work("R", [128, GQ, 2, SEQC])
        TV = work("TV", [128, 2, GQ * JP * SH])
        G = work("G", [128, GQ, 2, SEQC])

        y_in = [at(f"y_in{s}", [128, T], WK + (3072, 7168)[s]) for s in range(2)]
        gate_buf = [at(f"gate_buf{s}", [128, D], o_) for s, o_ in enumerate((HI + 40960, LO + 40960, HI + 49152, HI + 57344))]
        sg = at("sg", [128, T], WK + 12288)
        z_in = at("z_in", [128, T], WK + 4096)
        bf = at("bf", [128, T], WK)
        zp_in = [at(f"zp_in{s}", [128, T], WK + (8192, 45056)[s]) for s in range(2)]
        up_in = [at(f"up_in{s}", [128, 2, T], (WK + 16384, LO + 57344)[s]) for s in range(2)]
        inv_in = at("inv_in", [128, T], WK + 24576)
        PA = at("PA", [128, 2048], WK + 28672)
        PB = at("PB", [128, 2048], WK + 36864)
        pw_in = at("pw_in", [128, 2, PGW], WK + 49152)
        gate_row = at("gate_row", [128, NB], WK + 51200)
        ones = at("ones", [128, 128], WK + 53248)

        yb = at("yb", [128, 8, NB], WK)
        xb = at("xb", [128, 8, NB], WK + 16384)
        pb_in = [at(f"pb_in{s}", [128, T], WK + 16384 + 4096 * s) for s in range(4)]
        gate_bc = at("gate_bc", [128, D], WK + 32768)
        fg_bc = at("fg_bc", [128, D], WK + 40960)
        yfin = [at(f"yfin{s}", [128, 4, 3 * NB], (HI, LO)[s] + 32768) for s in range(2)]
        sq_junk2 = at("sq_junk2", [128, NB], WK + 49152)

        S = {}

        def sm(name):
            if name not in S:
                S[name] = es.enter_context(nc.semaphore(name))
            return S[name]

        START = {"bank_free0": 1, "bank_free1": 1, "strip_evicted": 1, "s_read": 1, "y_evicted": 1, "pool_evicted": 1,
                 "zst_stored0": 16, "zst_stored1": 16, "zst_stored2": 16, "zst_stored3": 16, "y_done": 1, "yst_stored": 16, "hs_ready": 1,
                 "s_done": 1, "y_ready": 1, "y_added": 1, "skipped": 1}

        def past(name, n):
            return sm(name), n + START[name]

        ps = es.enter_context(nc.psum_tensor("ps", [128, 8, NB], f32))
        block = es.enter_context(nc.Block())

        PROJ = 12
        T_SSM, T_Z, T_POOL, T_GLU, T_OUT, T_END = 0, 16, 48, 64, 80, 112
        G_SSM, G_Z, G_POOL, G_GLU = 0, 4, 12, 16
        OUT_ORDER = (4, 5, 6, 0, 1, 2, 3, 7)

        vec_src = [(c, V_C, 16), (c_ctx, V_CC, 16), (ada_b, V_ADAB, 48), (norm_g, V_NG, 16),
                   (glu_b, V_GLUB, 16), (pool_scale, V_PS, 8)]

        in_tiles = in_w.rearrange("o (a b p) n -> p (o a) b n", p=128, b=4)
        glu_tiles = glu_w.rearrange("o (b p) n -> p (o b) n", p=128)
        out_tiles = out_w.rearrange("o (a b p) n -> p (o a) b n", p=128, b=2)
        ada_rows = ada_w.rearrange("o (k p) n -> p (o k) n", p=128)

        @block.sync
        def _(sp):
            for v, row, n in vec_src:
                flat = v.rearrange("o (r q) -> (o r) q", q=128) if len(v.shape) == 2 else v.rearrange("(r q) -> r q", q=128)
                sp.dma_start(vecs[row:row + n, :], flat).then_inc(sm("vecs_loaded"), 16)

            sp.dma_start(d_nat[:, :], d_skip.rearrange("o (g h) -> (o g) h", h=SH)).then_inc(sm("d_loaded"), 16)

            def apart(semaphore, value):
                sp.wait_ge(semaphore, value)
                sp.sem_inc(sm("sp_passed"), 1)

            def ada_load(k, piece, s, buf=ada_buf):
                sp.dma_start(buf[s][:, :].unsqueeze(1), ada_rows[:, ds(k, 1), piece * D:(piece + 1) * D]) \
                    .then_inc(sm(f"ada_loaded{s}"), 16)

            for s in range(2):
                sp.dma_start(x_tile[s][:, :], ctx_in[0, 128 * s:128 * (s + 1), :]).then_inc(sm(f"xt_loaded{s}"), 16)
                ada_load(s, 0, 2 * s)
                ada_load(s, 1, 2 * s + 1)
            with sp.Fori(1, 5) as i:
                for s in range(4):
                    if s % 2 == 0:
                        sp.wait_ge(sm("tr_done0"), i * 4 + (s - 2))
                        apart(sm("tr_done1"), i * 4 + (s - 2))
                        sp.dma_start(x_tile[s // 2][:, :], x[0, ds(i * 256 + (64 * s - 256), 128), :]).then_inc(sm(f"xt_loaded{s // 2}"), 16)
                    apart(sm("ada_used"), i * 4 + (s - 3))
                    ada_load(i * 2 + s // 2, s % 2, s)
            with sp.Fori(5, 8) as i:
                for s in range(4):
                    apart(sm("ada_used"), i * 4 + (s - 3))
                    ada_load(i * 2 + s // 2, s % 2, s)

            def raw_free(t):
                apart(sm("w_lo_ready"), t - 1)

            def in_tile(col, a, s):
                sp.dma_start(w_raw[s][:, :].rearrange("p (b n) -> p b n", b=4),
                             in_tiles[:, a, :, ds(col, 256)]).then_inc(sm(f"w_loaded{s}"), 16)

            for j in range(4):
                if j < 2:
                    sp.wait_ge(sm("params_stored"), 16 * 3)
                    sp.wait_ge(sm("p_stored"), 16 * 24)
                else:
                    raw_free(T_SSM + j)
                in_tile(PW, j, j % 2)
            with sp.Fori(1, 4) as i:
                for j in range(4):
                    raw_free(i * 4 + (T_SSM + j))
                    in_tile(i * 256 + PW, j, j % 2)
            def proj_tile(i, j):
                raw_free(i * PROJ + (T_Z + j))
                i_, part = i + j // PROJ, j % PROJ // 4
                in_tile(*(((i_ * 512 + (D + 256 * part)),) if part < 2 else (i_ * 256,)), j % 4, j % 2)

            p_q = p_scr.rearrange("q d t ri g n -> q d t (ri g n)")
            b_q = b_scr.rearrange("q d h ri g n -> q d h (ri g n)")
            u_q = u_scr.rearrange("(q g h) t c -> q t h g c", g=GQ, h=SH)

            def load_u(q):
                for g in range(GQ):
                    sp.dma_start(X[:, g, :], u_q[ds(q, 1), :, :, g, :].rearrange("o t h c -> (o t) h c")).then_inc(sm("xq_loaded"), 16)

            def load_powers(q, d_):
                sp.dma_start(PT[:, :, :].rearrange("p a b -> p (a b)"),
                             p_q[ds(q, 1), d_, :, :].rearrange("o t f -> (o t) f").unsqueeze(1).broadcast_to([L, SH, 2 * GQ * SN])) \
                    .then_inc(sm("ptab_loaded"), 16)
                sp.dma_start(BT[:, :, :].rearrange("p a b -> p (a b)"),
                             b_q[ds(q, 1), d_, :, :].broadcast_to([L, SH, 2 * GQ * SN])) \
                    .then_inc(sm("ptab_loaded"), 16)

            def load_c(q):
                sp.dma_start(CQ[:, :, :, :], ctab[:, ds(q * GQ, GQ), :, :]).then_inc(sm("cq_loaded"), 16)
                sp.dma_start(QQ[:, :, :, :], qtab[:, ds(q * GQ, GQ), :, :]).then_inc(sm("cq_loaded"), 16)

            def load_b(q):
                for d_ in range(2):
                    rows = slice(64 * d_, 64 * d_ + 64)
                    sp.dma_start(BZ[rows, d_, :, :, :], btab[rows, ds(q * GQ, GQ), :, :]).then_inc(sm("bz_loaded"), 16)

            y_q = y_scr.rearrange("(q g h) t c -> q t h g c", g=GQ, h=SH)

            def lay_taps(q):
                for t_ in range(L):
                    sp.dma_start(M[SH * t_:SH * (t_ + 1), :, :],
                                 strip[:, :, L - 1 - t_:2 * L - 1 - t_, :].rearrange("p g a b -> p g (a b)")).then_inc(sm("m_loaded"), 16)

            def store_y(q):
                for g in range(GQ):
                    sp.dma_start(y_q[ds(q, 1), :, :, g, :].rearrange("o t h c -> (o t) h c"), yst[:, g, :]) \
                        .then_inc(sm("yst_stored"), 16)

            sp.sem_inc(sm("yst_stored"), START["yst_stored"])
            proj_tile(0, 0)
            proj_tile(0, 1)
            sp.wait_ge(sm("w_used"), T_Z - 2)
            load_powers(0, 0)
            proj_tile(0, 2)
            sp.wait_ge(sm("e_ready"), 1)
            load_powers(0, 1)
            sp.wait_ge(sm("w_used"), T_Z)
            load_c(0)
            sp.wait_ge(sm("u_stored"), 16 * 4)
            load_u(0)
            sp.wait_ge(sm("bz_zeroed"), 1)
            load_b(0)

            def proj_block(i, last):
                for j in range(PROJ):
                    a, r = divmod(j, 3)
                    q = i * 4 + a
                    more = not last or a < 3
                    if r == 2:
                        apart(*past("strip_evicted", q + 1))
                        lay_taps(q)
                    if not last or j < 9:
                        proj_tile(i, j + 3)
                    elif j == 9:
                        glu_tile_pair(0)
                    if last and j == PROJ - 1:
                        sp.wait_ge(sm("w_used"), T_GLU - 1)
                        ada_load(0, 2, 0, gate_buf)
                        sp.wait_ge(sm("e_ready"), 2 * NQ)
                        sp.wait_ge(*past("s_done", NQ))
                        for k in range(2):
                            sp.dma_start(y_in[k][:, :], y_scr.rearrange("(k p) t c -> k p (t c)", p=128)[k]).then_inc(sm(f"y_loaded{k}"), 16)
                        ada_load(1, 2, 1, gate_buf)
                    if r == 0 and more:
                        apart(sm("e_ready"), q * 2 + 2)
                        load_powers(q + 1, 0)
                    if r == 1 and more:
                        apart(sm("e_ready"), q * 2 + 3)
                        load_powers(q + 1, 1)
                        apart(sm("f_ready"), q + 1)
                        load_c(q + 1)
                    if r == 2:
                        if more:
                            load_b(q + 1)
                            apart(*past("skipped", q + 1))
                            load_u(q + 1)
                        if last and a == 3:
                            sp.wait_ge(sm("w_used"), T_GLU)
                        apart(*past("y_evicted", q + 1))
                        store_y(q)

            def glu_tile_pair(i):
                for h, col in enumerate((SW, 0)):
                    raw_free(i * 2 + (T_GLU + h))
                    sp.dma_start(w_raw[h][:, :].rearrange("p (b n) -> p b n", b=8),
                                 glu_tiles[:, :, ds(i * 128 + col, 128)]).then_inc(sm(f"w_loaded{h}"), 16)

            with sp.Fori(0, 3) as i:
                proj_block(i, False)
            proj_block(3, True)
            y_rows = y_scr.rearrange("(k p) t c -> k p (t c)", p=128)

            def load_y(k):
                sp.dma_start(y_in[k % 2][:, :], y_rows[k]).then_inc(sm(f"y_loaded{k % 2}"), 16)

            def load_gate(n):
                if n >= 4:
                    sp.wait_ge(sm("ada_used"), 32 + n - 3)
                ada_load(n, 2, n % 4, gate_buf)

            sp.wait_ge(*past("yst_stored", (NQ - 2) * 64))
            for k in range(2, 8):
                if k == 7:
                    sp.wait_ge(*past("yst_stored", NQ * 64))
                sp.wait_ge(*past("y_ready", k - 1))
                load_y(k)
                if k % 2 == 0:
                    load_gate(k // 2 + 1)
            load_gate(5)
            load_gate(6)

            def store_branch(g):
                sp.wait_ge(*past("pool_evicted", g + 1))
                sp.dma_start(pb_scr.rearrange("(g m p) t -> g p m t", m=2, p=128)[g], up_in[(g + 1) % 2][:, :, :]).then_inc(sm(f"bp_stored{(g + 1) % 2}"), 16)

            glu_tile_pair(1)
            for n in range(7, 13):
                load_gate(n)
            glu_tile_pair(2)
            for n in range(13, 16):
                load_gate(n)
            store_branch(0)
            glu_tile_pair(3)
            store_branch(1)
            with sp.Fori(4, 6) as i:
                glu_tile_pair(i)
            store_branch(2)
            with sp.Fori(6, 8) as i:
                glu_tile_pair(i)
            store_branch(3)
            with sp.Fori(0, 4) as i:
                for j, a in enumerate(OUT_ORDER):
                    raw_free(i * 8 + (T_OUT + j))
                    sp.dma_start(w_raw[j % 2][:, :].rearrange("p (b n) -> p b n", b=2),
                                 out_tiles[:, a, :, ds(i * NB, NB)]).then_inc(sm(f"w_loaded{j % 2}"), 16)

            for tok in range(8):
                sp.wait_ge(sm("out_b_ready"), tok + 1)
                sp.dma_start(out[0, 128 * tok:128 * (tok + 1), 3 * NB:], yb[:, tok, :]).then_inc(sm("stored"), 16)
                if tok < 4:
                    sp.wait_ge(sm("out_a_ready"), tok + 1)
                elif tok % 2 == 0:
                    sp.wait_ge(sm("out_a_ready"), 4 + (tok - 4) // 2 + 1)
                else:
                    sp.wait_ge(sm("out_v_ready"), (tok - 4) // 2 + 1)
                sp.dma_start(out[0, 128 * tok:128 * (tok + 1), 0:3 * NB], yfin[tok // 4][:, tok % 4, :]).then_inc(sm("stored"), 16)
            sp.wait_ge(sm("stored"), 16 * 16)

        @block.tensor
        def _(pe):
            pe.sem_inc(sm("y_done"), START["y_done"])
            pe.sem_inc(sm("s_done"), START["s_done"])

            def x_transposes(i, s):
                pe.wait_ge(sm("xn_ready"), i + 1)
                for kb in range(4):
                    b = kb % 2
                    n = 2 * i + kb // 2
                    if n > 0:
                        pe.wait_ge(sm(f"tr_evicted{b}"), n)
                    for r in range(4):
                        k = 4 * kb + r
                        mm = pe.transpose(ps[:, 2 + b, 128 * r:128 * (r + 1)], x_tile[s][:, 128 * k:128 * (k + 1)], ident[:, :])
                    mm.then_inc(sm(f"tr_done{b}"), 1)

            def ada_matmuls(n, k, piece, s, first, last):
                pe.wait_ge(sm(f"ada_loaded{s}"), 16 * (n // 4 + 1))
                for q in range(4):
                    mm = pe.matmul(ps[32 * q:32 * q + 2, piece, :], cs[:, k, :], ada_buf[s][:, NB * q:NB * (q + 1)],
                                   start=first, stop=last)
                mm.then_inc(sm("ada_used"), 1)

            pe.wait_ge(sm("ident_ready"), 2)
            pe.wait_ge(sm("vecs_loaded"), 16 * len(vec_src))
            pe.transpose(ps[:, 7, 0:V_END], vecs[:, :], ident[0:V_END, 0:V_END]).then_inc(sm("vT_done"), 1)
            pe.wait_ge(sm("d_rep_ready"), 1)
            pe.transpose(ps[:, 6, 0:SG], d_rep[:, :, :].rearrange("g t h -> g (t h)"), ident[0:SG, 0:SG]).then_inc(sm("vT_done"), 1)
            pe.wait_ge(sm("cs_ready"), 1)
            blocks = [pw_[:, j, ri, :] for j in range(L + 1) for ri in range(2)]
            blocks += [b_bar[:, h, ri, :] for h in range(SH) for ri in range(2)]
            blocks += [pp[w][:, :] for w in ("wr", "wi", "r8")]
            rounds = [blocks[0:8], blocks[8:16], blocks[16:18]] + [blocks[18 + 8 * r:26 + 8 * r] for r in range(4)] + [blocks[50:53]]
            ROUNDS = (15, 17, 19, 22, 24, 26, 28, 30)
            for n in range(32):
                ada_matmuls(n, n // 2, n % 2, n % 4, n < 2, n >= 30)
                if n % 2 == 1 and n // 2 < 10:
                    x_transposes(n // 2, (n // 2) % 2)
                if n in ROUNDS:
                    r = ROUNDS.index(n)
                    if r == 0:
                        pe.wait_ge(sm("pw_ready"), 1)
                        pe.wait_ge(sm("c_ready"), 1)
                    else:
                        pe.wait_ge(sm("pf_evicted"), r)
                        pe.wait_ge(sm("pbk_evicted"), r)
                    for i_, src in enumerate(rounds[r]):
                        for d_ in range(2):
                            lo_ = 64 * d_
                            mm = pe.matmul(ps[lo_:lo_ + 64, 4 + d_, 64 * i_:64 * i_ + 64], src[lo_:lo_ + 64, :],
                                           ident[lo_:lo_ + 64, lo_:lo_ + 64], start=True, stop=True)
                    mm.then_inc(sm("pt_done"), 1)
                    if r > 0:
                        pe.wait_ge(sm("ct_evicted"), r)
                    for e in range(3):
                        mm = pe.transpose(ps[:, 6, 128 * e:128 * (e + 1)],
                                          c_nat[:, r, e, :, :].rearrange("p d n -> p (d n)"), ident[:, :])
                    mm.then_inc(sm("ct_done"), 1)
            pe.wait_ge(sm("ada_row_ready"), 4)
            pe.wait_ge(sm("tr_evicted0"), 20)
            pick = ident[:, :].rearrange("p (q c) -> p q c", q=4)[:, :, 0:2]
            for h in range(2):
                for r in range(4):
                    mm = pe.matmul(ps[:, 2, 8 * (4 * h + r):8 * (4 * h + r) + 8], ada_row[:, h, 128 * r:128 * (r + 1)], pick,
                                   start=True, stop=True)
            mm.then_inc(sm("mod_done"), 1)
            pe.wait_ge(sm("mod_evicted"), 1)

            def three(bank, cols, w, a, start, stop):
                (wh, wl), (ah, al) = w, a
                pe.matmul(ps[:, bank, 0:cols], wh, ah, start=start, stop=False)
                pe.matmul(ps[:, bank, 0:cols], wh, al, start=False, stop=False)
                return pe.matmul(ps[:, bank, 0:cols], wl, ah, start=False, stop=stop)

            def in_tile(t, s, j, g, ctx):
                pe.wait_ge(sm("w_lo_ready"), t + 1)
                for kk in range(4):
                    k = 4 * j + kk
                    if ctx:
                        pe.wait_ge(sm("h_ready"), k + 1)
                    for m in range(2):
                        cut = slice(256 * kk + 128 * m, 256 * kk + 128 * (m + 1))
                        w = (w_hi[s][:, cut], w_lo[s][:, cut])
                        if k == 0:
                            pe.wait_ge(*past(f"bank_free{m}", g))
                        for n in range(2):
                            a = (act_hi[:, k, NB * n:NB * (n + 1)], act_lo[:, k, NB * n:NB * (n + 1)])
                            mm = three(2 * m + n, NB, w, a, k == 0, k == KT - 1)
                        if ctx:
                            if kk == 0 and m == 0:
                                pe.wait_ge(sm("hc_ready"), j + 1)
                            mm = three(4 + m, TC, w, (c_hi[:, k, :], c_lo[:, k, :]), k == 0, k == KT - 1)
                        if k == KT - 1 and m == 0:
                            mm.then_inc(sm("m0_done"), 1)
                mm.then_inc(sm("w_used"), 1)

            with pe.Fori(0, 4) as i:
                for j in range(4):
                    in_tile(i * 4 + (T_SSM + j), j % 2, j, i + G_SSM, True)
            def ssm_states(q):
                pe.wait_ge(sm("xq_loaded"), q * 64 + 64)
                pe.wait_ge(sm("e_ready"), q * 2 + 2)
                pe.wait_ge(*past("strip_evicted", q))
                pe.wait_ge(*past("skipped", q))
                for g in range(GQ):
                    for ri in range(2):
                        for d_, rhs in ((0, X[:, g, 0:SEQC]), (1, X[:, g, XC - 1:CC - 1:-1])):
                            mm = pe.matmul(ps[64 * d_:64 * d_ + 64, 4 + g, ri * SEQC:(ri + 1) * SEQC],
                                           E[:, d_, ri, SN * g:SN * (g + 1)], rhs, start=True, stop=True)
                mm.then_inc(sm("s_done"), 1)

            def ssm_strips(q):
                pe.wait_ge(sm("f_ready"), q + 1)
                pe.wait_ge(sm("bz_loaded"), q * 32 + 32)
                pe.wait_ge(*past("s_read", q + 1))
                for g in range(GQ):
                    o_ = LANES * SH * (g % 2)
                    for d_, lo_, j0 in ((1, 0, 2), (0, (L - 1) * SH, 0)):
                        for ri in range(2):
                            mm = pe.matmul(ps[0:SH, 4 + g // 2, o_ + lo_:o_ + lo_ + L * SH], BZ[:, d_, g, ri, :],
                                           F[:, g, ri, j0:j0 + L, :].rearrange("p j h -> p (j h)"),
                                           start=(d_ == 1 and ri == 0), stop=(d_ == 0 and ri == 1), skip_group_check=True)
                mm.then_inc(sm("strip_done"), 1)

            def ssm_readout(q):
                pe.wait_ge(sm("m_loaded"), q * 128 + 128)
                pe.wait_ge(*past("hs_ready", q + 1))
                for g in range(GQ):
                    o_ = ps[:, 6, CX * g:CX * (g + 1)]
                    pe.matmul(o_, M[:, g, :], X[:, g, CC:CC + CX], start=True, stop=False)
                    pe.matmul(o_, F[:, g, 0, 1:L + 1, :].rearrange("p j h -> p (j h)"), H[:, g, 0, :], start=False, stop=False)
                    mm = pe.matmul(o_, F[:, g, 1, 1:L + 1, :].rearrange("p j h -> p (j h)"), H[:, g, 1, :], start=False, stop=True)
                mm.then_inc(sm("y_done"), 1)

            pe.wait_ge(*past("bank_free1", G_Z))
            with pe.Fori(0, 4) as i:
                for j in range(PROJ):
                    in_tile(i * PROJ + (T_Z + j), j % 2, j % 4, i * 3 + (G_Z + j // 4), False)
                    (ssm_states, ssm_strips, ssm_readout)[j % 3](i * 4 + j // 3)

            def pool_matmuls(g):
                up = up_in[(g + 1) % 2]
                pe.wait_ge(sm("diff_ready"), g * 2 + 2)
                pe.wait_ge(sm("pw_loaded"), g * 16 + 16)
                pe.wait_ge(*past("pool_evicted", g))
                for mo in range(2):
                    if g < 2 and mo == 1:
                        pe.wait_ge(sm("gate_row_ready"), g + 1)
                    for n in range(2):
                        for k in range(2):
                            mm = pe.matmul(ps[:, 4 + 2 * mo + n, :], pw_in[:, k, 128 * mo:128 * (mo + 1)],
                                           up[:, k, NB * n:NB * (n + 1)], start=k == 0, stop=k == 1)
                    mm.then_inc(sm("pool_done"), 1)

            def gate_matmuls(n):
                pe.wait_ge(sm(f"ada_loaded{n % 4}"), 16 * (8 + n // 4 + 1))
                if n == 8:
                    pe.wait_ge(*past("pool_evicted", 1))
                for q in range(4):
                    mm = pe.matmul(ps[32 * q:32 * q + 1, 7, :], cs[:, n, 0:1], gate_buf[n % 4][:, NB * q:NB * (q + 1)],
                                   start=n % 8 == 0, stop=n % 8 == 7)
                mm.then_inc(sm("ada_used"), 1)

            def glu_group(i, gate=None):
                for h in range(2):
                    pe.wait_ge(sm("w_lo_ready"), i * 2 + (T_GLU + h + 1))
                    pe.wait_ge(*past(f"bank_free{1 - h}", i + G_GLU))
                    for k in range(8):
                        if gate == 0 and h == 0:
                            pe.wait_ge(*past("y_ready", k + 1))
                        w = (w_hi[h][:, 128 * k:128 * (k + 1)], w_lo[h][:, 128 * k:128 * (k + 1)])
                        for n in range(2):
                            a = (act_hi[:, k, NB * n:NB * (n + 1)], act_lo[:, k, NB * n:NB * (n + 1)])
                            mm = three(2 * (1 - h) + n, NB, w, a, k == 0, k == 7)
                        if k == 7:
                            mm.then_inc(sm("w_used"), 1)
                        if gate is not None and k % 2 == gate // 8:
                            gate_matmuls(gate + 4 * h + k // 2)

            pe.wait_ge(*past("s_read", NQ))
            glu_group(0, gate=0)
            pe.wait_ge(*past("skipped", NQ))
            pool_matmuls(0)
            glu_group(1, gate=8)
            pool_matmuls(1)
            for g, first, end in ((2, 2, 5), (3, 5, 7)):
                with pe.Fori(first, end) as i:
                    glu_group(i)
                pool_matmuls(g)
            glu_group(7)

            pe.wait_ge(*past("pool_evicted", 4))
            pe.wait_ge(sm("ones_ready"), 1)
            pe.wait_ge(sm("gate_row_ready"), 2)
            for q in range(4):
                mm = pe.matmul(ps[:, 4 + q, :], ones[32 * q:32 * q + 1, :], gate_row[32 * q:32 * q + 1, :], start=True, stop=True)
            mm.then_inc(sm("gate_done"), 1)
            def out_matmuls(i, j, toks):
                s = j % 2
                for kk in range(2):
                    k = 2 * OUT_ORDER[j] + kk
                    if k >= 8:
                        pe.wait_ge(sm("br_ready"), k - 8 + 1)
                    else:
                        pe.wait_ge(sm("pbr_ready"), k + 1)
                    for tok in toks:
                        first, last = (j == 0 and kk == 0), (j == 7 and kk == 1)
                        if first:
                            pe.wait_ge(sm("out_free"), i * 8 + tok + 1)
                        cols = slice(128 * tok, 128 * (tok + 1))
                        ah, al = act_hi[:, k, cols], act_lo[:, k, cols]
                        wh, wl = w_hi[s][:, NB * kk:NB * (kk + 1)], w_lo[s][:, NB * kk:NB * (kk + 1)]
                        pe.matmul(ps[:, tok, :], ah, wh, start=first, stop=False)
                        pe.matmul(ps[:, tok, :], ah, wl, start=False, stop=False)
                        mm = pe.matmul(ps[:, tok, :], al, wh, start=False, stop=last)
                        if last and tok < 7:
                            mm.then_inc(sm("tok_done"), 1)
                return mm

            with pe.Fori(0, 3) as i:
                for j in range(8):
                    pe.wait_ge(sm("w_lo_ready"), i * 8 + (T_OUT + j + 1))
                    out_matmuls(i, j, range(8)).then_inc(sm("w_used"), 1)
            for j in range(6):
                pe.wait_ge(sm("w_lo_ready"), T_END - 8 + j + 1)
                out_matmuls(3, j, range(8)).then_inc(sm("w_used"), 1)
            pe.wait_ge(sm("w_lo_ready"), T_END - 1)
            out_matmuls(3, 6, range(4))
            pe.wait_ge(sm("w_lo_ready"), T_END)
            for tok in range(4):
                out_matmuls(3, 7, (tok,))
            for tok in range(4, 8):
                e_ = out_matmuls(3, 6, (tok,))
                if tok == 7:
                    e_.then_inc(sm("w_used"), 1)
                e_ = out_matmuls(3, 7, (tok,))
            e_.then_inc(sm("w_used"), 1)

        @block.scalar
        def _(act):
            act.sem_inc(sm("bank_free0"), START["bank_free0"])
            act.sem_inc(sm("bank_free1"), START["bank_free1"])
            act.sem_inc(sm("strip_evicted"), START["strip_evicted"])
            act.sem_inc(sm("y_evicted"), START["y_evicted"])
            for n in range(4):
                act.sem_inc(sm(f"zst_stored{n}"), START[f"zst_stored{n}"])

            def split_hi(t, s, n_loaded):
                act.wait_ge(sm(f"w_loaded{s}"), n_loaded)
                if not isinstance(t, int) or t >= 2:
                    act.wait_ge(sm("w_used"), t - 1)
                act.activation(w_hi[s][:, :], w_raw[s][:, :], ACT.Copy).then_inc(sm("w_hi_ready"), 1)

            def tiles(base, per, i, js):
                for j in js:
                    t = (i * per + (base + j))
                    split_hi(t, (base + j) % 2, i * (16 * per // 2) + 16 * ((base + j) // 2 + 1))

            act.wait_ge(sm("vT_ready"), 1)
            act.activation(cs[:, :, :].rearrange("p k v -> p v k"), vT[:, V_C:V_C + 32].rearrange("p (v k) -> p v k", v=2),
                           ACT.Silu).then_inc(sm("cs_ready"), 1)

            def x_norm(i, s, n_sq, n_ld):
                act.wait_ge(sm(f"xt_loaded{s}"), n_ld)
                for h in range(4):
                    if not isinstance(n_sq, int) or n_sq > 0 or h > 0:
                        act.wait_ge(sm("sq_chain"), n_sq + h)
                    act.activation(sq_junk[:, :], x_tile[s][:, NB * h:NB * (h + 1)], ACT.Square,
                                   accum_out=ssq[:, s, h:h + 1]).then_inc(sm("sq_chain"), 1)

            def x_evict(i, dst, col):
                for kb in (0, 2):
                    act.wait_ge(sm("tr_done0"), 2 * i + kb // 2 + 1)
                    act.activation(dst[:, 4 * kb:4 * kb + 4, ds(col, 128)],
                                   ps[:, 2, :].rearrange("p (r n) -> p r n", r=4), ACT.Copy).then_inc(sm("tr_evicted0"), 1)

            for s in range(2):
                x_norm(s, s, 4 * s, 16)
            for s in range(2):
                x_evict(s, cT, 128 * s)
                x_norm(2 + s, s, 8 + 4 * s, 32)
            for n_, (dst, src, scale) in enumerate((("sh", "y", 0.5), ("s1", "y", 1.0), ("wi", "y8", 1.0), ("wr", "y8", 0.5))):
                act.wait_ge(sm("y_reduced"), 1 if src == "y" else 2)
                act.activation(pp[dst][:, :], pp[src][:, :], ACT.Sin, scale=scale).then_inc(sm("sin_done"), 1)
            with act.Fori(0, 3) as i:
                for s in range(2):
                    x_evict(i * 2 + (2 + s), xT, i * 256 + 128 * s)
                    x_norm(i * 2 + (4 + s), s, i * 8 + (16 + 4 * s), i * 16 + 48)
            nb = [8, 8, 2] + [8] * 4 + [3]

            def round_evict(r):
                act.wait_ge(sm("pt_done"), r + 1)
                src = ps[0:64, 4, 0:64 * nb[r]]
                if r < 3:
                    dst = q_st[0:64, :, :, 4 * r:4 * r + nb[r] // 2].rearrange("p g ri j -> p j ri g")
                    src = src.rearrange("p (j ri g) -> p j ri g", ri=2, g=SG)
                    for ri in range(2):
                        e_ = act.activation(dst[:, :, ri, :], src[:, :, ri, :], ACT.Copy)
                elif r < 7:
                    dst = b_st[0:64, :, :, 4 * (r - 3):4 * (r - 3) + 4].rearrange("p g ri h -> p h ri g")
                    src = src.rearrange("p (h ri g) -> p h ri g", ri=2, g=SG)
                    for ri in range(2):
                        e_ = act.activation(dst[:, :, ri, :], src[:, :, ri, :], ACT.Copy)
                else:
                    e_ = act.activation(wT[0:64, :, :].rearrange("p w g -> p (w g)"), src, ACT.Copy)
                e_.then_inc(sm("pf_evicted"), 1)
                act.wait_ge(sm("ct_done"), r + 1)
                act.activation(c_st[:, 8 * r:8 * r + 8, :, :].rearrange("p g e h -> p e g h"),
                               ps[:, 6, 0:384].rearrange("p (e g h) -> p e g h", e=3, g=8), ACT.Copy).then_inc(sm("ct_evicted"), 1)

            act.wait_ge(sm("pw_ready"), 1)
            act.wait_ge(sm("q_zeroed"), 1)
            for s in range(2):
                round_evict(s)
                x_evict(8 + s, xT, 768 + 128 * s)
            for r in range(2, 8):
                round_evict(r)
                if r in (2, 6):
                    act.wait_ge(sm("pf_evicted"), r + 1)
                    act.wait_ge(sm("pbk_evicted"), r + 1)
                    dst, src = ((qtab, q_st), (btab, b_st))[r == 6]
                    act.dma_start(dst, src[:, :, :, :]).then_inc(sm("params_stored"), 16)
            act.wait_ge(sm("ct_evicted"), 8)
            act.dma_start(ctab, c_st[:, :, :, :]).then_inc(sm("params_stored"), 16)

            act.wait_ge(sm("ada_row_zeroed"), 1)
            act.wait_ge(sm("ada_used"), 32)
            for q in range(2):
                act.activation(ada_row[32 * q:32 * q + 2, :, :], ps[32 * q:32 * q + 2, 0:2, :], ACT.Copy).then_inc(sm("ada_row_ready"), 1)

            def h_split(ks):
                with act.Fori(*ks) as k:
                    act.wait_ge(sm("h_scaled"), k + 1)
                    act.activation(act_hi[:, ds(k, 1), :], xT[:, ds(k, 1), :], ACT.Copy).then_inc(sm("h_hi_ready"), 1)

            def u_evict(i):
                act.wait_ge(sm("u_stored"), i * 16)
                for m in range(2):
                    if m == 0:
                        act.wait_ge(sm("m0_done"), i + (G_SSM + 1))
                    else:
                        act.wait_ge(sm("w_used"), i * 4 + (T_SSM + 4))
                    for n in range(2):
                        act.activation(ust[:, m, :, CC + 64 * n:CC + 64 * (n + 1)],
                                       ps[:, 2 * m + n, :].rearrange("p (c t) -> p t c", t=L), ACT.Copy)
                    for c0 in (0, SEQC):
                        e_ = act.activation(ust[:, m, :, c0:c0 + CC],
                                            ps[:, 4 + m, 0:TC].rearrange("p (c t) -> p t c", t=L), ACT.Copy)
                    e_.then_inc(sm(f"bank_free{m}"), 1)
                act.wait_ge(*past("bank_free1", i + 1))
                act.dma_start(u_scr.rearrange("(a m p) t c -> p a m (t c)", m=2, p=128)[:, ds(i, 1), :, :].rearrange("p o m f -> p (o m) f"),
                              ust[:, :, :, :].rearrange("p m t c -> p m (t c)")).then_inc(sm("u_stored"), 16)

            split_hi(0, 0, 16)
            for j in range(4):
                h_split((4 * j, 4 * j + 1))
                act.wait_ge(sm("hc_scaled"), 4 * (j + 1))
                act.activation(c_hi[:, 4 * j:4 * j + 4, :], cT[:, 4 * j:4 * j + 4, :], ACT.Copy).then_inc(sm("hc_hi_ready"), 1)
                h_split((4 * j + 1, 4 * j + 4))
                split_hi(j + 1, (j + 1) % 2, 16 * ((j + 1) // 2 + 1))
            act.wait_ge(sm("tabs_free"), 1)
            u_evict(0)
            with act.Fori(1, 4) as i:
                tiles(T_SSM, 4, i, (1, 2, 3, 4))
                u_evict(i)

            def evict_store(i, sub):
                func = ACT.Silu if sub < 2 else ACT.Copy
                for m in range(2):
                    if m == 0:
                        act.wait_ge(sm("m0_done"), i * 3 + (G_Z + sub + 1))
                    else:
                        act.wait_ge(sm("w_used"), i * PROJ + (T_Z + 4 * sub + 4))
                    for n in range(2):
                        row = 2 * m + n
                        act.wait_ge(*past(f"zst_stored{row}", i * 48 + 16 * sub))
                        act.activation(z_st[row][:, :], ps[:, row, :], func).then_inc(sm(f"zst_ready{row}"), 1)
                        act.wait_ge(sm(f"zst_ready{row}"), i * 3 + (sub + 1))
                        if sub < 2:
                            dst = z_scr.rearrange("(a s m p) t -> p a s m t", s=2, m=2, p=128)[:, ds(i, 1), sub, m, NB * n:NB * (n + 1)]
                        else:
                            dst = up_scr.rearrange("(a m p) t -> p a m t", m=2, p=128)[:, ds(i, 1), m, NB * n:NB * (n + 1)]
                        act.dma_start(dst, z_st[row][:, :].unsqueeze(1)).then_inc(sm(f"zst_stored{row}"), 16)
                    act.sem_inc(sm(f"bank_free{m}"), 1)

            def taps(q):
                act.wait_ge(sm("strip_done"), q + 1)
                act.wait_ge(*past("yst_stored", q * 64))
                act.activation(strip[:, :, :, :].rearrange("p (b g) a c -> p b (g a c)", b=2),
                               ps[0:SH, 4:6, 0:2 * LANES * SH], ACT.Copy).then_inc(sm("strip_evicted"), 1)

            def readout(q):
                act.wait_ge(*past("skipped", q + 1))
                act.activation(yst[:, :, :].rearrange("p g c -> p (g c)"), yst[:, :, :].rearrange("p g c -> p (g c)"),
                               ACT.Gelu_apprx_tanh).then_inc(sm("y_evicted"), 1)

            with act.Fori(0, 4) as i:
                for j in range(PROJ):
                    q = i * 4 + j // 3
                    if j % 3 == 2:
                        taps(q)
                    tiles(T_Z, PROJ, i, (j + 1,))
                    if j % 4 == 3:
                        evict_store(i, j // 4)
                    if j % 3 == 2:
                        readout(q)

            act.wait_ge(sm("w_used"), T_GLU)
            with act.Fori(0, 4) as i:
                for s in range(2):
                    act.wait_ge(sm(f"y_loaded{s}"), i * 16 + 16)
                    act.activation(act_hi[:, ds(i * 2 + s, 1), :], y_in[s][:, :].unsqueeze(1), ACT.Copy).then_inc(sm("y_hi_ready"), 1)

            def load_z(i):
                act.dma_start(z_in[:, :], z_scr.rearrange("(k p) t -> k p t", p=128)[ds(i + 8, 1), :, :].rearrange("o p t -> (o p) t")) \
                    .then_inc(sm("zb_loaded"), 16)

            def glu_group(i):
                tiles(T_GLU, 2, i, (1,))
                act.wait_ge(sm("w_used"), i * 2 + (T_GLU + 1))
                if not isinstance(i, int) or i > 0:
                    act.wait_ge(sm("bf_ready"), i)
                for n in range(2):
                    act.activation(sg[:, NB * n:NB * (n + 1)], ps[:, 2 + n, :], ACT.Sigmoid,
                                   bias=b2col[:, ds(i, 1)]).then_inc(sm("sg_ready"), 1)
                act.wait_ge(sm("sg_ready"), i * 2 + 2)
                act.sem_inc(sm("bank_free1"), 1)
                tiles(T_GLU, 2, i, (2,))

            def branch_hi(i, more):
                act.wait_ge(sm("bf_ready"), i + 1)
                act.activation(act_hi[:, ds(i + 8, 1), :], bf[:, :].unsqueeze(1), ACT.Copy).then_inc(sm("br_hi_ready"), 1)
                if more:
                    load_z(i + 1)

            for n in range(4):
                act.wait_ge(*past(f"zst_stored{n}", 16 * 12))
            act.wait_ge(*past("y_ready", 8))
            load_z(0)
            glu_group(0)
            branch_hi(0, True)
            with act.Fori(1, 7) as i:
                glu_group(i)
                branch_hi(i, True)
            glu_group(7)
            act.wait_ge(sm("gate_done"), 1)
            for q in range(4):
                e_ = act.activation(gate_bc[:, NB * q:NB * (q + 1)], ps[:, 4 + q, :], ACT.Copy)
            e_.then_inc(sm("gate_bc_ready"), 1)
            branch_hi(7, False)

            split_hi(T_OUT + 1, 1, 16 * (T_OUT // 2 + 1))
            act.wait_ge(sm("w_used"), T_OUT)
            for k in range(8):
                act.wait_ge(sm(f"pb_loaded{k % 4}"), 16 * (k // 4 + 1))
                act.activation(act_hi[:, k, :], pb_in[k % 4][:, :], ACT.Copy).then_inc(sm("pbr_hi_ready"), 1)
                if k in (3, 5):
                    tiles(T_OUT, 8, 0, (2 + k // 4,))

            def square_sums(i, n_, toks=range(8)):
                for tok in toks:
                    act.wait_ge(*past("y_added", i * 8 + tok + 1))
                    if not isinstance(n_, int) or n_ + tok > 0:
                        act.wait_ge(sm("ysq_chain"), n_ + tok)
                    act.activation(sq_junk2[:, :], yb[:, tok, :], ACT.Square, accum_out=ysq[:, tok, ds(i, 1)]) \
                        .then_inc(sm("ysq_chain"), 1)

            tiles(T_OUT, 8, 0, range(4, 9))
            square_sums(0, 0)
            with act.Fori(1, 3) as i:
                tiles(T_OUT, 8, i, range(1, 9))
                square_sums(i, i * 8)
            tiles(T_OUT, 8, 3, range(1, 8))

            for half, scaled in ((0, (0, 1, 2, 3)), (1, (4, 6))):
                square_sums(3, 24, range(4 * half, 4 * half + 4))
                act.wait_ge(sm("rs_ready"), half + 1)
                for tok in scaled:
                    act.activation(yfin[tok // 4][:, tok % 4, :], yfin[tok // 4][:, tok % 4, :], ACT.Copy,
                                   scale=rsq[:, 2, tok:tok + 1]).then_inc(sm("out_a_ready"), 1)

        @block.vector
        def _(dve):
            dve.sem_inc(sm("s_read"), START["s_read"])
            dve.sem_inc(sm("pool_evicted"), START["pool_evicted"])
            dve.sem_inc(sm("hs_ready"), START["hs_ready"])
            dve.sem_inc(sm("y_ready"), START["y_ready"])
            dve.sem_inc(sm("skipped"), START["skipped"])
            dve.sem_inc(sm("y_added"), START["y_added"])

            chained = [0, 0]

            def link(ins):
                chained[0] += 1
                ins.then_inc(sm("dve_chain"), 1)
                dve.wait_ge(sm("dve_chain"), chained[1] + chained[0])

            class repeat:
                def __init__(self, lo, hi, per):
                    self.lo, self.hi, self.per, self.f = lo, hi, per, dve.Fori(lo, hi)

                def __enter__(self):
                    i = self.f.__enter__()
                    self.base = chained[0]
                    chained[1] = i * self.per
                    chained[0] -= self.per * self.lo
                    return i

                def __exit__(self, *a):
                    chained[0] += self.per * self.lo
                    assert chained[0] - self.base == self.per, chained[0] - self.base
                    chained[0], chained[1] = self.base + self.per * (self.hi - self.lo), 0
                    return self.f.__exit__(*a)

            TT, TS, STT = dve.tensor_tensor, dve.tensor_scalar, dve.scalar_tensor_tensor

            def rsqrt(r, v, tmp):
                link(TS(r.bitcast(i32), v.bitcast(i32), -0.5, 1597463007.0, ALU.mult, ALU.add))
                for _ in range(3):
                    link(STT(tmp, r, v, r, ALU.mult, ALU.mult))
                    link(TS(tmp, tmp, -0.5, 1.5, ALU.mult, ALU.add))
                    link(TT(r, r, tmp, ALU.mult))

            dve.wait_ge(sm("d_loaded"), 16)
            dve.tensor_copy(d_rep[:, :, :], d_nat[:, :].unsqueeze(1).broadcast_to([SG, L, SH])).then_inc(sm("d_rep_ready"), 1)
            dve.wait_ge(sm("vT_done"), 1)
            dve.tensor_copy(vT[:, :], ps[:, 7, 0:V_END]).then_inc(sm("vT_ready"), 1)
            dve.wait_ge(sm("vT_ready"), 1)
            dve.tensor_copy(b2col[:, :], vT[:, V_GLUB + 8:V_GLUB + 16]).then_inc(sm("b2_ready"), 1)

            dve.wait_ge(sm("vT_done"), 2)
            dve.tensor_copy(dT[:, :], ps[:, 6, 0:SG]).then_inc(sm("dT_ready"), 1)

            def x_scale(i, s):
                dve.wait_ge(sm("sq_chain"), i * 4 + 4)
                link(dve.tensor_reduce(rs[:, 0:1], ssq[:, s, :], mybir.AxisListType.X, ALU.add))
                link(TS(rs[:, 1:2], rs[:, 0:1], 1.0 / D, EPS, ALU.mult, ALU.add))
                rsqrt(rs[:, 2:3], rs[:, 1:2], rs[:, 3:4])
                TS(x_tile[s][:, :], x_tile[s][:, :], rs[:, 2:3], None, ALU.mult).then_inc(sm("xn_ready"), 1)

            def x_evict(i, dst, col):
                for kb in (1, 3):
                    dve.wait_ge(sm("tr_done1"), 2 * i + kb // 2 + 1)
                    dve.tensor_copy(dst[:, 4 * kb:4 * kb + 4, ds(col, 128)],
                                    ps[:, 3, :].rearrange("p (r n) -> p r n", r=4)).then_inc(sm("tr_evicted1"), 1)

            for s in range(2):
                x_scale(s, s)
                x_evict(s, cT, 128 * s)
            def x_tiles(i):
                for s in range(2):
                    x_scale(i * 2 + s, s)
                    x_evict(i * 2 + s, xT, i * 256 + (128 * s - 256))

            x_tiles(1)
            dve.wait_ge(sm("norm_ready"), 1)
            dve.reciprocal(pp["inv"][:, :], pp["den"][:, :]).then_inc(sm("inv_ready"), 1)
            with repeat(2, 4, 2 * 12) as i:
                x_tiles(i)

            link(dve.memset(q_st[0:64, :, :, JP - 1], 0.0))
            link(dve.memset(q_st[64:128, :, :, 0], 0.0))
            dve.sem_inc(sm("q_zeroed"), 1)
            nb = [8, 8, 2] + [8] * 4 + [3]

            def round_evict(r):
                dve.wait_ge(sm("pt_done"), r + 1)
                src = ps[64:128, 5, 0:64 * nb[r]]
                if r < 3:
                    src = src.rearrange("p (j ri g) -> p j ri g", ri=2, g=SG)
                    n_, top = nb[r] // 2, L + 1 - 4 * r
                    dst = q_st[64:128, :, :, top:(top - n_ if top - n_ >= 0 else None):-1].rearrange("p g ri j -> p j ri g")
                    for ri in range(2):
                        e_ = dve.tensor_copy(dst[:, :, ri, :], src[:, :, ri, :])
                elif r < 7:
                    dst = b_st[64:128, :, :, 4 * (r - 3):4 * (r - 3) + 4].rearrange("p g ri h -> p h ri g")
                    src = src.rearrange("p (h ri g) -> p h ri g", ri=2, g=SG)
                    for ri in range(2):
                        e_ = dve.tensor_copy(dst[:, :, ri, :], src[:, :, ri, :])
                else:
                    e_ = dve.tensor_copy(wT[64:128, :, :].rearrange("p w g -> p (w g)"), src)
                e_.then_inc(sm("pbk_evicted"), 1)

            for s in range(2):
                x_scale(8 + s, s)
                round_evict(s)
                x_evict(8 + s, xT, 768 + 128 * s)
            for r in range(2, 8):
                round_evict(r)

            dve.wait_ge(sm("ada_row_zeroed"), 1)
            dve.wait_ge(sm("ada_used"), 32)
            for q in range(2, 4):
                dve.tensor_copy(ada_row[32 * q:32 * q + 2, :, :], ps[32 * q:32 * q + 2, 0:2, :]).then_inc(sm("ada_row_ready"), 1)

            def split_lo(t, s):
                dve.wait_ge(sm("w_hi_ready"), t + 1)
                TT(w_lo[s][:, :], w_raw[s][:, :], w_hi[s][:, :].bitcast(f32), ALU.subtract).then_inc(sm("w_lo_ready"), 1)

            def tiles(base, per, i, js):
                for j in js:
                    split_lo(i * per + (base + j), (base + j) % 2)

            dve.wait_ge(sm("mod_done"), 1)
            for q in range(4):
                e_ = TT(modT[:, :, 4 * q:4 * q + 4, :], ps[:, 2, 0:64].rearrange("p (h r q v) -> p h r q v", h=2, r=4, q=4)[:, :, :, q, :],
                        vT[:, V_ADAB:V_ADAB + 32].rearrange("p (h k) -> p h k", h=2)[:, :, 4 * q:4 * q + 4].unsqueeze(3)
                        .broadcast_to([128, 2, 4, 2]), ALU.add)
            link(e_)
            dve.sem_inc(sm("mod_evicted"), 1)
            link(STT(gmul[:, :, :], modT[:, 1, :, :], 1.0, vT[:, V_NG:V_NG + 16].unsqueeze(2).broadcast_to([128, KT, 2]),
                     ALU.add, ALU.mult))

            def h_scale(k):
                TS(xT[:, ds(k, 1), :], xT[:, ds(k, 1), :], gmul[:, ds(k, 1), 0], modT[:, 0, ds(k, 1), 0],
                   ALU.mult, ALU.add).then_inc(sm("h_scaled"), 1)

            def h_lo(k):
                dve.wait_ge(sm("h_hi_ready"), k + 1)
                TT(act_lo[:, ds(k, 1), :], xT[:, ds(k, 1), :], act_hi[:, ds(k, 1), :].bitcast(f32), ALU.subtract) \
                    .then_inc(sm("h_ready"), 1)

            for j in range(4):
                h_scale(4 * j)
                for k in range(4 * j, 4 * j + 4):
                    TS(cT[:, k, :], cT[:, k, :], gmul[:, k, 1:2], modT[:, 0, k, 1:2], ALU.mult, ALU.add).then_inc(sm("hc_scaled"), 1)
                if j == 0:
                    split_lo(0, 0)
                h_scale(4 * j + 1)
                h_lo(4 * j)
                dve.wait_ge(sm("hc_hi_ready"), j + 1)
                TT(c_lo[:, 4 * j:4 * j + 4, :], cT[:, 4 * j:4 * j + 4, :], c_hi[:, 4 * j:4 * j + 4, :].bitcast(f32), ALU.subtract) \
                    .then_inc(sm("hc_ready"), 1)
                with dve.Fori(4 * j + 1, 4 * j + 3) as k:
                    h_scale(k + 1)
                    h_lo(k)
                h_lo(4 * j + 3)
                split_lo(j + 1, (j + 1) % 2)
            dve.wait_ge(sm("params_stored"), 48)
            dve.sem_inc(sm("tabs_free"), 1)
            with dve.Fori(1, 4) as i:
                tiles(T_SSM, 4, i, (1, 2, 3, 4))

            dve.wait_ge(sm("w_used"), T_Z)
            dve.wait_ge(sm("u_stored"), 16 * 4)
            link(dve.memset(BZ[0:64, 1, :, :, :], 0.0))
            link(dve.memset(BZ[64:128, 0, :, :, :], 0.0))
            dve.sem_inc(sm("bz_zeroed"), 1)
            link(dve.memset(R[:, :, 0, 0], 1.0))
            link(dve.memset(R[:, :, 1, 0], 0.0))
            dve.sem_inc(sm("frame_set"), 1)

            def c_powers(q):
                dve.wait_ge(sm("cq_loaded"), q * 32 + 32)
                dve.wait_ge(*past("y_done", q))
                t0, t1 = (TV[:, i_, :].rearrange("p (g j h) -> p g j h", g=GQ, j=JP) for i_ in range(2))

                def cb(e):
                    return CQ[:, :, e:e + 1, :].broadcast_to([128, GQ, JP, SH])

                def qb(ri):
                    return QQ[:, :, ri, :].unsqueeze(3).broadcast_to([128, GQ, JP, SH])
                for ri, e0, e1 in ((0, 0, 1), (1, 1, 2)):
                    link(TT(t0, cb(e0), qb(0), ALU.mult))
                    link(TT(t1, cb(e1), qb(1), ALU.mult))
                    link(TT(F[:, :, ri, :, :], t0, t1, ALU.add))
                dve.sem_inc(sm("f_ready"), 1)

            def recurrence(q):
                dve.wait_ge(sm("r_ready"), q + 1)
                dve.wait_ge(*past("s_done", q + 1))
                for r in range(2):
                    src = ps[:, 4 + 2 * r:6 + 2 * r, 0:2 * SEQC].rearrange("p g (ri c) -> p g ri c", ri=2)
                    t0, t1 = (TV[:, i_, 0:4 * SEQC].rearrange("p (g ri c) -> p g ri c", g=2, ri=2) for i_ in range(2))
                    rr, ri_ = (R[:, 2 * r:2 * r + 2, i_:i_ + 1, :].broadcast_to([128, 2, 2, SEQC]) for i_ in range(2))
                    link(TT(t0, src, rr, ALU.mult))
                    link(TT(t1, src, ri_, ALU.mult))
                    link(TT(G[:, 2 * r:2 * r + 2, 0, :], t0[:, :, 0, :], t1[:, :, 1, :], ALU.subtract))
                    link(TT(G[:, 2 * r:2 * r + 2, 1, :], t0[:, :, 1, :], t1[:, :, 0, :], ALU.add))
                dve.sem_inc(sm("s_read"), 1)
                for g in range(GQ):
                    for ri in range(2):
                        e_ = dve.tensor_tensor_scan(G[:, g, ri, :], wT[:, 2, ds(q * GQ + g, 1)].broadcast_to([128, SEQC]),
                                                    G[:, g, ri, :], 0.0, ALU.mult, ALU.add)
                link(e_)

            def states(q):
                for r in range(2):
                    gs = slice(2 * r, 2 * r + 2)
                    src = G[:, gs, :, CC - 1:SEQC - 1]
                    t0, t1 = (TV[:, i_, 0:4 * CX].rearrange("p (g ri c) -> p g ri c", g=2, ri=2) for i_ in range(2))
                    rr, ri_ = (R[:, gs, i_:i_ + 1, CC - 1:SEQC - 1].broadcast_to([128, 2, 2, CX]) for i_ in range(2))
                    link(TT(t0, src, rr, ALU.mult))
                    link(TT(t1, src, ri_, ALU.mult))
                    for rows, way in ((slice(0, 64), slice(None)), (slice(64, 128), slice(None, None, -1))):
                        TT(H[rows, gs, 0, :], t0[rows, :, 0, way], t1[rows, :, 1, way], ALU.add)
                        e_ = TT(H[rows, gs, 1, :], t0[rows, :, 1, way], t1[rows, :, 0, way], ALU.subtract)
                    link(e_)
                dve.sem_inc(sm("hs_ready"), 1)

            def skip(q):
                dve.wait_ge(*past("y_done", q + 1))
                dve.wait_ge(sm("m_loaded"), q * 128 + 128)
                for g in range(GQ):
                    e_ = STT(yst[:, g, :], X[:, g, CC:CC + CX], dT[:, ds(q * GQ + g, 1)], ps[:, 6, CX * g:CX * (g + 1)],
                             ALU.mult, ALU.add)
                e_.then_inc(sm("skipped"), 1)

            with repeat(0, 4, 4 * (6 + 9 + 6)) as i:
                for j in range(PROJ):
                    if j % 3 == 2:
                        states(i * 4 + j // 3)
                    tiles(T_Z, PROJ, i, (j + 1,))
                    (c_powers, recurrence, skip)[j % 3](i * 4 + j // 3)

            with dve.Fori(0, 4) as i:
                for s in range(2):
                    dve.wait_ge(sm("y_hi_ready"), i * 2 + s + 1)
                    TT(act_lo[:, ds(i * 2 + s, 1), :], y_in[s][:, :].unsqueeze(1), act_hi[:, ds(i * 2 + s, 1), :].bitcast(f32),
                       ALU.subtract).then_inc(sm("y_ready"), 1)

            def glu_group(i):
                tiles(T_GLU, 2, i, (1, 2))
                if isinstance(i, int) and i < 2:
                    if i == 0:
                        dve.wait_ge(sm("gbias_loaded"), 16)
                    else:
                        dve.wait_ge(sm("gate_row_ready"), 1)
                    dve.wait_ge(sm("ada_used"), 40 + 8 * i)
                    for q in range(4):
                        rows = slice(32 * q, 32 * q + 1)
                        e_ = TT(gate_row[rows, :], ps[rows, 7, :], gate_row[rows, :], ALU.add)
                    e_.then_inc(sm("gate_row_ready"), 1)
                dve.wait_ge(sm("w_used"), i * 2 + (T_GLU + 2))
                dve.wait_ge(sm("sg_ready"), i * 2 + 2)
                for n in range(2):
                    e_ = STT(sg[:, NB * n:NB * (n + 1)], ps[:, n, :], vT[:, ds(i + V_GLUB, 1)], sg[:, NB * n:NB * (n + 1)],
                             ALU.add, ALU.mult)
                e_.then_inc(sm("bank_free0"), 1)
                dve.wait_ge(*past("bank_free0", i + (G_GLU + 1)))
                if isinstance(i, int) and i == 7:
                    dve.sem_inc(sm("out_free"), 4)
                dve.wait_ge(sm("zb_loaded"), i * 16 + 16)
                if not isinstance(i, int) or i > 0:
                    dve.wait_ge(sm("br_hi_ready"), i)
                TT(bf[:, :].rearrange("p (c t) -> p t c", t=L), sg[:, :].rearrange("p (t c) -> p t c", t=L),
                   z_in[:, :].rearrange("p (c t) -> p t c", t=L), ALU.mult).then_inc(sm("bf_ready"), 1)
                dve.wait_ge(sm("br_hi_ready"), i + 1)
                TT(act_lo[:, ds(i + 8, 1), :], bf[:, :].unsqueeze(1), act_hi[:, ds(i + 8, 1), :].bitcast(f32), ALU.subtract) \
                    .then_inc(sm("br_ready"), 1)

            def pool_evict(g):
                dve.wait_ge(sm("pool_done"), g * 2 + 2)
                dve.wait_ge(sm("zp_loaded"), g * 32 + 32)
                for mo in range(2):
                    for n in range(2):
                        e_ = STT(up_in[(g + 1) % 2][:, mo, NB * n:NB * (n + 1)], ps[:, 4 + 2 * mo + n, :], vT[:, ds(g * 2 + (V_PS + mo), 1)],
                                 zp_in[mo][:, NB * n:NB * (n + 1)], ALU.mult, ALU.mult)
                e_.then_inc(sm("pool_evicted"), 1)

            glu_group(0)
            pool_evict(0)
            glu_group(1)
            pool_evict(1)
            for g, first, end in ((2, 2, 5), (3, 5, 7)):
                if g == 3:
                    dve.wait_ge(sm("bp_stored1"), 32)
                with dve.Fori(first, end) as i:
                    glu_group(i)
                pool_evict(g)
            glu_group(7)

            dve.wait_ge(sm("gate_bc_ready"), 1)
            dve.sem_inc(sm("out_free"), 4)
            tiles(T_OUT, 8, 0, (1,))
            for k in range(8):
                dve.wait_ge(sm("pbr_hi_ready"), k + 1)
                TT(act_lo[:, k, :], pb_in[k % 4][:, :], act_hi[:, k, :].bitcast(f32), ALU.subtract).then_inc(sm("pbr_ready"), 1)
                if k in (3, 5):
                    tiles(T_OUT, 8, 0, (2 + k // 4,))

            def out_evict(i, toks=range(8), last=False):
                dve.wait_ge(sm("yb_stored"), i * 16)
                if not isinstance(i, int) or i > 0:
                    dve.wait_ge(sm("ysq_chain"), i * 8)
                def gated(tok):
                    if tok < 7:
                        dve.wait_ge(sm("tok_done"), i * 7 + tok + 1)
                    else:
                        dve.wait_ge(sm("w_used"), i * 8 + (T_OUT + 8))
                    TT(yb[:, tok, :], ps[:, tok, :], gate_bc[:, ds(i * NB, NB)], ALU.mult).then_inc(sm("out_free"), 1)

                def added(tok):
                    dve.wait_ge(sm("out_free"), i * 8 + (9 + tok))
                    TT(yb[:, tok, :], yb[:, tok, :], xb[:, tok, :], ALU.add).then_inc(sm("y_added"), 1)

                for tok in toks:
                    gated(tok)
                    if last:
                        dve.wait_ge(sm("xb_loaded"), 64)
                        added(tok)
                if not last:
                    dve.wait_ge(sm("xb_loaded"), i * 16 + 16)
                    for tok in range(8):
                        added(tok)

            tiles(T_OUT, 8, 0, range(4, 9))
            out_evict(0)
            with dve.Fori(1, 3) as i:
                tiles(T_OUT, 8, i, range(1, 9))
                out_evict(i)
            for j in range(1, 8):
                tiles(T_OUT, 8, 3, (j,))
                if j == 4:
                    dve.wait_ge(sm("fg_loaded"), 16)
                if j >= 4:
                    for tok in (2 * j - 8, 2 * j - 7):
                        dve.wait_ge(sm(f"yfin_loaded{tok}"), 16)
                        TT(yfin[tok // 4][:, tok % 4, :], yfin[tok // 4][:, tok % 4, :], fg_bc[:, 0:3 * NB], ALU.mult) \
                            .then_inc(sm("yfin_weighted"), 1)

            dve.wait_ge(sm("yfin_weighted"), 8)
            for half, scaled in ((0, ()), (1, (5, 7))):
                toks = slice(4 * half, 4 * half + 4)
                out_evict(3, range(4 * half, 4 * half + 4), last=True)
                sums, mean, root, t0 = (rsq[:, i_, toks] for i_ in range(4))
                dve.wait_ge(sm("ysq_chain"), 28 + 4 * half)
                link(dve.tensor_reduce(sums, ysq[:, toks, :], mybir.AxisListType.X, ALU.add))
                link(TS(mean, sums, 1.0 / D, EPS, ALU.mult, ALU.add))
                link(TS(root.bitcast(i32), mean.bitcast(i32), -0.5, 1597463007.0, ALU.mult, ALU.add))
                for _ in range(3):
                    link(TT(t0, root, root, ALU.mult))
                    link(TT(t0, t0, mean, ALU.mult))
                    link(TS(t0, t0, -0.5, 1.5, ALU.mult, ALU.add))
                    link(TT(root, root, t0, ALU.mult))
                dve.sem_inc(sm("rs_ready"), 1)
                for tok in range(4 * half, 4 * half + 4):
                    STT(yb[:, tok, :], yb[:, tok, :], rsq[:, 2, tok:tok + 1], fg_bc[:, 3 * NB:], ALU.mult, ALU.mult) \
                        .then_inc(sm("out_b_ready"), 1)
                    if tok in scaled:
                        TS(yfin[tok // 4][:, tok % 4, :], yfin[tok // 4][:, tok % 4, :], rsq[:, 2, tok:tok + 1], None, ALU.mult) \
                            .then_inc(sm("out_v_ready"), 1)

        @block.gpsimd
        def _(gp):
            TT, TS = gp.tensor_tensor, gp.tensor_scalar
            chained = [0, 0]

            def link(ins):
                chained[0] += 1
                ins.then_inc(sm("gp_chain"), 1)
                gp.wait_ge(sm("gp_chain"), chained[1] + chained[0])

            class repeat:
                def __init__(self, lo, hi, per):
                    self.lo, self.hi, self.per, self.f = lo, hi, per, gp.Fori(lo, hi)

                def __enter__(self):
                    i = self.f.__enter__()
                    self.base = chained[0]
                    chained[1] = i * self.per
                    return i

                def __exit__(self, *a):
                    assert self.lo == 0 and chained[0] - self.base == self.per, chained[0] - self.base
                    chained[0], chained[1] = self.base + self.per * self.hi, 0
                    return self.f.__exit__(*a)

            gp.memset(ident[:, :], 0.0).then_inc(sm("ident_ready"), 1)
            gp.wait_ge(sm("ident_ready"), 1)
            gp.affine_select(out=ident[:, :], in_=ident[:, :], compare_op=ALU.not_equal, fill=1.0, base=0,
                             pattern=[[-1, 128]], channel_multiplier=1).then_inc(sm("ident_ready"), 1)

            def apart(semaphore, value):
                gp.wait_ge(semaphore, value)
                gp.sem_inc(sm("gp_passed"), 1)

            gp.dma_start(pp["lre"][:, :], lam_re.rearrange("o d g n -> (o d g) n")).then_inc(sm("lam_loaded"), 16)
            gp.dma_start(pp["lim"][:, :], lam_im.rearrange("o d g n -> (o d g) n")).then_inc(sm("lam_loaded"), 16)
            gp.dma_start(dt_col[:, 0:1], log_dt.rearrange("o d (g u) -> (o d g) u", u=1)).then_inc(sm("lam_loaded"), 16)
            for ri, b_ in enumerate((b_re, b_im)):
                gp.dma_start(b_nat[:, ri, :, :], b_.rearrange("o d g n h -> (o d g) n h")).then_inc(sm("b_loaded"), 16)
            P = {n_: t[:, :] for n_, t in pp.items()}

            def STT(dst, in0, scalar, in1, op0, op1):
                step = pp["step"][:, 0:dst.shape[-1]]
                link(TS(step, in0, scalar, None, op0))
                return TT(dst, step, in1, op1)

            def exp(dst, x_, n_, r_, p_, bits):
                MAGIC = 12582912.0
                link(TS(r_, x_, -88.0, 89.0, ALU.max, ALU.min))
                link(TS(n_, r_, 1.0 / math.log(2.0), MAGIC, ALU.mult, ALU.add))
                link(TS(n_, n_, MAGIC, None, ALU.subtract))
                link(STT(r_, n_, -0.693359375, r_, ALU.mult, ALU.add))
                link(STT(r_, n_, 2.12194440e-4, r_, ALU.mult, ALU.add))
                link(TS(p_, r_, 1.0 / 5040, None, ALU.mult))
                for k in (720, 120, 24, 6, 2, 1):
                    link(STT(p_, p_, 1.0 / k, r_, ALU.add, ALU.mult))
                link(TS(bits, n_, 127.0, 8388608.0, ALU.add, ALU.mult))
                link(STT(dst, p_, 1.0, bits.bitcast(f32), ALU.add, ALU.mult))

            def reduce_angle(dst, x_, n_):
                MAGIC = 12582912.0
                link(TS(n_, x_, 1.0 / (2 * math.pi), MAGIC, ALU.mult, ALU.add))
                link(TS(n_, n_, MAGIC, None, ALU.subtract))
                c1 = 6.28125
                c2 = float(np.float32(np.floor((2 * math.pi - c1) * 2 ** 21) / 2 ** 21))
                c3 = 2 * math.pi - c1 - c2
                link(STT(dst, n_, -c1, x_, ALU.mult, ALU.add))
                link(STT(dst, n_, -c2, dst, ALU.mult, ALU.add))
                link(STT(dst, n_, -c3, dst, ALU.mult, ALU.add))
                return TS(dst, dst, -math.pi, math.pi, ALU.max, ALU.min)

            gp.wait_ge(sm("lam_loaded"), 16 * 3)
            link(TT(P["t"], P["lre"], P["lre"], ALU.mult))
            link(TT(P["t3"], P["lim"], P["lim"], ALU.mult))
            link(TT(P["den"], P["t"], P["t3"], ALU.add))
            gp.sem_inc(sm("norm_ready"), 1)
            col = lambda i_: dt_col[:, i_:i_ + 1]
            exp(col(4), col(0), col(1), col(2), col(3), dt_bits[:, :])
            link(TS(P["zr"], P["lre"], col(4), None, ALU.mult))
            link(TS(P["zi"], P["lim"], col(4), None, ALU.mult))
            link(reduce_angle(P["y"], P["zi"], P["n"]))
            gp.sem_inc(sm("y_reduced"), 1)
            link(TS(P["t"], P["y"], 8.0, None, ALU.mult))
            link(reduce_angle(P["y8"], P["t"], P["n"]))
            gp.sem_inc(sm("y_reduced"), 1)
            exp(P["e"], P["zr"], P["n"], P["r"], P["p"], e_bits[:, :])
            link(TT(P["r8"], P["e"], P["e"], ALU.mult))
            link(TT(P["r8"], P["r8"], P["r8"], ALU.mult))
            link(TT(P["r8"], P["r8"], P["r8"], ALU.mult))
            gp.wait_ge(sm("sin_done"), 4)
            link(STT(P["cm"], P["sh"], -2.0, P["sh"], ALU.mult, ALU.mult))
            link(STT(P["t"], P["wr"], -2.0, P["wr"], ALU.mult, ALU.mult))
            link(TS(P["wr"], P["t"], 1.0, None, ALU.add))
            link(TS(P["wi"], P["wi"], -1.0, None, ALU.mult))
            a_r, a_i = pw_[:, 1, 0, :], pw_[:, 1, 1, :]
            link(TT(P["t"], P["e"], P["cm"], ALU.mult))
            link(STT(P["t2"], P["e"], -1.0, P["t"], ALU.add, ALU.add))
            link(TT(a_r, P["t"], P["e"], ALU.add))
            link(TT(a_i, P["e"], P["s1"], ALU.mult))
            link(TT(P["kr"], P["t2"], P["lre"], ALU.mult))
            link(TT(P["t"], a_i, P["lim"], ALU.mult))
            link(TT(P["kr"], P["kr"], P["t"], ALU.add))
            gp.wait_ge(sm("inv_ready"), 1)
            link(TT(P["kr"], P["kr"], P["inv"], ALU.mult))
            link(TT(P["ki"], a_i, P["lre"], ALU.mult))
            link(TT(P["t"], P["t2"], P["lim"], ALU.mult))
            link(TT(P["ki"], P["ki"], P["t"], ALU.subtract))
            link(TT(P["ki"], P["ki"], P["inv"], ALU.mult))
            for ri, c_ in enumerate((c_re, c_im)):
                for d_ in range(2):
                    gp.dma_start(c_nat[:, :, ri, d_, :], c_[0, d_].rearrange("(oc g) h n -> (g h) oc n", g=8)).then_inc(sm("c_loaded"), 16)
            gp.memset(pw_[:, 0, 0, :], 1.0)
            gp.memset(pw_[:, 0, 1, :], 0.0)
            for m in (1, 2, 4):
                src = pw_[:, 1:m + 1, :, :]
                link(TT(ptmp[:, 0, 0:m, :, :], src, pw_[:, m:m + 1, 0:1, :].broadcast_to([128, m, 2, SN]), ALU.mult))
                link(TT(ptmp[:, 1, 0:m, :, :], src, pw_[:, m:m + 1, 1:2, :].broadcast_to([128, m, 2, SN]), ALU.mult))
                link(TT(pw_[:, m + 1:2 * m + 1, 0, :], ptmp[:, 0, 0:m, 0, :], ptmp[:, 1, 0:m, 1, :], ALU.subtract))
                link(TT(pw_[:, m + 1:2 * m + 1, 1, :], ptmp[:, 0, 0:m, 1, :], ptmp[:, 1, 0:m, 0, :], ALU.add))
            gp.wait_ge(sm("b_loaded"), 32)
            br_, bi_ = (b_nat[:, i_, :, :].rearrange("p n h -> p h n") for i_ in range(2))
            kr_, ki_ = (P[n_].unsqueeze(1).broadcast_to([128, SH, SN]) for n_ in ("kr", "ki"))
            for o_, (u0, v0), (u1, v1), op in ((0, (br_, kr_), (bi_, ki_), ALU.subtract), (1, (bi_, kr_), (br_, ki_), ALU.add)):
                link(TT(b_tmp[:, 0, :, :], u0, v0, ALU.mult))
                link(TT(b_tmp[:, 1, :, :], u1, v1, ALU.mult))
                link(TT(b_bar[:, :, o_, :], b_tmp[:, 0, :, :], b_tmp[:, 1, :, :], op))
            gp.sem_inc(sm("pw_ready"), 1)

            gp.wait_ge(sm("dT_ready"), 1)
            gp.memset(ada_row[:, :, :], 0.0).then_inc(sm("ada_row_zeroed"), 1)
            gp.wait_ge(sm("c_loaded"), 64)
            link(TS(c_nat[:, :, 1, :, :], c_nat[:, :, 1, :, :], -1.0, None, ALU.mult))
            link(TS(c_nat[:, :, 2, :, :], c_nat[:, :, 0, :, :], -1.0, None, ALU.mult))
            gp.sem_inc(sm("c_ready"), 1)
            for d_ in range(2):
                for g in range(GQ):
                    rows = slice(64 * d_ + g, 64 * d_ + 64, GQ)
                    src = pw_[rows, 0:L, :, :] if d_ == 1 else pw_[rows, L - 1::-1, :, :]
                    for ri in range(2):
                        gp.dma_start(p_scr[:, d_, :, ri, g, :], src[:, :, ri, :]).then_inc(sm("p_stored"), 16)
                    gp.dma_start(b_scr[:, d_, :, :, g, :].rearrange("q h ri n -> q (h ri) n"),
                                 b_bar[rows, :, :, :].rearrange("p h ri n -> p (h ri) n")).then_inc(sm("p_stored"), 16)
            gp.wait_ge(sm("p_stored"), 16 * 24)

            gp.wait_ge(sm("w_used"), T_Z - 1)
            spans = [(0, 1, 1), (0, 2, 2), (0, 4, 4), (0, 8, 8), (0, 16, 16), (0, 32, 32), (0, 64, 32), (32, 64, 32),
                     (0, 128, SEQC - 1 - 128)]
            with repeat(0, NQ, 16 + 1 + 4 * len(spans)) as q:
                for d_ in range(2):
                    gp.wait_ge(sm("ptab_loaded"), q * 64 + 32 * (d_ + 1))
                    if d_ == 0:
                        gp.wait_ge(*past("s_done", q))
                    for half in range(2):
                        cols = slice(2 * SN * half, 2 * SN * (half + 1))
                        t0, t1 = (TG[:, i_, :].rearrange("p (ri f) -> p ri f", ri=2) for i_ in range(2))
                        link(TT(t0, BT[:, :, cols], PT[:, 0:1, cols].broadcast_to([128, 2, 2 * SN]), ALU.mult))
                        link(TT(t1, BT[:, :, cols], PT[:, 1:2, cols].broadcast_to([128, 2, 2 * SN]), ALU.mult))
                        link(TT(E[:, d_, 0, cols], t0[:, 0, :], t1[:, 1, :], ALU.subtract))
                        link(TT(E[:, d_, 1, cols], t0[:, 1, :], t1[:, 0, :], ALU.add))
                    gp.sem_inc(sm("e_ready"), 1)
                gp.wait_ge(sm("frame_set"), 1)
                gp.wait_ge(*past("hs_ready", q))
                link(gp.tensor_copy(R[:, :, :, 1], wT[:, 0:2, ds(q * GQ, GQ)].rearrange("p w g -> p g w")))
                for s0, m, n in spans:
                    src = R[:, :, :, s0 + 1:s0 + n + 1]
                    t0, t1 = (TG[:, i_, 0:GQ * 2 * n].rearrange("p (g ri n) -> p g ri n", g=GQ, ri=2) for i_ in range(2))
                    link(TT(t0, src, R[:, :, 0:1, m:m + 1].broadcast_to([128, GQ, 2, n]), ALU.mult))
                    link(TT(t1, src, R[:, :, 1:2, m:m + 1].broadcast_to([128, GQ, 2, n]), ALU.mult))
                    o_ = slice(m + s0 + 1, m + s0 + 1 + n)
                    link(TT(R[:, :, 0, o_], t0[:, :, 0, :], t1[:, :, 1, :], ALU.subtract))
                    link(TT(R[:, :, 1, o_], t0[:, :, 1, :], t1[:, :, 0, :], ALU.add))
                gp.sem_inc(sm("r_ready"), 1)

            z_rows = z_scr.rearrange("(k p) t -> k p t", p=128)
            up_rows = up_scr.rearrange("(g m p) t -> g p m t", m=2, p=128)
            gp.wait_ge(*past("hs_ready", NQ))
            gp.wait_ge(*past("y_done", NQ))
            gp.wait_ge(*past("yst_stored", NQ * 64))
            gp.wait_ge(sm("w_used"), T_GLU)
            for n in range(4):
                gp.wait_ge(*past(f"zst_stored{n}", 16 * 12))
            gp.memset(ones[:, :], 1.0).then_inc(sm("ones_ready"), 1)
            gp.dma_start(gate_row[0:128:32, :], ada_b[0:1, 2 * D:3 * D].rearrange("o (q n) -> (o q) n", q=4)).then_inc(sm("gbias_loaded"), 16)
            def load_group(g):
                if g == 0:
                    gp.wait_ge(*past("y_ready", 8))
                else:
                    gp.wait_ge(*past("pool_evicted", g))
                gp.dma_start(pw_in[:, :, :], pool_w[0, g].rearrange("(k p) n -> p k n", p=128)).then_inc(sm("pw_loaded"), 16)
                for mo in range(2):
                    gp.dma_start(zp_in[mo][:, :], z_rows[2 * g + mo]).then_inc(sm("zp_loaded"), 16)

            for g, w in enumerate(WINDOWS):
                up = up_in[(g + 1) % 2]
                if g >= 2:
                    gp.wait_ge(sm(f"bp_stored{(g + 1) % 2}"), 16)
                gp.dma_start(up[:, :, :], up_rows[g]).then_inc(sm("up_loaded"), 16)
                gp.dma_start(inv_in[:, :], inv_count[g:g + 1, :].to_broadcast([128, T])).then_inc(sm("up_loaded"), 16)
                gp.wait_ge(sm("up_loaded"), 32 * (g + 1))
                for m in range(2):
                    half = w // 2
                    rows = GR + w
                    cur, oth = PA, PB
                    x3 = up[:, m, :].rearrange("p (r c) -> p r c", c=GW)
                    d_, n = 1, rows
                    cols = GW + w
                    while d_ < w:
                        n -= d_
                        lastlevel = 2 * d_ == w
                        if d_ == 1:
                            n_out = GR if lastlevel else n
                            width = cols if lastlevel else GW
                            o3 = oth[:, 0:n_out * width].rearrange("p (r c) -> p r c", c=width)
                            if lastlevel:
                                gp.memset(o3[:, :, 0:half], 0.0)
                                gp.memset(o3[:, :, half + GW:], 0.0)
                                o3 = o3[:, :, half:half + GW]
                            if half > 1:
                                gp.memset(o3[:, 0:half - 1, :], 0.0)
                            gp.tensor_copy(o3[:, half - 1, :], x3[:, 0, :])
                            if half + GR - 1 < n_out:
                                gp.tensor_copy(o3[:, half + GR - 1, :], x3[:, GR - 1, :])
                            if half + GR < n_out:
                                gp.memset(o3[:, half + GR:, :], 0.0)
                            link(TT(o3[:, half:half + GR - 1, :], x3[:, 0:GR - 1, :], x3[:, 1:GR, :], ALU.add))
                        elif lastlevel:
                            pad = oth[:, 0:GR * cols].rearrange("p (r c) -> p r c", c=cols)
                            gp.memset(pad[:, :, 0:half], 0.0)
                            gp.memset(pad[:, :, half + GW:], 0.0)
                            c3 = cur[:, :].rearrange("p (r c) -> p r c", c=GW)
                            link(TT(pad[:, :, half:half + GW], c3[:, 0:GR, :], c3[:, d_:d_ + GR, :], ALU.add))
                        else:
                            link(TT(oth[:, 0:n * GW], cur[:, 0:n * GW], cur[:, d_ * GW:(d_ + n) * GW], ALU.add))
                        cur, oth = oth, cur
                        d_ *= 2
                    d_, n = 1, cols
                    cv = cur[:, 0:GR * cols].rearrange("p (r c) -> p r c", c=cols)
                    while d_ < w:
                        n = GW if 2 * d_ == w else n - d_
                        ov = oth[:, 0:GR * n].rearrange("p (r c) -> p r c", c=n)
                        link(TT(ov, cv[:, :, 0:n], cv[:, :, d_:d_ + n], ALU.add))
                        cur, oth = oth, cur
                        cv = ov
                        d_ *= 2
                    link(TT(cur[:, 0:T], cur[:, 0:T], inv_in[:, :], ALU.mult))
                    link(TT(up[:, m, :], cur[:, 0:T], up[:, m, :], ALU.subtract))
                    gp.sem_inc(sm("diff_ready"), 1)
                    if m == int(g == 0):
                        load_group(g)

            gp.wait_ge(sm("bp_stored0"), 32)
            gp.wait_ge(sm("bp_stored1"), 32)
            for k in range(8):
                if k >= 4:
                    gp.wait_ge(sm("pbr_ready"), k - 3)
                gp.dma_start(pb_in[k % 4][:, :], pb_scr[128 * k:128 * (k + 1), :]).then_inc(sm(f"pb_loaded{k % 4}"), 16)
            gp.wait_ge(sm("pbr_ready"), 8)
            x_v = x[0].rearrange("(a p) n -> p a n", p=128)
            yo_v = yo_scr.rearrange("(a p) n -> p a n", p=128)
            with gp.Fori(0, 3) as i:
                apart(*past("y_added", i * 8))
                gp.dma_start(xb[:, :, :], x_v[:, :, ds(i * NB, NB)]).then_inc(sm("xb_loaded"), 16)
                apart(*past("y_added", i * 8 + 8))
                gp.dma_start(yo_v[:, :, ds(i * NB, NB)], yb[:, :, :]).then_inc(sm("yb_stored"), 16)
            gp.dma_start(fg_bc[:, :], final_g.unsqueeze(0).to_broadcast([128, D])).then_inc(sm("fg_loaded"), 16)
            apart(*past("y_added", 24))
            gp.dma_start(xb[:, :, :], x_v[:, :, 3 * NB:]).then_inc(sm("xb_loaded"), 16)
            gp.wait_ge(sm("yb_stored"), 48)
            gp.wait_ge(sm("w_used"), T_END - 5)
            for tok in range(8):
                gp.dma_start(yfin[tok // 4][:, tok % 4, :], yo_v[:, tok, 0:3 * NB]).then_inc(sm(f"yfin_loaded{tok}"), 16)


_INS = ["x", "c", "ctx", "c_ctx", "ada_w", "ada_b", "norm_g", "in_w", "pool_w", "pool_scale", "s5_lam_re", "s5_lam_im",
        "s5_log_dt", "s5_b_re", "s5_b_im", "s5_c_re", "s5_c_im", "s5_d", "glu_w", "glu_b", "out_w", "final_g"]
_OUTS = [((1, T, D), "float32")]


def _inv_counts():
    def counts(n, w):
        t = np.arange(n)
        return np.clip(t + w - w // 2, 0, n) - np.clip(t - w // 2, 0, n)
    return np.stack([(1.0 / np.outer(counts(GR, w), counts(GW, w))).reshape(T) for w in WINDOWS]).astype(np.float32)


def kernel(**inputs):
    import numpy as _np
    import concourse.bacc as _bacc
    from concourse import mybir as _mybir
    from concourse.bass_utils import run_bass_kernel_spmd as _run

    nc = _bacc.Bacc("TRN2", target_bir_lowering=False, num_devices=1)
    arrays, args = {}, []
    for name in _INS:
        a = _np.ascontiguousarray(inputs[name])
        arrays[f"in_{name}_dram"] = a
        args.append(nc.dram_tensor(f"in_{name}_dram", a.shape, _mybir.dt.from_np(a.dtype), kind="ExternalInput").ap())
    a = _inv_counts()
    arrays["inv_count_dram"] = a
    args.append(nc.dram_tensor("inv_count_dram", a.shape, _mybir.dt.from_np(a.dtype), kind="ExternalInput").ap())
    for i, (shape, dtype) in enumerate(_OUTS):
        dt = _mybir.dt.from_np(_np.dtype(dtype))
        args.append(nc.dram_tensor(f"out_{i}_dram", shape, dt, kind="ExternalOutput").ap())
    hybrid_block(nc, *args)
    r = _run(nc, [arrays], core_ids=[0])
    return r.results[0]["out_0_dram"]
```
